# Optimizing a Trainium2 kernel written in Bass

```python
import math
import jax
import jax.numpy as jnp
from jax import lax
import numpy as np

D_MODEL = 1024
BATCH = 1
SEQ = 256
DEPTH = 2

GRID_W = 64
CTX_LEN = 256
N_MIXERS = 3
ADA_CHUNKS = 6
NORM_EPS = 1e-6
CONV_KERNEL = 31
DA_HEAD_DIM = 64
DA_HEADS = D_MODEL // (2 * DA_HEAD_DIM)
DA_Q_BLOCK = 128
ROPE_THETA = 10000.0
ROPE_FREQS = DA_HEAD_DIM // 4
GDN_DK = 128
GDN_DV = 128
GDN_HEADS = D_MODEL // GDN_DK
GDN_SHORT_CONV = 5
GDN_CHUNK = 64
GDN_QK_W = GDN_HEADS * GDN_DK
GDN_V_W = GDN_HEADS * GDN_DV
GDN_CONV_CH = 2 * GDN_QK_W + GDN_V_W
GDN_IN_W = GDN_CONV_CH + GDN_V_W + 4 * GDN_HEADS
N_EXPERTS = 16
N_GROUPS = 4
GROUP_SIZE = N_EXPERTS // N_GROUPS
TOP_K = 2
D_EXPERT = 512

kernel_name = 'hybrid_conv_diffattn_gdn_moe_dit'

def _n_layers_of_kind(kind):
    return len(range(kind, DEPTH, N_MIXERS))

def _rms_norm(x, g):
    x32 = x.astype(jnp.float32)
    y = x32 * lax.rsqrt(jnp.mean(x32 * x32, axis=-1, keepdims=True) + NORM_EPS)
    return (y * g.astype(jnp.float32)).astype(x.dtype)

def _layer_norm(x, g, b):
    x32 = x.astype(jnp.float32)
    xc = x32 - jnp.mean(x32, axis=-1, keepdims=True)
    y = xc * lax.rsqrt(jnp.mean(xc * xc, axis=-1, keepdims=True) + NORM_EPS)
    return (y * g.astype(jnp.float32) + b.astype(jnp.float32)).astype(x.dtype)

def _l2_normalize(t):
    return t * lax.rsqrt(jnp.sum(t * t, axis=-1, keepdims=True) + NORM_EPS)

def _modulate(h, shift, scale):
    return h * (1 + scale) + shift

def _depthwise_conv(x, w):
    pad = w.shape[0] // 2
    return lax.conv_general_dilated(x, w[:, None, :], window_strides=(1,), padding=[(pad, pad)],
                                    dimension_numbers=('NWC', 'WIO', 'NWC'),
                                    feature_group_count=x.shape[-1])

def _axial_rope_tables(seqlen, dtype):
    rows = seqlen // GRID_W
    row = jnp.repeat(jnp.arange(rows, dtype=jnp.float32), GRID_W)
    col = jnp.tile(jnp.arange(GRID_W, dtype=jnp.float32), rows)
    inv_freq = ROPE_THETA ** (-jnp.arange(ROPE_FREQS, dtype=jnp.float32) / ROPE_FREQS)
    ang = jnp.stack([row[:, None] * inv_freq, col[:, None] * inv_freq], axis=1)
    return jnp.cos(ang).astype(dtype), jnp.sin(ang).astype(dtype)

def _apply_axial_rope(t, cos, sin):
    shp = t.shape
    t = t.reshape(*shp[:-1], 2, 2, ROPE_FREQS)
    t1, t2 = t[..., 0, :], t[..., 1, :]
    cs = cos[None, :, None, None]
    sn = sin[None, :, None, None]
    out = jnp.stack([t1 * cs - t2 * sn, t2 * cs + t1 * sn], axis=-2)
    return out.reshape(shp)

def _conv_module(h, pw1_w, pw1_b, dw_w, dw_b, ln_g, ln_b, pw2_w, pw2_b):
    a = h @ pw1_w + pw1_b
    half = a.shape[-1] // 2
    a = a[..., :half] * jax.nn.sigmoid(a[..., half:])
    a = _depthwise_conv(a, dw_w) + dw_b
    a = jax.nn.silu(_layer_norm(a, ln_g, ln_b))
    return a @ pw2_w + pw2_b

def _diff_attention(h_ctx, h_lat, w_qkv, lam_vecs, subln_g, w_o, lam_init, cos, sin, ctx_out):
    scale = DA_HEAD_DIM ** -0.5

    def project(h):
        bsz, n = h.shape[:2]
        q, k, v = jnp.split(h @ w_qkv, 3, axis=-1)
        q = q.reshape(bsz, n, DA_HEADS, 2, DA_HEAD_DIM)
        k = k.reshape(bsz, n, DA_HEADS, 2, DA_HEAD_DIM)
        v = v.reshape(bsz, n, DA_HEADS, 2 * DA_HEAD_DIM)
        return q, k, v

    lv = lam_vecs.astype(jnp.float32)
    lam = jnp.exp(jnp.sum(lv[0] * lv[1])) - jnp.exp(jnp.sum(lv[2] * lv[3])) + lam_init

    def attend(q, k, v):
        s = jnp.einsum('bqhcd,bkhcd->bhcqk', q, k, preferred_element_type=jnp.float32) * scale
        p = jax.nn.softmax(s, axis=-1)
        a = (p[:, :, 0] - lam * p[:, :, 1]).astype(v.dtype)
        return jnp.einsum('bhqk,bkhe->bqhe', a, v)

    def finish(o):
        bsz, n = o.shape[:2]
        o = _rms_norm(o, subln_g) * (1.0 - lam_init)
        return o.reshape(bsz, n, -1) @ w_o

    q_c, k_c, v_c = project(h_ctx)
    q_l, k_l, v_l = project(h_lat)
    q_l = _apply_axial_rope(q_l, cos, sin)
    k_l = _apply_axial_rope(k_l, cos, sin)
    k_all = jnp.concatenate([k_c, k_l], axis=1)
    v_all = jnp.concatenate([v_c, v_l], axis=1)
    bsz, seqlen = h_lat.shape[:2]
    n_blk = seqlen // DA_Q_BLOCK
    q_blocks = jnp.moveaxis(q_l.reshape(bsz, n_blk, DA_Q_BLOCK, DA_HEADS, 2, DA_HEAD_DIM), 1, 0)
    o_blocks = lax.map(lambda qb: attend(qb, k_all, v_all), q_blocks)
    o_lat = jnp.moveaxis(o_blocks, 0, 1).reshape(bsz, seqlen, DA_HEADS, 2 * DA_HEAD_DIM)
    y_lat = finish(o_lat)
    y_ctx = finish(attend(q_c, k_c, v_c)) if ctx_out else None
    return y_ctx, y_lat

def _gated_delta_chunked(q, k, v, g, beta, s0, with_output):
    bsz, seqlen, nh = q.shape[:3]
    dv = v.shape[-1]
    n = seqlen // GDN_CHUNK

    def to_chunks(t):
        t = t.reshape(bsz, n, GDN_CHUNK, nh, *t.shape[3:])
        return jnp.moveaxis(t, (1, 2), (0, 3))

    q, k, v, g, beta = (to_chunks(t) for t in (q, k, v, g, beta))
    G = jnp.cumsum(g, axis=-1)
    idx = jnp.arange(GDN_CHUNK)
    incl = idx[:, None] >= idx[None, :]
    strict = idx[:, None] > idx[None, :]
    decay = jnp.exp(jnp.where(incl, G[..., :, None] - G[..., None, :], -jnp.inf))
    kk = jnp.einsum('nbhid,nbhjd->nbhij', k, k)
    a_mat = jnp.where(strict, beta[..., :, None] * kk * decay, 0.0) + jnp.eye(GDN_CHUNK, dtype=k.dtype)
    rhs = jnp.concatenate([v * beta[..., None], k * (beta * jnp.exp(G))[..., None]], axis=-1)
    sol = lax.linalg.triangular_solve(a_mat, rhs, left_side=True, lower=True, unit_diagonal=True)
    u, w = sol[..., :dv], sol[..., dv:]
    k_tail = k * jnp.exp(G[..., -1:] - G)[..., None]
    chunk_decay = jnp.exp(G[..., -1])
    xs = (u, w, k_tail, chunk_decay)
    if with_output:
        qk = jnp.einsum('nbhid,nbhjd->nbhij', q, k) * decay
        xs = xs + (q * jnp.exp(G)[..., None], qk)

    def step(s, inp):
        u_c, w_c, kt_c, cd_c = inp[:4]
        v_new = u_c - jnp.einsum('bhcd,bhde->bhce', w_c, s)
        s_next = cd_c[..., None, None] * s + jnp.einsum('bhcd,bhce->bhde', kt_c, v_new)
        if with_output:
            qd_c, qk_c = inp[4:]
            o = jnp.einsum('bhcd,bhde->bhce', qd_c, s) + jnp.einsum('bhij,bhje->bhie', qk_c, v_new)
            return s_next, o
        return s_next, None

    s_final, o = lax.scan(step, s0, xs)
    if with_output:
        o = jnp.moveaxis(o, (0, 3), (1, 2)).reshape(bsz, seqlen, nh, dv)
    return o, s_final

def _gdn_mixer(h_ctx, h_lat, w_in, conv_w, a_log, dt_bias, norm_g, w_o, ctx_out):
    def project(h):
        bsz, n = h.shape[:2]
        zz = h @ w_in
        qkv = jax.nn.silu(_depthwise_conv(zz[..., :GDN_CONV_CH], conv_w)).astype(jnp.float32)
        q = _l2_normalize(qkv[..., :GDN_QK_W].reshape(bsz, n, GDN_HEADS, GDN_DK)) * (GDN_DK ** -0.5)
        k = _l2_normalize(qkv[..., GDN_QK_W:2 * GDN_QK_W].reshape(bsz, n, GDN_HEADS, GDN_DK))
        v = qkv[..., 2 * GDN_QK_W:].reshape(bsz, n, GDN_HEADS, GDN_DV)
        z = zz[..., GDN_CONV_CH:GDN_CONV_CH + GDN_V_W]
        ba = zz[..., GDN_CONV_CH + GDN_V_W:].astype(jnp.float32)
        beta = jax.nn.sigmoid(ba[..., :2 * GDN_HEADS]).reshape(bsz, n, 2, GDN_HEADS)
        g = -jnp.exp(a_log.astype(jnp.float32)) * jax.nn.softplus(
            ba[..., 2 * GDN_HEADS:].reshape(bsz, n, 2, GDN_HEADS) + dt_bias.astype(jnp.float32))
        return q, k, v, z, beta, g

    def finish(o, z):
        bsz, n = o.shape[:2]
        zg = jax.nn.silu(z.reshape(bsz, n, GDN_HEADS, GDN_DV).astype(jnp.float32))
        o = (_rms_norm(o, norm_g) * zg).astype(z.dtype)
        return o.reshape(bsz, n, GDN_V_W) @ w_o

    rev = lambda t: t[:, ::-1]
    q_c, k_c, v_c, z_c, b_c, g_c = project(h_ctx)
    q_l, k_l, v_l, z_l, b_l, g_l = project(h_lat)
    s0 = jnp.zeros((h_lat.shape[0], GDN_HEADS, GDN_DK, GDN_DV), jnp.float32)
    o_cf, s_f = _gated_delta_chunked(q_c, k_c, v_c, g_c[:, :, 0], b_c[:, :, 0], s0, ctx_out)
    o_cb, s_b = _gated_delta_chunked(rev(q_c), rev(k_c), rev(v_c), rev(g_c[:, :, 1]), rev(b_c[:, :, 1]), s0, ctx_out)
    o_lf, _ = _gated_delta_chunked(q_l, k_l, v_l, g_l[:, :, 0], b_l[:, :, 0], s_f, True)
    o_lb, _ = _gated_delta_chunked(rev(q_l), rev(k_l), rev(v_l), rev(g_l[:, :, 1]), rev(b_l[:, :, 1]), s_b, True)
    y_lat = finish(o_lf + rev(o_lb), z_l)
    y_ctx = finish(o_cf + rev(o_cb), z_c) if ctx_out else None
    return y_ctx, y_lat

def _moe(h, router_w, router_b, w_gate, w_up, w_down):
    n_tok = h.shape[0]
    scores = jax.nn.sigmoid((h @ router_w).astype(jnp.float32))
    sel = scores + router_b.astype(jnp.float32)
    group_score = jnp.sum(lax.top_k(sel.reshape(n_tok, N_GROUPS, GROUP_SIZE), TOP_K)[0], axis=-1)
    best_group = jnp.argmax(group_score, axis=-1)
    in_group = (jnp.arange(N_EXPERTS) // GROUP_SIZE)[None, :] == best_group[:, None]
    _, idx = lax.top_k(jnp.where(in_group, sel, -jnp.inf), TOP_K)
    wts = jnp.take_along_axis(scores, idx, axis=-1)
    wts = wts / jnp.sum(wts, axis=-1, keepdims=True)
    gates = jnp.sum(jax.nn.one_hot(idx, N_EXPERTS, dtype=jnp.float32) * wts[..., None], axis=1).astype(h.dtype)
    out = jnp.zeros_like(h)
    for e in range(N_EXPERTS):
        a = jax.nn.silu(h @ w_gate[e]) * (h @ w_up[e])
        out = out + gates[:, e:e + 1] * (a @ w_down[e])
    return out

def setup_inputs(seed: int = 0) -> dict:
    key = jax.random.key(seed)
    keys = iter(jax.random.split(key, 40))

    def nrm(shape, scale):
        return jax.random.normal(next(keys), shape, jnp.float32) * scale

    d = D_MODEL
    n_conv, n_diff, n_gdn = (_n_layers_of_kind(kk) for kk in range(N_MIXERS))
    dt = jnp.exp(jax.random.uniform(next(keys), (n_gdn, 2, GDN_HEADS), jnp.float32,
                                    math.log(1e-3), math.log(1e-1)))
    return {
        'x': nrm((BATCH, SEQ, d), 1.0),
        'c': nrm((BATCH, d), 1.0),
        'ctx': nrm((BATCH, CTX_LEN, d), 1.0),
        'c_ctx': nrm((d,), 1.0),
        'ada_w': nrm((DEPTH, d, ADA_CHUNKS * d), 0.5 * d ** -0.5),
        'ada_b': nrm((DEPTH, ADA_CHUNKS * d), 0.02),
        'norm_mix_g': 1.0 + nrm((DEPTH, d), 0.02),
        'norm_ffn_g': 1.0 + nrm((DEPTH, d), 0.02),
        'final_norm_g': 1.0 + nrm((d,), 0.02),
        'conv_pw1_w': nrm((n_conv, d, 2 * d), d ** -0.5),
        'conv_pw1_b': nrm((n_conv, 2 * d), 0.02),
        'conv_dw_w': nrm((n_conv, CONV_KERNEL, d), CONV_KERNEL ** -0.5),
        'conv_dw_b': nrm((n_conv, d), 0.02),
        'conv_ln_g': 1.0 + nrm((n_conv, d), 0.02),
        'conv_ln_b': nrm((n_conv, d), 0.02),
        'conv_pw2_w': nrm((n_conv, d, d), d ** -0.5),
        'conv_pw2_b': nrm((n_conv, d), 0.02),
        'diff_w_qkv': nrm((n_diff, d, 3 * d), d ** -0.5),
        'diff_lambda': nrm((n_diff, 4, DA_HEAD_DIM), 0.1),
        'diff_subln_g': 1.0 + nrm((n_diff, 2 * DA_HEAD_DIM), 0.02),
        'diff_w_o': nrm((n_diff, d, d), d ** -0.5),
        'gdn_w_in': nrm((n_gdn, d, GDN_IN_W), d ** -0.5),
        'gdn_conv_w': nrm((n_gdn, GDN_SHORT_CONV, GDN_CONV_CH), GDN_SHORT_CONV ** -0.5),
        'gdn_a_log': jnp.log(jax.random.uniform(next(keys), (n_gdn, 2, GDN_HEADS), jnp.float32, 1.0, 16.0)),
        'gdn_dt_bias': dt + jnp.log(-jnp.expm1(-dt)),
        'gdn_norm_g': 1.0 + nrm((n_gdn, GDN_DV), 0.02),
        'gdn_w_o': nrm((n_gdn, GDN_V_W, d), GDN_V_W ** -0.5),
        'router_w': nrm((d, N_EXPERTS), d ** -0.5),
        'router_b': nrm((N_EXPERTS,), 0.01),
        'moe_w_gate': nrm((DEPTH, N_EXPERTS, d, D_EXPERT), d ** -0.5),
        'moe_w_up': nrm((DEPTH, N_EXPERTS, d, D_EXPERT), d ** -0.5),
        'moe_w_down': nrm((DEPTH, N_EXPERTS, D_EXPERT, d), D_EXPERT ** -0.5),
    }

def reference(x, c, ctx, c_ctx, ada_w, ada_b, norm_mix_g, norm_ffn_g, final_norm_g,
              conv_pw1_w, conv_pw1_b, conv_dw_w, conv_dw_b, conv_ln_g, conv_ln_b, conv_pw2_w, conv_pw2_b,
              diff_w_qkv, diff_lambda, diff_subln_g, diff_w_o,
              gdn_w_in, gdn_conv_w, gdn_a_log, gdn_dt_bias, gdn_norm_g, gdn_w_o,
              router_w, router_b, moe_w_gate, moe_w_up, moe_w_down):
    bsz, seqlen, d = x.shape
    n_ctx = ctx.shape[1]
    cos, sin = _axial_rope_tables(seqlen, x.dtype)
    silu_c = jax.nn.silu(c)
    silu_cc = jax.nn.silu(c_ctx)
    lat, cx = x, ctx
    for i in range(DEPTH):
        last = i == DEPTH - 1
        kind, j = i % N_MIXERS, i // N_MIXERS
        m_lat = jnp.split((silu_c @ ada_w[i] + ada_b[i])[:, None, :], ADA_CHUNKS, axis=-1)
        h_lat = _modulate(_rms_norm(lat, norm_mix_g[i]), m_lat[0], m_lat[1])
        need_ctx = (not last) or kind != 0
        if need_ctx:
            m_ctx = jnp.split(silu_cc @ ada_w[i] + ada_b[i], ADA_CHUNKS, axis=-1)
            h_ctx = _modulate(_rms_norm(cx, norm_mix_g[i]), m_ctx[0], m_ctx[1])
        if kind == 0:
            p = (conv_pw1_w[j], conv_pw1_b[j], conv_dw_w[j], conv_dw_b[j],
                 conv_ln_g[j], conv_ln_b[j], conv_pw2_w[j], conv_pw2_b[j])
            y_lat = _conv_module(h_lat, *p)
            y_ctx = None if last else _conv_module(h_ctx, *p)
        elif kind == 1:
            lam_init = 0.8 - 0.6 * math.exp(-0.3 * i)
            y_ctx, y_lat = _diff_attention(h_ctx, h_lat, diff_w_qkv[j], diff_lambda[j], diff_subln_g[j],
                                           diff_w_o[j], lam_init, cos, sin, not last)
        else:
            y_ctx, y_lat = _gdn_mixer(h_ctx, h_lat, gdn_w_in[j], gdn_conv_w[j], gdn_a_log[j], gdn_dt_bias[j],
                                      gdn_norm_g[j], gdn_w_o[j], not last)
        lat = lat + m_lat[2] * y_lat
        h2_lat = _modulate(_rms_norm(lat, norm_ffn_g[i]), m_lat[3], m_lat[4])
        if last:
            y = _moe(h2_lat.reshape(-1, d), router_w, router_b, moe_w_gate[i], moe_w_up[i], moe_w_down[i])
            lat = lat + m_lat[5] * y.reshape(bsz, seqlen, d)
        else:
            cx = cx + m_ctx[2] * y_ctx
            h2_ctx = _modulate(_rms_norm(cx, norm_ffn_g[i]), m_ctx[3], m_ctx[4])
            tokens = jnp.concatenate([h2_ctx.reshape(-1, d), h2_lat.reshape(-1, d)], axis=0)
            y = _moe(tokens, router_w, router_b, moe_w_gate[i], moe_w_up[i], moe_w_down[i])
            cx = cx + m_ctx[5] * y[:bsz * n_ctx].reshape(bsz, n_ctx, d)
            lat = lat + m_lat[5] * y[bsz * n_ctx:].reshape(bsz, seqlen, d)
    return _rms_norm(lat, final_norm_g)


_drawn_inputs = setup_inputs


def setup_inputs(seed=0):
    import zlib

    import numpy as np

    out = dict(_drawn_inputs(seed))
    spreads = {}
    factors = {'norm_mix_g': 2.994,
     'final_norm_g': 2.858,
     'conv_pw1_b': 4.611,
     'conv_dw_b': 3.321,
     'conv_pw2_b': 4.154,
     'diff_subln_g': 4.554}
    for name, (base, spread) in spreads.items():
        noise = np.random.default_rng([zlib.crc32(name.encode()), seed]).standard_normal(out[name].shape)
        drawn = base * np.exp(spread * noise) if base else spread * noise
        out[name] = jnp.asarray(drawn.astype(out[name].dtype))
    for name, factor in factors.items():
        out[name] = (out[name] * factor).astype(out[name].dtype)
    return out
```

```python
from contextlib import ExitStack
import math

import numpy as np

import concourse.bass as bass
from concourse import mybir

F32 = mybir.dt.float32
I32 = mybir.dt.int32
U32 = mybir.dt.uint32
ALU = mybir.AluOpType
ACT = mybir.ActivationFunctionType
AX = mybir.AxisListType

P = 128
D = 1024
KC = D // P
SEQ, CTX = 256, 256
NTOK = SEQ + CTX
NT = NTOK // P
DEPTH = 2
ADA = 6
MODC = ADA * KC
TAPS = 31
PAD = TAPS // 2
UW = SEQ + 2 * PAD
HEADS = 8
HD = 64
E = 16
GROUPS = 4
GS = E // GROUPS
FE = 512
FC = FE // P
EPS = 1e-6
LAM_INIT = 0.8 - 0.6 * math.exp(-0.3 * 1)
SCALE = HD ** -0.5
GRID_W = 64
FREQS = HD // 4
THETA = 10000.0
OVER = 2 * NTOK // (P + 1)
PIECE = KC * FE
RING = 6
BIG = 1e30

C_ID, C_MEAN, C_HEAD, C_ONE, C_BEFORE, C_ROT = (P * k for k in range(6))
C_COS = 6 * P
C_SIN = C_COS + SEQ
C_EKEY = C_SIN + SEQ
C_GKEY = C_EKEY + NT * E
C_PASS = C_GKEY + NT * GROUPS
C_EXP = C_PASS + OVER * E
C_END = C_EXP + OVER * E

STEPS = ("free", "turned", "rows", "gate", "silu", "up", "act", "act_turned", "act_rows", "down", "out")

A_ADA, A_C, A_CC, A_PW1 = 0, DEPTH * MODC, DEPTH * MODC + KC, DEPTH * MODC + 2 * KC
B_MIX, B_FFN, B_FIN, B_DWB, B_LNG, B_LNB, B_PW2, B_SUB = 0, 16, 32, 40, 48, 56, 64, 72
B_ROWS = 73

ADA_PC = ADA * D // FE
SEQ_ADA0A = [(("ada", 0, n)) for n in range(4)]
SEQ_PW1 = [("pw1", 0, 0), ("pw1", 0, 2), ("pw1", 0, 1), ("pw1", 0, 3)]
SEQ_A = (SEQ_ADA0A + SEQ_PW1 + [("ada", 0, n) for n in range(4, ADA_PC)]
         + [("ada", 1, n) for n in range(ADA_PC)] + [("pw2", 0, 0), ("pw2", 0, 1)])
SEQ_B = [("qkv", 0, n) for n in range(6)] + [("wo", 0, n) for n in range(2)]
BASE_B = len(SEQ_A) + 3 * E
MOE_BASE = [len(SEQ_A), BASE_B + len(SEQ_B)]
PLACE = {key: n for n, key in enumerate(SEQ_A)}
PLACE.update({key: BASE_B + n for n, key in enumerate(SEQ_B)})


def constants():
    c = np.zeros((P, C_END), np.float32)
    i = np.arange(P)
    c[:, C_ID:C_ID + P] = np.eye(P)
    c[:, C_MEAN:C_MEAN + P] = 1.0 / D
    c[:, C_HEAD:C_HEAD + P] = 1.0 / P
    c[:, C_ONE:C_ONE + P] = 1.0
    c[:, C_BEFORE:C_BEFORE + P] = i[:, None] < i[None, :]
    half = (i // FREQS) % 2
    for m in range(P):
        if half[m]:
            c[m - FREQS, C_ROT + m] = 1.0
        else:
            c[m + FREQS, C_ROT + m] = -1.0
    axis, f = (i // (2 * FREQS)) % 2, i % FREQS
    tok = np.arange(SEQ)
    inv = (THETA ** (-np.arange(FREQS, dtype=np.float64) / FREQS)).astype(np.float32)
    pos = np.where(axis[:, None] == 0, tok[None, :] // GRID_W, tok[None, :] % GRID_W).astype(np.float32)
    ang = pos * inv[f][:, None]
    c[:, C_COS:C_COS + SEQ] = np.cos(ang)
    c[:, C_SIN:C_SIN + SEQ] = np.sin(ang)
    c[:, C_EKEY:C_EKEY + NT * E] = np.tile(E - np.arange(E), NT)
    c[:, C_GKEY:C_GKEY + NT * GROUPS] = np.tile(GROUPS - np.arange(GROUPS), NT)
    c[:, C_PASS:C_PASS + OVER * E] = np.repeat(np.arange(OVER), E)
    c[:, C_EXP:C_EXP + OVER * E] = np.tile(np.arange(E), OVER)
    return c


def build(nc, a, out):
    with ExitStack() as ctx:
        def sb(name, shape, dt=F32):
            return ctx.enter_context(nc.sbuf_tensor(name, shape, dt))

        def sem(name):
            return ctx.enter_context(nc.semaphore(name))

        ring = sb("ring", [P, RING, PIECE])
        X = sb("X", [P, KC, NTOK])
        H = sb("H", [P, KC, NTOK])
        UB = sb("UB", [P, KC * 2 * UW])
        V = sb("V", [P, KC * NTOK])
        W = sb("W", [P, NT * D])
        cst = sb("cst", [P, C_END])
        rowsA = sb("rowsA", [P, P])
        rowsB = sb("rowsB", [P, P])
        colA = sb("colA", [P, P])
        colB = sb("colB", [P, B_ROWS])
        cw = sb("cw", [P, KC, 32])
        rw = sb("rw", [P, KC, E])
        rb = sb("rb", [P, E])
        sc = sb("sc", [P, KC, 2])
        mod = [sb(f"mod{l}", [P, MODC, 2]) for l in range(DEPTH)]
        modA = sb("modA", [P, 2, KC, 2])
        gb2 = sb("gb2", [P, KC, 2])
        R = sb("R", [P, NTOK])
        epsc = sb("epsc", [P, 1])
        sg = sb("sg", [P, 2, NTOK])
        lam = sb("lam", [P, 4, HD])
        lamt = sb("lamt", [P, 8])
        sm = sb("sm", [P, 2, 2, 4])
        subg = sb("subg", [P, 1])
        score = sb("score", [P, NT, E])
        sel = sb("sel", [P, NT, E])
        msel = sb("msel", [P, NT, E])
        tA = sb("tA", [P, NT, E])
        tB = sb("tB", [P, NT, E])
        oh = sb("oh", [P, 2, NT, E])
        pair = sb("pair", [P, 2, NT, E])
        g4 = sb("g4", [P, 10, NT * GROUPS])
        t1 = sb("t1", [P, 12, NT])
        wk = sb("wk", [P, 2, NT])
        slot = sb("slot", [P, 2 * NT], I32)
        ints = sb("ints", [P, 2, 24])
        offI = sb("offI", [P, 24], I32)
        cum = sb("cum", [P, 2, 8 + E])
        ov = sb("ov", [P, 4, OVER * E])
        ovf = sb("ovf", [P, 2, 8])
        ovI = sb("ovI", [P, 3, 8], I32)
        novI = sb("novI", [P, 1], I32)
        zrow = sb("zrow", [P, D])
        ps = ctx.enter_context(nc.psum_tensor("ps", [P, 8, 512], F32))

        tap_rows = H[:, 0:2, :].rearrange("p j t -> p (j t)")
        U = UB[:, :].rearrange("p (j s w) -> p j s w", j=KC, s=2)
        Vt = V[:, :].rearrange("p (j t) -> p j t", j=KC)
        Wt = W[:, :].rearrange("p (t d) -> p t d", t=NT)
        Ht = H[:, :, :].rearrange("p j t -> p (j t)").rearrange("p (t d) -> p t d", t=NT)
        hrow = UB[:, 0:2 * D].rearrange("p (b d) -> p b d", b=2)
        hT = UB[:, 2 * D:4 * D].rearrange("p (b d) -> p b d", b=2)
        yrow = V[:, 0:2 * D].rearrange("p (b d) -> p b d", b=2)
        eg = V[:, 2 * D:2 * D + FE]
        ea = V[:, 2 * D + FE:2 * D + 2 * FE]
        eaT = V[:, 3 * D:3 * D + FE]
        Q = UB[:, 0:HEADS * SEQ].rearrange("p (h t) -> p h t", h=HEADS)
        pr = UB[:, HEADS * SEQ:HEADS * SEQ + 4 * NTOK].rearrange("p (b c t) -> p b c t", b=2, c=2)
        K = Vt
        O = H[:, 0:4, :].rearrange("p j t -> p (j t)").rearrange("p (h t) -> p h t", h=HEADS)
        OF = H[:, 0:4, :].rearrange("p j t -> p (j t)")
        aT = H[:, 4:8, :].rearrange("p j t -> p (j t)").rearrange("p (b k t) -> p b k t", b=2, k=NT)
        rope = R

        Hs = nc.dram_tensor("token_rows", (2 * NTOK + P, D), F32, kind="Internal").ap()
        Ys = nc.dram_tensor("expert_rows", (2 * NTOK + P, D), F32, kind="Internal").ap()

        def C(at, n=P):
            return cst[:, at:at + n]

        ident, mean, head_mean, ones, before, rot = (C(k) for k in (C_ID, C_MEAN, C_HEAD, C_ONE, C_BEFORE, C_ROT))

        w_in = [sem(f"w_in{s}") for s in range(RING)]
        cst_in, vec_in, x_in, rw_in, lam_in = (sem(n) for n in ("cst_in", "vec_in", "x_in", "rw_in", "lam_in"))
        vec_t, vec_c = sem("vec_t"), sem("vec_c")
        x_t, x_c = sem("x_t"), sem("x_c")
        c_silu = sem("c_silu")
        ada_p, ada_c = sem("ada_p"), sem("ada_c")
        modA_r, modB_r = sem("modA_r"), sem("modB_r")
        pad_z = sem("pad_z")
        dve = sem("dve_chain")
        pw1_p, pw1_s, pw1_g = sem("pw1_p"), sem("pw1_s"), sem("pw1_g")
        conv_a = sem("conv_a")
        mean_p, cen, cen_sq, var_p, lnz, ln_s = (sem(n) for n in ("mean_p", "cen", "cen_sq", "var_p", "lnz", "ln_s"))
        pw2_p, pw2_t, pw2_x = sem("pw2_p"), sem("pw2_t"), sem("pw2_x")
        q_p, q_c, rot_p, q_r = sem("q_p"), sem("q_c"), sem("rot_p"), sem("q_r")
        v_p, v_c = sem("v_p"), sem("v_c")
        s_p, s_m, s_e, s_a, a_t, a_c, o_p, o_c = (sem(n) for n in (
            "s_p", "s_m", "s_e", "s_a", "a_t", "a_c", "o_p", "o_c"))
        o_sq, o_ms, o_n = sem("o_sq"), sem("o_ms"), sem("o_n")
        wo_p, wo_x = sem("wo_p"), sem("wo_x")
        fin_t, fin_c, out_w = sem("fin_t"), sem("fin_c"), sem("out_w")
        hs_pad = sem("hs_pad")
        lam_s, lam_e = sem("lam_s"), sem("lam_e")
        eps_r, root = sem("eps_r"), sem("root")
        ROOTS = {"mix0": 1, "ln": 2, "ffn0": 3, "mix1": 4, "heads": 5, "ffn1": 9, "fin": 10}

        class Norm:
            def __init__(self, n):
                self.sq, self.ms, self.hr, self.h = (sem(f"{n}_{k}") for k in ("sq", "ms", "hr", "h"))

        norms = {k: Norm(k) for k in ("mix0", "ffn0", "mix1", "ffn1", "fin")}

        class Moe:
            def __init__(self, l):
                def s(k):
                    return sem(f"m{l}_{k}")
                self.route_p, self.score_r, self.pair_r, self.rank_p, self.slot_r = (
                    s(k) for k in ("route_p", "score_r", "pair_r", "rank_p", "slot_r"))
                self.rows_t, self.rows_c, self.scat = s("rows_t"), s("rows_c"), s("scat")
                self.h_in = [s("h_in0"), s("h_in1")]
                self.h_t, self.h_c = s("h_t"), s("h_c")
                self.gate_p, self.gate_s, self.up_p, self.act_r = (s(k) for k in ("gate_p", "gate_s", "up_p", "act_r"))
                self.act_t, self.act_c = s("act_t"), s("act_c")
                self.down_p, self.y0_c, self.y1_c = s("down_p"), s("y0_c"), s("y1_c")
                self.y_out, self.y_free = s("y_out"), s("y_free")
                self.end = s("end")
                self.o_step, self.o_in, self.o_w, self.o_out = (s(k) for k in ("o_step", "o_in", "o_w", "o_out"))
                self.y_in, self.mix_r, self.mix_t, self.mix_x = (s(k) for k in ("y_in", "mix_r", "mix_t", "mix_x"))

        moes = [Moe(l) for l in range(DEPTH)]
        VECS = 13
        TL = [NT, SEQ // P]
        T0 = [0, CTX // P]

        def piece_src(kind, l, n):
            cols = slice(n * FE, (n + 1) * FE)
            w = {"ada": a["ada_w"][l], "pw1": a["conv_pw1_w"][0], "pw2": a["conv_pw2_w"][0],
                 "qkv": a["diff_w_qkv"][0], "wo": a["diff_w_o"][0]}[kind]
            return w[:, cols].rearrange("(j p) n -> p j n", p=P)

        def piece(key):
            return ring[:, PLACE[key] % RING, :].rearrange("p (j n) -> p j n", j=KC)

        def landed(eng, key):
            eng.wait_ge(w_in[PLACE[key] % RING], 16 * (PLACE[key] // RING + 1))

        last_read = {}
        for n in range(ADA_PC):
            last_read[("ada", 0, n)] = (ada_p, n + 1)
            last_read[("ada", 1, n)] = (ada_p, ADA_PC + n + 1)
        last_read[("pw1", 0, 0)] = last_read[("pw1", 0, 2)] = (pw1_p, KC)
        last_read[("pw1", 0, 1)] = last_read[("pw1", 0, 3)] = (pw1_p, 2 * KC)
        last_read[("pw2", 0, 0)], last_read[("pw2", 0, 1)] = (pw2_p, KC // 2), (pw2_p, KC)
        for n in range(4):
            last_read[("qkv", 0, n)] = (q_p, 4 * (n + 1))
        for n in range(2):
            last_read[("qkv", 0, 4 + n)] = (v_p, NT * (n + 1))
            last_read[("wo", 0, n)] = (wo_p, KC // 2 * (n + 1))
        by_place = {PLACE[k]: v for k, v in last_read.items()}

        def expert_slots(l, b):
            s = [(MOE_BASE[l] + 3 * b + k) % RING for k in range(3)]
            return s

        def expert_landed(eng, l, b, k, i):
            s = MOE_BASE[l] + 3 * b + k
            eng.wait_ge(w_in[s % RING], i * 16 + 16 * (s // RING + 1))

        def step_done(eng, m, j, step):
            eng.wait_ge(m.o_step, j * len(STEPS) + (STEPS.index(step) + 1))

        def gate_tile(s):
            return ring[:, s, :].rearrange("p (j n) -> p j n", j=KC)

        def down_tile(s):
            return ring[:, s, :].rearrange("p (j n) -> p j n", j=FC)

        block = ctx.enter_context(nc.Block())

        @block.sync
        def _(sp):
            def load(n, key):
                before_it = by_place.get(n - RING)
                if before_it is not None:
                    sp.wait_ge(*before_it)
                kind, l, m = key
                sp.dma_start(ring[:, n % RING, :].rearrange("p (j n) -> p j n", j=KC),
                             piece_src(kind, l, m)).then_inc(w_in[n % RING], 16)

            def expert_srcs(l, e):
                return [a["moe_w_gate"][l].rearrange("e (p j) n -> e p (j n)", j=KC)[e],
                        a["moe_w_up"][l].rearrange("e (p j) n -> e p (j n)", j=KC)[e],
                        a["moe_w_down"][l].rearrange("e (p j) n -> e p (j n)", j=FC)[e]]

            def experts(l):
                m = moes[l]
                for b in range(2):
                    for k, src in enumerate(expert_srcs(l, b)):
                        s = MOE_BASE[l] + 3 * b + k
                        sp.wait_ge(*by_place[s - RING])
                        sp.dma_start(ring[:, s % RING, :], src).then_inc(w_in[s % RING], 16)
                with sp.Fori(0, E // 2 - 1) as i:
                    for b in range(2):
                        for k, src in enumerate(expert_srcs(l, i * 2 + (2 + b))):
                            if k == 0:
                                sp.wait_ge(m.gate_p, i * 2 + (b + 1))
                            elif k == 1:
                                sp.wait_ge(m.up_p, i * 2 + (b + 1))
                            else:
                                sp.wait_ge(m.down_p, i * 4 + 2 * (b + 1))
                            sp.dma_start(ring[:, expert_slots(l, b)[k], :], src).then_inc(
                                w_in[expert_slots(l, b)[k]], 16)
                sp.wait_ge(m.slot_r, 1)
                n_over = sp.value_load(novI[0:1, 0:1], min_val=0, max_val=OVER)
                with sp.If(n_over > 0):
                    with sp.Fori(0, n_over) as j:
                        e = sp.value_load(ovI[0:1, 0, bass.ds(j, 1)], min_val=0, max_val=E - 1)
                        step_done(sp, m, j, "free")
                        for k, src in enumerate(expert_srcs(l, e)):
                            sp.dma_start(ring[:, expert_slots(l, 0)[k], :], src).then_inc(m.o_w, 16)
                with sp.Else():
                    sp.nop()
                sp.wait_ge(m.end, 1)

            for n, key in enumerate(SEQ_A):
                load(n, key)
            experts(0)
            for n, key in enumerate(SEQ_B):
                load(BASE_B + n, key)
            experts(1)
            sp.wait_ge(fin_c, 2 * KC // 4)
            for t in range(2):
                sp.dma_start(out[0, t * P:(t + 1) * P, :], Wt[:, t, :]).then_inc(out_w, 16)
            sp.wait_ge(out_w, 32)

        @block.gpsimd
        def _(pool):
            pool.memset(UB[:, :], 0.0).then_inc(pad_z, 1)
            pool.memset(zrow[:, :], 0.0).then_inc(pad_z, 1)
            pool.wait_ge(pad_z, 2)
            for rows in (Hs, Ys):
                pool.dma_start(rows[2 * NTOK:2 * NTOK + P, :], zrow[:, :]).then_inc(hs_pad, 16)

            def experts(l):
                m = moes[l]
                T = TL[l]
                pool.wait_ge(m.slot_r, 1)
                for t in range(T):
                    pool.wait_ge(m.rows_c, 2 * (t + 1))
                    for k in range(2):
                        pool.indirect_dma_start(
                            Hs[:, :], bass.IndirectOffsetOnAxis(ap=slot[:, k * NT + t:k * NT + t + 1].bitcast(U32), axis=0),
                            Wt[:, t, :], None).then_inc(m.scat, 16)
                pool.wait_ge(m.scat, 32 * T)
                if l == 0:
                    pool.wait_ge(hs_pad, 32)
                for b in range(2):
                    pool.nop().then_inc(m.y_free, 1)
                for b in range(2):
                    r = pool.value_load(offI[0:1, b:b + 1], min_val=0, max_val=2 * NTOK)
                    pool.dma_start(hrow[:, b, :], Hs[bass.ds(r, P), :]).then_inc(m.h_in[b], 16)
                with pool.Fori(0, E // 2) as i:
                    for b in range(2):
                        r = pool.value_load(offI[0:1, bass.ds(i * 2 + b, 1)], min_val=0, max_val=2 * NTOK)
                        pool.wait_ge(m.y0_c, i * 2 + (b + 2))
                        pool.wait_ge(m.y1_c, i * 2 + (b + 2))
                        pool.wait_ge(m.slot_r, 1)
                        pool.dma_start(Ys[bass.ds(r, P), :], yrow[:, b, :]).then_inc(m.y_out, 16)
                        r2 = pool.value_load(offI[0:1, bass.ds(i * 2 + (b + 2), 1)], min_val=0, max_val=2 * NTOK)
                        pool.wait_ge(m.h_t, i * 4 + 2 * (b + 1))
                        pool.wait_ge(m.scat, 32 * T)
                        pool.dma_start(hrow[:, b, :], Hs[bass.ds(r2, P), :]).then_inc(m.h_in[b], 16)
                        pool.wait_ge(m.y_out, i * 32 + 16 * (b + 1))
                        pool.nop().then_inc(m.y_free, 1)
                for b in range(2):
                    pool.wait_ge(m.h_in[b], 16 * (E // 2 + 1))
                n_over = pool.value_load(novI[0:1, 0:1], min_val=0, max_val=OVER)
                with pool.If(n_over > 0):
                    with pool.Fori(0, n_over) as j:
                        r = pool.value_load(ovI[0:1, 1, bass.ds(j, 1)], min_val=0, max_val=2 * NTOK)
                        step_done(pool, m, j, "free")
                        pool.wait_ge(m.scat, 32 * T)
                        pool.dma_start(hrow[:, 0, :], Hs[bass.ds(r, P), :]).then_inc(m.o_in, 16)
                        step_done(pool, m, j, "out")
                        r = pool.value_load(ovI[0:1, 2, bass.ds(j, 1)], min_val=0, max_val=2 * NTOK)
                        pool.dma_start(Ys[bass.ds(r, P), :], yrow[:, 0, :]).then_inc(m.o_out, 16)
                        pool.wait_ge(m.o_out, j * 16 + 16)
                with pool.Else():
                    pool.nop()
                pool.wait_ge(m.end, 1)
                for t in range(T):
                    for k, dst in enumerate((Wt, Ht)):
                        pool.indirect_dma_start(
                            dst[:, t, :], None, Ys[:, :],
                            bass.IndirectOffsetOnAxis(ap=slot[:, k * NT + t:k * NT + t + 1].bitcast(U32), axis=0)
                        ).then_inc(m.y_in, 16)

            for l in range(DEPTH):
                experts(l)

        @block.tensor
        def _(pe):
            def turn(out, in_, n=P):
                return pe.transpose(out, in_, ident[0:n, 0:n])

            def ada(l, n):
                g = l * ADA_PC + n
                landed(pe, ("ada", l, n))
                if g >= 2:
                    pe.wait_ge(ada_c, g - 1)
                w = piece(("ada", l, n))
                for q in range(4):
                    for k in range(KC):
                        mm = pe.matmul(ps[:, g % 2, 2 * q:2 * q + 2], w[:, k, q * P:(q + 1) * P], sc[:, k, :],
                                       start=(k == 0), stop=(k == KC - 1))
                mm.then_inc(ada_p, 1)

            def norm(s, sq, c0, bank):
                for k in range(KC):
                    pe.wait_ge(s.sq, k + 1)
                    mm = pe.matmul(ps[:, bank, c0:NTOK], mean, sq[:, k, c0:NTOK], start=(k == 0), stop=(k == KC - 1))
                mm.then_inc(s.ms, 1)

            def experts(l):
                m = moes[l]
                T, t0 = TL[l], T0[l]
                n = norms[f"ffn{l}"]
                pe.wait_ge(n.h, KC)
                pe.wait_ge(rw_in, 32)
                for t in range(T):
                    for k in range(KC):
                        mm = pe.matmul(ps[:, 3, t * E:(t + 1) * E], H[:, k, (t0 + t) * P:(t0 + t + 1) * P], rw[:, k, :],
                                       start=(k == 0), stop=(k == KC - 1))
                mm.then_inc(m.route_p, 1)
                for t in range(T):
                    for h in range(2):
                        g = 2 * t + h
                        if g >= 4:
                            pe.wait_ge(m.rows_c, g - 3)
                        for k in range(4):
                            mm = turn(ps[:, 4 + g % 4, k * P:(k + 1) * P],
                                      H[:, 4 * h + k, (t0 + t) * P:(t0 + t + 1) * P])
                        mm.then_inc(m.rows_t, 1)
                pe.wait_ge(m.pair_r, 1)
                for t in range(T):
                    o = ps[:, 2, t * E:(t + 1) * E]
                    for u in range(T):
                        pe.matmul(o, ones, pair[:, 1, u, :], start=(u == 0), stop=False)
                    for u in range(t):
                        pe.matmul(o, ones, pair[:, 0, u, :], start=False, stop=False)
                    pe.matmul(o, before, pair[:, 0, t, :], start=False, stop=True)
                for q in (1, 0):
                    for u in range(T):
                        mm = pe.matmul(ps[:, 2, (T + q) * E:(T + q + 1) * E], ones, pair[:, q, u, :],
                                       start=(u == 0), stop=(u == T - 1))
                mm.then_inc(m.rank_p, 1)

                def rows_turned(b, h, s):
                    hv = hrow[:, b, :].rearrange("p (n j) -> p j n", j=KC)
                    for k in range(4):
                        mm = turn(ps[:, 5 + h, k * P:(k + 1) * P], hv[:, 4 * h + k, :])
                    if s is not None:
                        mm.then_inc(s, 1)

                def product_in(b, bank, w, s):
                    for k in range(KC):
                        mm = pe.matmul(ps[:, bank, :], hT[:, b, k * P:(k + 1) * P], w[:, k, :],
                                       start=(k == 0), stop=(k == KC - 1))
                    mm.then_inc(s, 1)

                def act_turned(s):
                    av = ea.rearrange("p (n j) -> p j n", j=FC)
                    for k in range(FC):
                        mm = turn(ps[:, 2, k * P:(k + 1) * P], av[:, k, :])
                    mm.then_inc(s, 1)

                def product_down(w, s, each=True):
                    for h in range(2):
                        for k in range(FC):
                            mm = pe.matmul(ps[:, 3 + h, :], eaT[:, k * P:(k + 1) * P], w[:, k, h * 512:(h + 1) * 512],
                                           start=(k == 0), stop=(k == FC - 1))
                        if each or h:
                            mm.then_inc(s, 1)

                pe.wait_ge(m.slot_r, 1)
                pe.wait_ge(m.rows_c, 2 * T)
                pe.wait_ge(m.h_in[0], 16)
                rows_turned(0, 0, m.h_t)
                rows_turned(0, 1, m.h_t)
                with pe.Fori(0, E // 2) as i:
                    for b in range(2):
                        s = expert_slots(l, b)
                        pe.wait_ge(m.h_c, i * 2 + (b + 1))
                        expert_landed(pe, l, b, 0, i)
                        product_in(b, 0, gate_tile(s[0]), m.gate_p)
                        expert_landed(pe, l, b, 1, i)
                        product_in(b, 1, gate_tile(s[1]), m.up_p)
                        pe.wait_ge(m.h_in[1 - b], i * 16 + 16 * (1 + b))
                        rows_turned(1 - b, 0, m.h_t)
                        pe.wait_ge(m.act_r, i * 2 + (b + 1))
                        act_turned(m.act_t)
                        rows_turned(1 - b, 1, m.h_t)
                        expert_landed(pe, l, b, 2, i)
                        pe.wait_ge(m.act_c, i * 2 + (b + 1))
                        pe.wait_ge(m.y0_c, i * 2 + (b + 1))
                        pe.wait_ge(m.y1_c, i * 2 + (b + 1))
                        product_down(down_tile(s[2]), m.down_p)
                n_over = pe.value_load(novI[0:1, 0:1], min_val=0, max_val=OVER)
                pe.wait_ge(m.h_c, E + 1)
                pe.wait_ge(m.y0_c, E + 1)
                pe.wait_ge(m.y1_c, E + 1)
                pe.wait_ge(m.y_free, E + 2)
                pe.nop().then_inc(m.o_step, 1)
                with pe.If(n_over > 0):
                    with pe.Fori(0, n_over) as j:
                        s = expert_slots(l, 0)
                        pe.wait_ge(m.o_in, j * 16 + 16)
                        pe.wait_ge(m.o_w, j * 48 + 48)
                        rows_turned(0, 0, None)
                        rows_turned(0, 1, m.o_step)
                        step_done(pe, m, j, "rows")
                        product_in(0, 0, gate_tile(s[0]), m.o_step)
                        step_done(pe, m, j, "silu")
                        product_in(0, 1, gate_tile(s[1]), m.o_step)
                        step_done(pe, m, j, "act")
                        act_turned(m.o_step)
                        step_done(pe, m, j, "act_rows")
                        product_down(down_tile(s[2]), m.o_step, each=False)
                        step_done(pe, m, j, "out")
                        pe.wait_ge(m.o_out, j * 16 + 16)
                        pe.nop().then_inc(m.o_step, 1)
                with pe.Else():
                    pe.nop()
                pe.nop().then_inc(m.end, 1)
                pe.wait_ge(m.mix_r, T)
                for k in range(KC):
                    if k >= 4:
                        pe.wait_ge(m.mix_x, k - 3)
                    for t in range(T):
                        mm = turn(ps[:, 4 + k % 4, (t0 + t) * P:(t0 + t + 1) * P], Wt[:, t, k * P:(k + 1) * P])
                    mm.then_inc(m.mix_t, 1)

            def rotate(g):
                is_k, h = divmod(g, HEADS)
                pe.wait_ge(q_c, g + 1)
                if g >= 2:
                    pe.wait_ge(q_r, g - 1)
                src = K[:, h, CTX:NTOK] if is_k else Q[:, h, :]
                pe.matmul(ps[:, 5 + g % 2, 0:SEQ], rot, src, start=True, stop=True).then_inc(rot_p, 1)

            pe.wait_ge(cst_in, 16)
            pe.wait_ge(vec_in, 16 * VECS)
            turn(ps[:, 0, 0:P], rowsA[:, :])
            turn(ps[:, 0, P:P + B_ROWS], rowsB[0:B_ROWS, :], B_ROWS)
            for k in range(KC):
                mm = turn(ps[:, 1, 32 * k:32 * k + TAPS], tap_rows[0:TAPS, k * P:(k + 1) * P], TAPS)
            mm.then_inc(vec_t, 1)
            pe.wait_ge(x_in, 32)
            for k in range(KC):
                if k >= 4:
                    pe.wait_ge(x_c, k - 3)
                for t in range(NT):
                    mm = turn(ps[:, 4 + k % 4, t * P:(t + 1) * P], Wt[:, t, k * P:(k + 1) * P])
                mm.then_inc(x_t, 1)
            pe.wait_ge(c_silu, 2)
            pe.wait_ge(vec_c, 1)
            for n in range(4):
                ada(0, n)
            norm(norms["mix0"], Vt, 0, 2)
            pe.wait_ge(x_c, KC)
            for j in range(KC):
                if j >= 2:
                    pe.wait_ge(pw1_g, j - 1)
                for h in (1, 0):
                    key = ("pw1", 0, 2 * h + j // 4)
                    landed(pe, key)
                    w = piece(key)
                    for k in range(KC):
                        if j == 0 and h:
                            pe.wait_ge(norms["mix0"].h, k + 1)
                        mm = pe.matmul(ps[:, 3 + 2 * (j % 2) + h, :], w[:, k, (j % 4) * P:(j % 4 + 1) * P], H[:, k, :],
                                       start=(k == 0), stop=(k == KC - 1))
                    mm.then_inc(pw1_p, 1)
            for n in range(4, ADA_PC):
                ada(0, n)
            for n in range(ADA_PC):
                ada(1, n)
            for k in range(KC):
                pe.wait_ge(conv_a, k + 1)
                mm = pe.matmul(ps[:, 2, :], mean, Vt[:, k, :], start=(k == 0), stop=(k == KC - 1))
            mm.then_inc(mean_p, 1)
            for k in range(KC):
                pe.wait_ge(cen_sq, k + 1)
                mm = pe.matmul(ps[:, 3, :], mean, H[:, k, :], start=(k == 0), stop=(k == KC - 1))
            mm.then_inc(var_p, 1)
            pe.wait_ge(pw1_g, KC)
            for j in range(KC):
                key = ("pw2", 0, j // 4)
                landed(pe, key)
                if j >= 4:
                    pe.wait_ge(pw2_t, j - 3)
                for k in range(KC):
                    if j == 0:
                        pe.wait_ge(ln_s, k + 1)
                    mm = pe.matmul(ps[:, 4 + j % 4, :], piece(key)[:, k, (j % 4) * P:(j % 4 + 1) * P], H[:, k, :],
                                   start=(k == 0), stop=(k == KC - 1))
                mm.then_inc(pw2_p, 1)
            norm(norms["ffn0"], Vt, 0, 2)
            experts(0)

            norm(norms["mix1"], Vt, 0, 2)
            pe.wait_ge(norms["mix1"].h, KC)
            for g in range(2 * HEADS):
                is_k, h = divmod(g, HEADS)
                key = ("qkv", 0, 2 * is_k + h // 4)
                landed(pe, key)
                if g >= 2:
                    pe.wait_ge(q_c, g - 1)
                c0 = 0 if is_k else CTX
                for k in range(KC):
                    mm = pe.matmul(ps[:, 3 + g % 2, c0:NTOK], piece(key)[:, k, (h % 4) * P:(h % 4 + 1) * P],
                                   H[:, k, c0:NTOK], start=(k == 0), stop=(k == KC - 1))
                mm.then_inc(q_p, 1)
                if g >= 1:
                    rotate(g - 1)
            rotate(2 * HEADS - 1)
            for n in range(2):
                key = ("qkv", 0, 4 + n)
                landed(pe, key)
                for t in range(NT):
                    g = n * NT + t
                    if g >= 2:
                        pe.wait_ge(v_c, g - 1)
                    for k in range(KC):
                        mm = pe.matmul(ps[:, g % 2, :], H[:, k, t * P:(t + 1) * P], piece(key)[:, k, :],
                                       start=(k == 0), stop=(k == KC - 1))
                    mm.then_inc(v_p, 1)

            units = [(h, qt) for h in range(HEADS) for qt in range(2)]

            def scores(u):
                h, qt = units[u]
                if u >= 2:
                    pe.wait_ge(s_e, 2 * (u - 1))
                for c in range(2):
                    pe.matmul(ps[:, 2 * (u % 2) + c, :], Q[c * HD:(c + 1) * HD, h, qt * P:(qt + 1) * P],
                              K[c * HD:(c + 1) * HD, h, :], start=True, stop=True).then_inc(s_p, 1)

            def weights(u):
                pe.wait_ge(s_a, u + 1)
                if u >= 2:
                    pe.wait_ge(a_c, u - 1)
                for k in range(NT):
                    mm = turn(ps[:, 4 + u % 2, k * P:(k + 1) * P], pr[:, u % 2, 0, k * P:(k + 1) * P])
                mm.then_inc(a_t, 1)

            def values(h):
                pe.wait_ge(a_c, 2 * (h + 1))
                if h >= 2:
                    pe.wait_ge(o_c, h - 1)
                for k in range(NT):
                    mm = pe.matmul(ps[:, 6 + h % 2, 0:SEQ], Wt[:, k, h * P:(h + 1) * P], aT[:, h % 2, k, :],
                                   start=(k == 0), stop=(k == NT - 1))
                mm.then_inc(o_p, 1)

            pe.wait_ge(q_r, 2 * HEADS)
            pe.wait_ge(v_c, 2 * NT)
            for u in range(len(units) + 2):
                if u < len(units):
                    scores(u)
                if 1 <= u <= len(units):
                    weights(u - 1)
                if u >= 2 and u % 2 == 1:
                    values((u - 3) // 2)
            for g in range(HEADS // 2):
                pe.wait_ge(o_sq, g + 1)
                pe.matmul(ps[:, g, :], head_mean, V[:, g * 512:(g + 1) * 512], start=True, stop=True).then_inc(o_ms, 1)
            pe.wait_ge(o_n, HEADS // 2)
            for j in range(KC):
                key = ("wo", 0, j // 4)
                landed(pe, key)
                if j >= 4:
                    pe.wait_ge(wo_x, j - 3)
                for k in range(KC):
                    mm = pe.matmul(ps[:, 4 + j % 4, CTX:NTOK], piece(key)[:, k, (j % 4) * P:(j % 4 + 1) * P], O[:, k, :],
                                   start=(k == 0), stop=(k == KC - 1))
                mm.then_inc(wo_p, 1)
            norm(norms["ffn1"], Vt, CTX, 2)
            experts(1)
            norm(norms["fin"], Vt, CTX, 2)
            for t in range(2):
                for h in range(2):
                    for k in range(4):
                        pe.wait_ge(norms["fin"].h, 4 * h + k + 1)
                        mm = turn(ps[:, 4 + 2 * t + h, k * P:(k + 1) * P],
                                  H[:, 4 * h + k, CTX + t * P:CTX + (t + 1) * P])
                    mm.then_inc(fin_t, 1)

        @block.scalar
        def _(act):
            act.dma_start(cst[:, :], a["consts"]).then_inc(cst_in, 16)

            def rows(dst, src, n):
                act.dma_start(dst, src.rearrange("(r p) -> r p", p=P) if n > 1 else src).then_inc(vec_in, 16)

            flat = {k: a[k] for k in ("ada_b", "norm_mix_g", "norm_ffn_g", "conv_pw1_b", "conv_dw_b", "conv_ln_g",
                                      "conv_ln_b", "conv_pw2_b", "c")}
            flat = {k: v.rearrange("l d -> (l d)") for k, v in flat.items()}
            for dst, at, n, src in ((rowsA, A_ADA, DEPTH * MODC, flat["ada_b"]), (rowsA, A_C, KC, flat["c"]),
                                    (rowsA, A_CC, KC, a["c_ctx"]), (rowsA, A_PW1, 2 * KC, flat["conv_pw1_b"]),
                                    (rowsB, B_MIX, DEPTH * KC, flat["norm_mix_g"]),
                                    (rowsB, B_FFN, DEPTH * KC, flat["norm_ffn_g"]),
                                    (rowsB, B_FIN, KC, a["final_norm_g"]), (rowsB, B_DWB, KC, flat["conv_dw_b"]),
                                    (rowsB, B_LNG, KC, flat["conv_ln_g"]), (rowsB, B_LNB, KC, flat["conv_ln_b"]),
                                    (rowsB, B_PW2, KC, flat["conv_pw2_b"])):
                rows(dst[at:at + n, :], src, n)
            rows(rowsB[B_SUB:B_SUB + 1, :], a["diff_subln_g"], 1)
            rows(tap_rows[0:TAPS, :], a["conv_dw_w"][0], 1)
            act.dma_start(Wt[:, 0:2, :], a["ctx"][0].rearrange("(t p) d -> p t d", p=P)).then_inc(x_in, 16)
            act.dma_start(Wt[:, 2:4, :], a["x"][0].rearrange("(t p) d -> p t d", p=P)).then_inc(x_in, 16)
            act.dma_start(rw[:, :, :], a["router_w"].rearrange("(j p) e -> p j e", p=P)).then_inc(rw_in, 16)
            act.dma_start(rb[:, :], a["router_b"].partition_broadcast(P)).then_inc(rw_in, 16)
            act.dma_start(lam[:, :, :].rearrange("p a b -> p (a b)"),
                          a["diff_lambda"].rearrange("l a b -> (l a b)").partition_broadcast(P)).then_inc(lam_in, 16)

            act.wait_ge(vec_c, 1)
            act.activation(sc[:, :, 0], colA[:, A_CC:A_CC + KC], ACT.Silu).then_inc(c_silu, 1)
            act.activation(sc[:, :, 1], colA[:, A_C:A_C + KC], ACT.Silu).then_inc(c_silu, 1)

            def ada_copy(l, n):
                g = l * ADA_PC + n
                act.wait_ge(ada_p, g + 1)
                act.copy(mod[l][:, 4 * n:4 * n + 4, :].rearrange("p a b -> p (a b)"), ps[:, g % 2, 0:8]).then_inc(ada_c, 1)

            def squares(s, c0, ready):
                for k in range(KC):
                    act.wait_ge(*ready(k))
                    act.activation(Vt[:, k, c0:NTOK], X[:, k, c0:NTOK], ACT.Square).then_inc(s.sq, 1)

            def take_root(ready, bank, c0):
                act.wait_ge(ready, 1)
                act.activation(R[:, c0:NTOK], ps[:, bank, c0:NTOK], ACT.Sqrt, bias=epsc[:, 0:1]).then_inc(root, 1)

            def modulate(s, l, which, c0):
                for k in range(KC):
                    act.wait_ge(s.hr, k + 1)
                    for st in range(c0 // CTX, 2):
                        v = H[:, k, st * CTX:(st + 1) * CTX]
                        i = act.activation(v, v, ACT.Identity, bias=mod[l][:, (3 * which) * KC + k, st:st + 1],
                                           scale=modA[:, which, k, st:st + 1])
                    i.then_inc(s.h, 1)

            def experts(l):
                m = moes[l]
                T = TL[l]
                act.wait_ge(m.route_p, 1)
                act.activation(score[:, 0:T, :].rearrange("p t e -> p (t e)"), ps[:, 3, 0:T * E],
                               ACT.Sigmoid).then_inc(m.score_r, 1)
                for g in range(2 * T):
                    act.wait_ge(m.rows_t, g + 1)
                    act.copy(Wt[:, g // 2, (g % 2) * 512:(g % 2 + 1) * 512], ps[:, 4 + g % 4, :]).then_inc(m.rows_c, 1)
                act.nop().then_inc(m.y0_c, 1)
                with act.Fori(0, E // 2) as i:
                    for b in range(2):
                        act.wait_ge(m.gate_p, i * 2 + (b + 1))
                        act.activation(eg, ps[:, 0, :], ACT.Silu).then_inc(m.gate_s, 1)
                        act.wait_ge(m.down_p, i * 4 + (2 * b + 1))
                        act.wait_ge(m.y_free, i * 2 + (b + 1))
                        act.copy(yrow[:, b, 0:512], ps[:, 3, :]).then_inc(m.y0_c, 1)
                n_over = act.value_load(novI[0:1, 0:1], min_val=0, max_val=OVER)
                with act.If(n_over > 0):
                    with act.Fori(0, n_over) as j:
                        step_done(act, m, j, "gate")
                        act.activation(eg, ps[:, 0, :], ACT.Silu).then_inc(m.o_step, 1)
                with act.Else():
                    act.nop()

            for k in range(KC):
                act.wait_ge(x_t, k + 1)
                act.copy(X[:, k, :], ps[:, 4 + k % 4, :]).then_inc(x_c, 1)
            squares(norms["mix0"], 0, lambda k: (x_c, k + 1))
            for n in range(4):
                ada_copy(0, n)
            act.wait_ge(eps_r, 1)
            take_root(norms["mix0"].ms, 2, 0)
            act.wait_ge(modA_r, 1)
            modulate(norms["mix0"], 0, 0, 0)
            for j in range(KC):
                act.wait_ge(pw1_p, 2 * j + 1)
                if j >= 2:
                    act.wait_ge(pw1_g, j - 1)
                act.activation(sg[:, j % 2, :], ps[:, 4 + 2 * (j % 2), :], ACT.Sigmoid,
                               bias=colA[:, A_PW1 + KC + j:A_PW1 + KC + j + 1]).then_inc(pw1_s, 1)
            for n in range(4, ADA_PC):
                ada_copy(0, n)
            for n in range(ADA_PC):
                ada_copy(1, n)
            for k in range(KC):
                act.wait_ge(cen, k + 1)
                act.activation(H[:, k, :], Vt[:, k, :], ACT.Square).then_inc(cen_sq, 1)
            take_root(var_p, 3, 0)
            for k in range(KC):
                act.wait_ge(lnz, k + 1)
                act.activation(H[:, k, :], Vt[:, k, :], ACT.Silu, bias=colB[:, B_LNB + k:B_LNB + k + 1],
                               scale=colB[:, B_LNG + k:B_LNG + k + 1]).then_inc(ln_s, 1)
            act.wait_ge(modA_r, 2)
            for j in range(KC):
                act.wait_ge(pw2_p, j + 1)
                if j >= 2:
                    act.wait_ge(pw2_x, j - 1)
                for st in range(2):
                    cs = slice(st * CTX, (st + 1) * CTX)
                    i = act.activation(sg[:, j % 2, cs], ps[:, 4 + j % 4, cs], ACT.Identity,
                                       bias=gb2[:, j, st:st + 1], scale=mod[0][:, 2 * KC + j, st:st + 1])
                i.then_inc(pw2_t, 1)
            squares(norms["ffn0"], 0, lambda k: (pw2_x, k + 1))
            take_root(norms["ffn0"].ms, 2, 0)
            modulate(norms["ffn0"], 0, 1, 0)
            experts(0)
            squares(norms["mix1"], 0, lambda k: (moes[0].mix_x, k + 1))
            take_root(norms["mix1"].ms, 2, 0)
            act.wait_ge(modB_r, 1)
            modulate(norms["mix1"], 1, 0, 0)
            for g in range(2 * HEADS):
                is_k, h = divmod(g, HEADS)
                act.wait_ge(q_p, g + 1)
                if is_k:
                    i = act.copy(K[:, h, :], ps[:, 3 + g % 2, :])
                else:
                    i = act.copy(Q[:, h, :], ps[:, 3 + g % 2, CTX:NTOK])
                i.then_inc(q_c, 1)
            for g in range(2 * NT):
                act.wait_ge(v_p, g + 1)
                act.copy(Wt[:, g % NT, (g // NT) * 512:(g // NT + 1) * 512], ps[:, g % 2, :]).then_inc(v_c, 1)

            def turned_copy(u):
                h, qt = divmod(u, 2)
                act.wait_ge(a_t, u + 1)
                if u >= 4:
                    act.wait_ge(o_p, h - 1)
                act.copy(aT[:, h % 2, :, qt * P:(qt + 1) * P],
                         ps[:, 4 + u % 2, :].rearrange("p (k t) -> p k t", k=NT)).then_inc(a_c, 1)

            act.wait_ge(lam_s, 1)
            for k in range(2):
                act.activation(lamt[:, 2 + k:3 + k], lamt[:, k:k + 1], ACT.Exp).then_inc(lam_e, 1)
            for u in range(2 * HEADS):
                b = u % 2
                for c in range(2):
                    act.wait_ge(s_m, 2 * u + c + 1)
                    if u >= 2:
                        act.wait_ge(a_t, u - 1)
                    act.activation(pr[:, b, c, :], ps[:, 2 * b + c, :], ACT.Exp, bias=sm[:, b, c, 0:1], scale=SCALE,
                                   accum_out=sm[:, b, c, 1:2]).then_inc(s_e, 1)
                if u >= 1:
                    turned_copy(u - 1)
            turned_copy(2 * HEADS - 1)
            for g in range(HEADS // 2):
                act.wait_ge(o_c, 2 * (g + 1))
                act.activation(V[:, g * 512:(g + 1) * 512], OF[:, g * 512:(g + 1) * 512], ACT.Square).then_inc(o_sq, 1)
            for g in range(HEADS // 2):
                act.wait_ge(o_ms, g + 1)
                act.activation(UB[:, g * 512:(g + 1) * 512], ps[:, g, :], ACT.Sqrt, bias=epsc[:, 0:1]).then_inc(root, 1)
            squares(norms["ffn1"], CTX, lambda k: (wo_x, k + 1))
            take_root(norms["ffn1"].ms, 2, CTX)
            modulate(norms["ffn1"], 1, 1, CTX)
            experts(1)
            squares(norms["fin"], CTX, lambda k: (moes[1].mix_x, k + 1))
            take_root(norms["fin"].ms, 2, CTX)
            for g in range(4):
                act.wait_ge(fin_t, g + 1)
                act.copy(Wt[:, g // 2, (g % 2) * 512:(g % 2 + 1) * 512], ps[:, 4 + g, :]).then_inc(fin_c, 1)

        @block.vector
        def _(v):
            count = [0]

            def link(i):
                count[0] += 1
                i.then_inc(dve, 1)
                v.wait_ge(dve, count[0])

            def bc(ap, shape):
                return ap.to_broadcast(shape)

            def rstd(name, c0):
                v.wait_ge(root, ROOTS[name])
                link(v.reciprocal(R[:, c0:NTOK], R[:, c0:NTOK]))

            def norm(name, c0):
                s = norms[name]
                rstd(name, c0)
                for k in range(KC):
                    v.tensor_tensor(H[:, k, c0:NTOK], X[:, k, c0:NTOK], R[:, c0:NTOK], ALU.mult).then_inc(s.hr, 1)

            def bias_mods(l, a0, a1):
                link(v.tensor_tensor(mod[l][:, a0:a1, :], mod[l][:, a0:a1, :],
                                     colA[:, A_ADA + l * MODC + a0:A_ADA + l * MODC + a1].unsqueeze(2).to_broadcast([P, a1 - a0, 2]), ALU.add))

            def gain(l, which):
                at = (B_FFN if which else B_MIX) + l * KC
                return v.scalar_tensor_tensor(modA[:, which, :, :], mod[l][:, (3 * which + 1) * KC:(3 * which + 2) * KC, :],
                                              1.0, colB[:, at:at + KC].unsqueeze(2).to_broadcast([P, KC, 2]), ALU.add, ALU.mult)

            def experts(l):
                m = moes[l]
                T, t0 = TL[l], T0[l]
                G4 = T * GROUPS

                def te(x):
                    return x[:, 0:T, :]

                def per_tok(x):
                    return x.unsqueeze(2).to_broadcast([P, T, E])

                def tok(n):
                    return t1[:, n, 0:T]

                ekey = cst[:, C_EKEY:C_EKEY + T * E].rearrange("p (t e) -> p t e", t=T)
                gkey = cst[:, C_GKEY:C_GKEY + G4].rearrange("p (t g) -> p t g", t=T)
                v.wait_ge(m.score_r, 1)
                if l == 0:
                    v.wait_ge(rw_in, 32)
                link(v.tensor_tensor(te(sel), te(score), rb[:, :].unsqueeze(1).to_broadcast([P, T, E]), ALU.add))
                s4 = te(sel).rearrange("p t (g i) -> p (t g) i", i=GS)

                def q(n):
                    return g4[:, n, 0:G4]

                v.tensor_tensor(q(0), s4[:, :, 0], s4[:, :, 1], ALU.max)
                v.tensor_tensor(q(1), s4[:, :, 0], s4[:, :, 1], ALU.min)
                v.tensor_tensor(q(2), s4[:, :, 2], s4[:, :, 3], ALU.max)
                link(v.tensor_tensor(q(3), s4[:, :, 2], s4[:, :, 3], ALU.min))
                v.tensor_tensor(q(4), q(0), q(2), ALU.max)
                v.tensor_tensor(q(5), q(0), q(2), ALU.min)
                link(v.tensor_tensor(q(6), q(1), q(3), ALU.max))
                link(v.tensor_tensor(q(5), q(5), q(6), ALU.max))
                link(v.tensor_tensor(q(7), q(4), q(5), ALU.add))

                def tg(n):
                    return q(n).rearrange("p (t g) -> p t g", t=T)

                def tok_g(n):
                    return tok(n).unsqueeze(2).to_broadcast([P, T, GROUPS])

                link(v.tensor_reduce(tok(0), tg(7), AX.X, ALU.max))
                link(v.tensor_tensor(tg(8), tg(7), tok_g(0), ALU.is_equal))
                link(v.tensor_tensor(tg(8), tg(8), gkey, ALU.mult))
                link(v.tensor_reduce(tok(1), tg(8), AX.X, ALU.max))
                link(v.tensor_tensor(tg(9), tg(8), tok_g(1), ALU.is_equal))
                m4 = te(msel).rearrange("p t (g i) -> p (t g) i", i=GS)
                in_g = q(9).unsqueeze(2).to_broadcast([P, G4, GS])
                link(v.tensor_tensor(m4, s4, in_g, ALU.mult))
                link(v.tensor_scalar(q(8), q(9), -1.0, BIG, ALU.add, ALU.mult))
                link(v.tensor_tensor(m4, m4, q(8).unsqueeze(2).to_broadcast([P, G4, GS]), ALU.add))
                for k in range(2):
                    one = oh[:, k, 0:T, :]
                    link(v.tensor_reduce(tok(2), te(msel), AX.X, ALU.max))
                    link(v.tensor_tensor(te(tA), te(msel), per_tok(tok(2)), ALU.is_equal))
                    link(v.tensor_tensor(te(tA), te(tA), ekey, ALU.mult))
                    link(v.tensor_reduce(tok(3), te(tA), AX.X, ALU.max))
                    link(v.tensor_tensor(one, te(tA), per_tok(tok(3)), ALU.is_equal))
                    link(v.tensor_tensor(te(tA) if k else te(tB), ekey, per_tok(tok(3)), ALU.is_lt))
                    if k == 0:
                        link(v.scalar_tensor_tensor(te(msel), one, -3.0 * BIG, te(msel), ALU.mult, ALU.add))
                v.tensor_tensor(pair[:, 1, 0:T, :], te(tA), te(tB), ALU.add)
                v.tensor_tensor(pair[:, 0, 0:T, :], oh[:, 0, 0:T, :], oh[:, 1, 0:T, :], ALU.add).then_inc(m.pair_r, 1)
                for k in range(2):
                    link(v.tensor_tensor(te(sel), te(score), oh[:, k, 0:T, :], ALU.mult))
                    link(v.tensor_reduce(tok(4 + k), te(sel), AX.X, ALU.add))
                link(v.tensor_tensor(tok(6), tok(4), tok(5), ALU.add))
                link(v.reciprocal(tok(7), tok(6)))
                for k in range(2):
                    link(v.tensor_tensor(wk[:, k, 0:T], tok(4 + k), tok(7), ALU.mult))
                v.wait_ge(m.rank_p, 1)
                for k in range(2):
                    rank = ps[:, 2, 0:T * E].rearrange("p (t e) -> p t e", t=T)
                    link(v.tensor_tensor(te(tA), rank, oh[:, k, 0:T, :], ALU.mult))
                    link(v.tensor_reduce(tok(8 + k), te(tA), AX.X, ALU.add))
                    link(v.tensor_copy(slot[:, k * NT:k * NT + T], tok(8 + k)))
                off, num = ints[:, 0, 0:E], ints[:, 1, 0:E]
                link(v.memset(ints[:, 0, E:24], float(2 * T * P)))
                link(v.tensor_copy(num, ps[:, 2, T * E:(T + 1) * E]))
                link(v.tensor_copy(off, ps[:, 2, (T + 1) * E:(T + 2) * E]))
                link(v.tensor_copy(offI[:, :], ints[:, 0, :]))
                link(v.memset(cum[:, :, :], 0.0))
                link(v.tensor_scalar(tA[:, 0, :], num, float(P), None, ALU.is_gt))
                for k in range(2, NT):
                    link(v.scalar_tensor_tensor(tA[:, 0, :], num, float(k * P), tA[:, 0, :], ALU.is_gt, ALU.add))
                link(v.tensor_copy(cum[:, 0, 8:8 + E], tA[:, 0, :]))
                src = 0
                for step in (1, 2, 4, 8):
                    link(v.tensor_tensor(cum[:, 1 - src, 8:8 + E], cum[:, src, 8:8 + E],
                                         cum[:, src, 8 - step:8 + E - step], ALU.add))
                    src = 1 - src
                up_to = cum[:, src, 8:8 + E]
                link(v.tensor_copy(novI[:, :], cum[:, src, 8 + E - 1:8 + E]))

                def oe(n):
                    return ov[:, n, :].rearrange("p (i e) -> p i e", e=E)

                def over_e(x):
                    return x.unsqueeze(1).to_broadcast([P, OVER, E])

                passes = cst[:, C_PASS:C_PASS + OVER * E].rearrange("p (i e) -> p i e", e=E)
                expert = cst[:, C_EXP:C_EXP + OVER * E].rearrange("p (i e) -> p i e", e=E)
                link(v.tensor_tensor(oe(0), over_e(up_to), passes, ALU.is_le))
                link(v.tensor_reduce(ovf[:, 0, 0:OVER], oe(0), AX.X, ALU.add))
                link(v.tensor_tensor(oe(1), expert, ovf[:, 0, 0:OVER].unsqueeze(2).to_broadcast([P, OVER, E]), ALU.is_equal))
                link(v.tensor_tensor(tB[:, 0, :], up_to, tA[:, 0, :], ALU.subtract))
                link(v.tensor_tensor(oe(2), passes, over_e(tB[:, 0, :]), ALU.subtract))
                link(v.tensor_scalar(oe(2), oe(2), 1.0, float(P), ALU.add, ALU.mult))
                link(v.tensor_tensor(oe(2), oe(2), over_e(off), ALU.add))
                link(v.tensor_tensor(tB[:, 1, :], off, num, ALU.add))
                link(v.tensor_scalar(tB[:, 1, :], tB[:, 1, :], -float(P), None, ALU.add))
                link(v.tensor_tensor(oe(2), oe(2), over_e(tB[:, 1, :]), ALU.min))
                link(v.tensor_tensor(oe(2), oe(2), oe(1), ALU.mult))
                link(v.tensor_reduce(ovf[:, 1, 0:OVER], oe(2), AX.X, ALU.add))
                for k in range(3):
                    link(v.tensor_copy(ovI[:, k, 0:OVER], ovf[:, min(k, 1), 0:OVER]))
                v.tensor_copy(R[:, 0:1], R[:, 0:1]).then_inc(m.slot_r, 1)

                def rows_copy(b, h):
                    return v.tensor_copy(hT[:, b, h * 512:(h + 1) * 512], ps[:, 5 + h, :])

                v.wait_ge(m.h_t, 1)
                rows_copy(0, 0)
                v.wait_ge(m.h_t, 2)
                rows_copy(0, 1).then_inc(m.h_c, 1)
                v.nop().then_inc(m.y1_c, 1)
                with v.Fori(0, E // 2) as i:
                    for b in range(2):
                        v.wait_ge(m.gate_s, i * 2 + (b + 1))
                        v.wait_ge(m.up_p, i * 2 + (b + 1))
                        v.tensor_tensor(ea, eg, ps[:, 1, :], ALU.mult).then_inc(m.act_r, 1)
                        v.wait_ge(m.h_t, i * 4 + (2 * b + 3))
                        rows_copy(1 - b, 0)
                        v.wait_ge(m.act_t, i * 2 + (b + 1))
                        v.tensor_copy(eaT, ps[:, 2, :]).then_inc(m.act_c, 1)
                        v.wait_ge(m.h_t, i * 4 + (2 * b + 4))
                        rows_copy(1 - b, 1).then_inc(m.h_c, 1)
                        v.wait_ge(m.down_p, i * 4 + (2 * b + 2))
                        v.wait_ge(m.y_free, i * 2 + (b + 1))
                        v.tensor_copy(yrow[:, b, 512:1024], ps[:, 4, :]).then_inc(m.y1_c, 1)
                n_over = v.value_load(novI[0:1, 0:1], min_val=0, max_val=OVER)
                with v.If(n_over > 0):
                    with v.Fori(0, n_over) as j:
                        step_done(v, m, j, "turned")
                        rows_copy(0, 0)
                        rows_copy(0, 1).then_inc(m.o_step, 1)
                        step_done(v, m, j, "up")
                        v.tensor_tensor(ea, eg, ps[:, 1, :], ALU.mult).then_inc(m.o_step, 1)
                        step_done(v, m, j, "act_turned")
                        v.tensor_copy(eaT, ps[:, 2, :]).then_inc(m.o_step, 1)
                        step_done(v, m, j, "down")
                        v.tensor_copy(yrow[:, 0, 0:512], ps[:, 3, :])
                        v.tensor_copy(yrow[:, 0, 512:1024], ps[:, 4, :]).then_inc(m.o_step, 1)
                with v.Else():
                    v.nop()
                v.wait_ge(m.y_in, 32 * T)
                for t in range(T):
                    link(v.tensor_scalar(Wt[:, t, :], Wt[:, t, :], wk[:, 0, t:t + 1], None, ALU.mult))
                    v.scalar_tensor_tensor(Wt[:, t, :], Ht[:, t, :], wk[:, 1, t:t + 1], Wt[:, t, :],
                                           ALU.mult, ALU.add).then_inc(m.mix_r, 1)
                for k in range(KC):
                    v.wait_ge(m.mix_t, k + 1)
                    for st in range(t0 // 2, 2):
                        cs = slice(st * CTX, (st + 1) * CTX)
                        i = v.scalar_tensor_tensor(X[:, k, cs], ps[:, 4 + k % 4, cs], mod[l][:, 5 * KC + k, st:st + 1],
                                                   X[:, k, cs], ALU.mult, ALU.add)
                    i.then_inc(m.mix_x, 1)

            v.memset(epsc[:, :], EPS).then_inc(eps_r, 1)
            v.wait_ge(vec_t, 1)
            link(v.tensor_copy(colA[:, :], ps[:, 0, 0:P]))
            link(v.tensor_copy(colB[:, :], ps[:, 0, P:P + B_ROWS]))
            v.tensor_copy(cw[:, :, 0:TAPS], ps[:, 1, 0:256].rearrange("p (j t) -> p j t", j=KC)[:, :, 0:TAPS]).then_inc(vec_c, 1)
            v.wait_ge(vec_c, 1)
            v.wait_ge(ada_c, 4)
            bias_mods(0, 0, 16)
            gain(0, 0).then_inc(modA_r, 1)
            v.wait_ge(x_c, KC)
            norm("mix0", 0)
            v.wait_ge(pad_z, 1)
            for j in range(KC):
                v.wait_ge(pw1_p, 2 * j + 2)
                v.wait_ge(pw1_s, j + 1)
                v.scalar_tensor_tensor(U[:, j, :, PAD:PAD + SEQ],
                                       ps[:, 3 + 2 * (j % 2), :].rearrange("p (s t) -> p s t", s=2),
                                       colA[:, A_PW1 + j:A_PW1 + j + 1],
                                       sg[:, j % 2, :].rearrange("p (s t) -> p s t", s=2),
                                       ALU.add, ALU.mult).then_inc(pw1_g, 1)
            v.wait_ge(pw1_g, KC)
            for j in range(0, KC, 2):
                for tap in range(TAPS):
                    for jj in (j, j + 1):
                        o = Vt[:, jj, :].rearrange("p (s t) -> p s t", s=2)
                        src = U[:, jj, :, tap:tap + SEQ]
                        w = cw[:, jj, tap:tap + 1]
                        if tap == 0:
                            i = v.tensor_scalar(o, src, w, colB[:, B_DWB + jj:B_DWB + jj + 1], ALU.mult, ALU.add)
                        else:
                            v.wait_ge(dve, count[0] - (0 if tap == TAPS - 1 and jj > j else 1))
                            i = v.scalar_tensor_tensor(o, src, w, o, ALU.mult, ALU.add)
                        if tap < TAPS - 1:
                            i.then_inc(dve, 1)
                            count[0] += 1
                        else:
                            i.then_inc(conv_a, 1)
            v.wait_ge(ada_c, 2 * ADA_PC)
            bias_mods(0, 16, MODC)
            bias_mods(1, 0, MODC)
            link(gain(0, 1))
            v.tensor_tensor(gb2[:, :, :], mod[0][:, 2 * KC:3 * KC, :],
                            colB[:, B_PW2:B_PW2 + KC].unsqueeze(2).to_broadcast([P, KC, 2]), ALU.mult).then_inc(modA_r, 1)
            v.wait_ge(mean_p, 1)
            v.wait_ge(conv_a, KC)
            for k in range(KC):
                v.tensor_tensor(Vt[:, k, :], Vt[:, k, :], ps[:, 2, :], ALU.subtract).then_inc(cen, 1)
            rstd("ln", 0)
            v.wait_ge(cen, KC)
            for k in range(KC):
                v.tensor_tensor(Vt[:, k, :], Vt[:, k, :], R[:, :], ALU.mult).then_inc(lnz, 1)
            for j in range(KC):
                v.wait_ge(pw2_t, j + 1)
                v.tensor_tensor(X[:, j, :], X[:, j, :], sg[:, j % 2, :], ALU.add).then_inc(pw2_x, 1)
            v.wait_ge(pw2_x, KC)
            norm("ffn0", 0)
            experts(0)

            v.wait_ge(norms["ffn0"].h, KC)
            link(gain(1, 0))
            gain(1, 1).then_inc(modB_r, 1)
            v.wait_ge(moes[0].mix_x, KC)
            norm("mix1", 0)
            v.wait_ge(lam_in, 16)
            for k in range(2):
                link(v.tensor_tensor(lam[:, 2 * k, :], lam[:, 2 * k, :], lam[:, 2 * k + 1, :], ALU.mult))
                link(v.tensor_reduce(lamt[:, k:k + 1], lam[:, 2 * k, :], AX.X, ALU.add))
            v.nop().then_inc(lam_s, 1)
            link(v.tensor_scalar(subg[:, :], colB[:, B_SUB:B_SUB + 1], 1.0 - LAM_INIT, None, ALU.mult))
            cos, sin = cst[:, C_COS:C_COS + SEQ], cst[:, C_SIN:C_SIN + SEQ]
            for g in range(2 * HEADS):
                is_k, h = divmod(g, HEADS)
                t = K[:, h, CTX:NTOK] if is_k else Q[:, h, :]
                v.wait_ge(rot_p, g + 1)
                part = R[:, (g % 2) * SEQ:(g % 2 + 1) * SEQ]
                if g >= 2:
                    v.wait_ge(q_r, g - 1)
                v.tensor_tensor(part, ps[:, 5 + g % 2, 0:SEQ], sin, ALU.mult)
                link(v.tensor_tensor(t, t, cos, ALU.mult))
                v.tensor_tensor(t, t, part, ALU.add).then_inc(q_r, 1)
            v.wait_ge(lam_e, 2)
            link(v.tensor_tensor(lamt[:, 4:5], lamt[:, 3:4], lamt[:, 2:3], ALU.subtract))
            link(v.tensor_scalar(lamt[:, 5:6], lamt[:, 4:5], -LAM_INIT, None, ALU.add))

            def maxima(u):
                b = u % 2
                for c in range(2):
                    v.wait_ge(s_p, 2 * u + c + 1)
                    if u >= 2:
                        v.wait_ge(s_e, 2 * (u - 2) + c + 1)
                    link(v.tensor_reduce(sm[:, b, c, 2:3], ps[:, 2 * b + c, :], AX.X, ALU.max))
                    v.tensor_scalar(sm[:, b, c, 0:1], sm[:, b, c, 2:3], -SCALE, None, ALU.mult).then_inc(s_m, 1)

            def combine(u):
                b = u % 2
                v.wait_ge(s_e, 2 * u + 2)
                link(v.reciprocal(sm[:, b, :, 3], sm[:, b, :, 1]))
                link(v.tensor_tensor(sm[:, b, 1, 3:4], sm[:, b, 1, 3:4], lamt[:, 5:6], ALU.mult))
                link(v.tensor_scalar(pr[:, b, 0, :], pr[:, b, 0, :], sm[:, b, 0, 3:4], None, ALU.mult))
                v.scalar_tensor_tensor(pr[:, b, 0, :], pr[:, b, 1, :], sm[:, b, 1, 3:4], pr[:, b, 0, :],
                                       ALU.mult, ALU.add).then_inc(s_a, 1)

            def out_copy(h):
                v.wait_ge(o_p, h + 1)
                v.tensor_copy(O[:, h, :], ps[:, 6 + h % 2, 0:SEQ]).then_inc(o_c, 1)

            for u in range(2 * HEADS + 1):
                if u < 2 * HEADS:
                    maxima(u)
                if u >= 1:
                    combine(u - 1)
                if u >= 4 and u % 2 == 0:
                    out_copy(u // 2 - 2)
            out_copy(HEADS - 1)
            for g in range(HEADS // 2):
                v.wait_ge(root, ROOTS["heads"] + g)
                r = UB[:, g * 512:(g + 1) * 512]
                link(v.reciprocal(r, r))
                o = OF[:, g * 512:(g + 1) * 512]
                if g == 0:
                    v.wait_ge(o_c, HEADS)
                v.scalar_tensor_tensor(o, o, subg[:, 0:1], r, ALU.mult, ALU.mult).then_inc(o_n, 1)
            for j in range(KC):
                v.wait_ge(wo_p, j + 1)
                v.scalar_tensor_tensor(X[:, j, CTX:NTOK], ps[:, 4 + j % 4, CTX:NTOK], mod[1][:, 2 * KC + j, 1:2],
                                       X[:, j, CTX:NTOK], ALU.mult, ALU.add).then_inc(wo_x, 1)
            v.wait_ge(wo_x, KC)
            norm("ffn1", CTX)
            experts(1)
            s = norms["fin"]
            v.wait_ge(moes[1].mix_x, KC)
            rstd("fin", CTX)
            for k in range(KC):
                v.scalar_tensor_tensor(H[:, k, CTX:NTOK], X[:, k, CTX:NTOK], colB[:, B_FIN + k:B_FIN + k + 1],
                                       R[:, CTX:NTOK], ALU.mult, ALU.mult).then_inc(s.h, 1)


_INS = ["x", "c", "ctx", "c_ctx", "ada_w", "ada_b", "norm_mix_g", "norm_ffn_g", "final_norm_g",
        "conv_pw1_w", "conv_pw1_b", "conv_dw_w", "conv_dw_b", "conv_ln_g", "conv_ln_b", "conv_pw2_w",
        "conv_pw2_b", "diff_w_qkv", "diff_lambda", "diff_subln_g", "diff_w_o", "router_w", "router_b",
        "moe_w_gate", "moe_w_up", "moe_w_down"]


def kernel(**inputs):
    import numpy as _np
    import concourse.bacc as _bacc
    from concourse import mybir as _mybir
    from concourse.bass_utils import run_bass_kernel_spmd as _run

    nc = _bacc.Bacc("TRN2", target_bir_lowering=False, num_devices=1)
    arrays, aps = {}, {}
    given = {name: _np.ascontiguousarray(inputs[name]) for name in _INS}
    given["consts"] = constants()
    for name, arr in given.items():
        arrays[f"in_{name}"] = arr
        aps[name] = nc.dram_tensor(f"in_{name}", arr.shape, _mybir.dt.from_np(arr.dtype), kind="ExternalInput").ap()
    out = nc.dram_tensor("out_0", (1, SEQ, D), F32, kind="ExternalOutput").ap()
    build(nc, aps, out)
    r = _run(nc, [arrays], core_ids=[0])
    return r.results[0]["out_0"]
```

```python
from contextlib import ExitStack
import math

import numpy as np

import concourse.bass as bass
from concourse import mybir

F32 = mybir.dt.float32
I32 = mybir.dt.int32
U32 = mybir.dt.uint32
ALU = mybir.AluOpType
ACT = mybir.ActivationFunctionType
AX = mybir.AxisListType

P = 128
D = 1024
KC = D // P
SEQ, CTX = 256, 256
NTOK = SEQ + CTX
NT = NTOK // P
DEPTH = 2
ADA = 6
MODC = ADA * KC
TAPS = 31
PAD = TAPS // 2
UW = SEQ + 2 * PAD
HEADS = 8
HD = 64
E = 16
GROUPS = 4
GS = E // GROUPS
FE = 512
FC = FE // P
EPS = 1e-6
LAM_INIT = 0.8 - 0.6 * math.exp(-0.3 * 1)
SCALE = HD ** -0.5
GRID_W = 64
FREQS = HD // 4
THETA = 10000.0
OVER = 2 * NTOK // (P + 1)
PIECE = KC * FE
RING = 6
BIG = 1e30
QW = 32
QUADS = P // QW

C_ID, C_MEAN, C_HEAD, C_ONE, C_BEFORE, C_ROT = (P * k for k in range(6))
C_COS = 6 * P
C_SIN = C_COS + SEQ
C_EKEY = C_SIN + SEQ
C_GKEY = C_EKEY + NT * E
C_PASS = C_GKEY + NT * GROUPS
C_EXP = C_PASS + OVER * E
C_SEL = C_EXP + OVER * E
C_SELE = C_SEL + 2
C_END = C_SELE + E

STEPS = ("free", "turned", "rows", "gate", "silu", "up", "act", "act_turned", "act_rows", "down", "out")

A_ADA, A_C, A_CC, A_PW1 = 0, DEPTH * MODC, DEPTH * MODC + KC, DEPTH * MODC + 2 * KC
B_MIX, B_FFN, B_FIN, B_DWB, B_LNG, B_LNB, B_PW2, B_SUB = 0, 16, 32, 40, 48, 56, 64, 72
B_ROWS = 73

TM = [P, P // 2]

ADA_PC = ADA * D // FE
REST = [("ada", 0, n) for n in range(4, ADA_PC)] + [("ada", 1, n) for n in range(ADA_PC)]
SEQ_A = ([(("ada", 0, 0), 4), (("ada", 0, 1), 5), (("ada", 0, 2), 0), (("ada", 0, 3), 1),
          (("pw1", 0, 0), 2), (("pw1", 0, 2), 3)]
         + [(REST[0], 4), (REST[1], 5), (REST[2], 6), (("pw1", 0, 1), 0), (("pw1", 0, 3), 1)]
         + [(key, (4, 5, 6)[n % 3]) for n, key in enumerate(REST) if n >= 3]
         + [(("pw2", 0, 0), 2), (("pw2", 0, 1), 3)])
SEQ_B = [(("qkv", 0, n), slot) for n, slot in zip((0, 2, 4, 1, 3, 5), (0, 1, 4, 5, 2, 3))] + [(("wo", 0, 0), 0), (("wo", 0, 1), 1)]
SETS = [((0, 1, 4), (5, 2, 3)), ((4, 5, 2), (3, 0, 1))]
FILL = [range(n, n + 2) for n in range(4, 12, 2)] + [range(n, n + 3) for n in range(12, 24, 3)]

UNITS = 2 * HEADS
PLAN = []
for _i in range(12):
    PLAN += [("product", _i)] + ([("rotate", _i - 1)] if 1 <= _i <= 8 else [])
_next = 12
for _u in range(UNITS + 3):
    if _u < UNITS:
        PLAN.append(("scores", _u))
    if _u >= 4 and _u % 2 == 0:
        PLAN.append(("values", (_u - 3) // 2))
    if 2 <= _u < UNITS + 2:
        PLAN.append(("weights", _u - 2))
    for _ in range((2 - _u % 2) if _u < UNITS // 2 else 0):
        PLAN.append(("product", _next))
        if 13 <= _next <= 20:
            PLAN.append(("rotate", _next - 5))
        _next += 1
    if 1 <= _u <= UNITS:
        PLAN.append(("combine", _u - 1))

PLACE, _held = {}, [[] for _ in range(RING + 1)]
for _l, _seq in enumerate((SEQ_A, SEQ_B)):
    for _key, _slot in _seq:
        PLACE[_key] = (_slot, len(_held[_slot]), _held[_slot][-1] if _held[_slot] else None)
        _held[_slot].append(_key)
    for _b in range(2):
        for _k in range(3):
            _slot = SETS[_l][_b][_k]
            PLACE[("moe", _l, _b, _k)] = (_slot, len(_held[_slot]), _held[_slot][-1])
            _held[_slot] += [("moe", _l, _b, _k)] * (E // 2)


def constants():
    c = np.zeros((P, C_END), np.float32)
    i = np.arange(P)
    c[:, C_ID:C_ID + P] = np.eye(P)
    c[:, C_MEAN:C_MEAN + P] = 1.0 / D
    c[:, C_HEAD:C_HEAD + P] = 1.0 / P
    c[:, C_ONE:C_ONE + P] = 1.0
    c[:, C_BEFORE:C_BEFORE + P] = i[:, None] < i[None, :]
    half = (i // FREQS) % 2
    for m in range(P):
        if half[m]:
            c[m - FREQS, C_ROT + m] = 1.0
        else:
            c[m + FREQS, C_ROT + m] = -1.0
    axis, f = (i // (2 * FREQS)) % 2, i % FREQS
    tok = np.arange(SEQ)
    inv = (THETA ** (-np.arange(FREQS, dtype=np.float64) / FREQS)).astype(np.float32)
    pos = np.where(axis[:, None] == 0, tok[None, :] // GRID_W, tok[None, :] % GRID_W).astype(np.float32)
    ang = pos * inv[f][:, None]
    c[:, C_COS:C_COS + SEQ] = np.cos(ang)
    c[:, C_SIN:C_SIN + SEQ] = np.sin(ang)
    c[:, C_EKEY:C_EKEY + NT * E] = np.tile(E - np.arange(E), NT)
    c[:, C_GKEY:C_GKEY + NT * GROUPS] = np.tile(GROUPS - np.arange(GROUPS), NT)
    c[:, C_PASS:C_PASS + OVER * E] = np.repeat(np.arange(OVER), E)
    c[:, C_EXP:C_EXP + OVER * E] = np.tile(np.arange(E), OVER)
    for s in range(2):
        c[s::QW, C_SEL + s] = 1.0
    for e in range(E):
        c[e::QW, C_SELE + e] = 1.0
    return c


def build(nc, a, out):
    with ExitStack() as ctx:
        def sb(name, shape, dt=F32):
            return ctx.enter_context(nc.sbuf_tensor(name, shape, dt))

        def sem(name):
            return ctx.enter_context(nc.semaphore(name))

        ring = sb("ring", [P, RING, PIECE])
        X = sb("X", [P, KC, NTOK])
        H = sb("H", [P, KC, NTOK])
        UB = sb("UB", [P, KC * 2 * UW])
        V = sb("V", [P, KC * NTOK])
        W = sb("W", [P, NT * D])
        cst = sb("cst", [P, C_END])
        rowsA = sb("rowsA", [P, P])
        rowsB = sb("rowsB", [P, P])
        colA = sb("colA", [P, P])
        colB = sb("colB", [P, B_ROWS])
        cw = sb("cw", [P, KC, 32])
        rw = sb("rw", [P, KC, QW])
        rb = sb("rb", [P, E])
        sc = sb("sc", [P, KC, QW])
        mod = [sb(f"mod{l}", [P, MODC, 2]) for l in range(DEPTH)]
        modA = sb("modA", [P, 2, KC, 2])
        gb2 = sb("gb2", [P, KC, 2])
        R = sb("R", [P, NTOK])
        epsc = sb("epsc", [P, 1])
        sg = sb("sg", [P, 2, NTOK])
        lam = sb("lam", [P, 4, HD])
        lamt = sb("lamt", [P, 8])
        sm = sb("sm", [P, 2, 2, 4])
        subg = sb("subg", [P, 1])
        score = sb("score", [P, NT, E])
        sel = sb("sel", [P, NT, E])
        msel = sb("msel", [P, NT, E])
        tA = sb("tA", [P, NT, E])
        tB = sb("tB", [P, NT, E])
        oh = sb("oh", [P, 2, NT, E])
        pair = sb("pair", [P, 2, NT, E])
        g4 = sb("g4", [P, 10, NT * GROUPS])
        t1 = sb("t1", [P, 12, NT])
        wk = sb("wk", [P, 2, NT])
        slot = sb("slot", [P, 2 * NT], I32)
        ints = sb("ints", [P, 2, 24])
        offI = sb("offI", [P, 24], I32)
        cum = sb("cum", [P, 2, 8 + E])
        ov = sb("ov", [P, 4, OVER * E])
        ovf = sb("ovf", [P, 2, 8])
        ovI = sb("ovI", [P, 3, 8], I32)
        novI = sb("novI", [P, 1], I32)
        zrow = sb("zrow", [P, D])
        ps = ctx.enter_context(nc.psum_tensor("ps", [P, 8, 512], F32))

        tap_rows = H[:, 0:2, :].rearrange("p j t -> p (j t)")
        U = UB[:, :].rearrange("p (j s w) -> p j s w", j=KC, s=2)
        Vt = V[:, :].rearrange("p (j t) -> p j t", j=KC)
        Wt = W[:, :].rearrange("p (t d) -> p t d", t=NT)
        Ht = H[:, :, :].rearrange("p j t -> p (j t)").rearrange("p (t d) -> p t d", t=NT)
        hrow = UB[:, 0:2 * D].rearrange("p (b d) -> p b d", b=2)
        hT = UB[:, 2 * D:4 * D].rearrange("p (b d) -> p b d", b=2)
        yrow = V[:, 0:2 * D].rearrange("p (b d) -> p b d", b=2)
        eg = V[:, 2 * D:2 * D + FE]
        ea = V[:, 2 * D + FE:2 * D + 2 * FE]
        eaT = V[:, 3 * D:3 * D + FE]
        Q = UB[:, 0:HEADS * SEQ].rearrange("p (h t) -> p h t", h=HEADS)
        pr = UB[:, HEADS * SEQ:HEADS * SEQ + 4 * NTOK].rearrange("p (b c t) -> p b c t", b=2, c=2)
        K = Vt
        O = Q
        OF = UB[:, 0:HEADS * SEQ]
        aT = [x.rearrange("p (k t) -> p k t", k=NT) for x in (sg[:, :, :].rearrange("p a b -> p (a b)"), zrow[:, :])]
        adaR = zrow[:, :].rearrange("p (b n) -> p b n", b=2)
        HR = H[:, 0:4, :].rearrange("p j t -> p (j t)")

        Hs = nc.dram_tensor("token_rows", (2 * NTOK + P, D), F32, kind="Internal").ap()
        Ys = nc.dram_tensor("expert_rows", (2 * NTOK + P, D), F32, kind="Internal").ap()

        def C(at, n=P):
            return cst[:, at:at + n]

        ident, mean, head_mean, ones, before, rot = (C(k) for k in (C_ID, C_MEAN, C_HEAD, C_ONE, C_BEFORE, C_ROT))

        w_in = [sem(f"w_in{s}") for s in range(RING + 1)]
        cst_in, vec_in, x_in, rw_in, lam_in = (sem(n) for n in ("cst_in", "vec_in", "x_in", "rw_in", "lam_in"))
        vecA_in = sem("vecA_in")
        vec_t, vec_c = sem("vec_t"), sem("vec_c")
        x_t, x_c = sem("x_t"), sem("x_c")
        c_silu = sem("c_silu")
        ada_p, ada_r, ada_t, ada_c = sem("ada_p"), sem("ada_r"), sem("ada_t"), sem("ada_c")
        modA_r, modB_r = sem("modA_r"), sem("modB_r")
        pad_z = sem("pad_z")
        dve = sem("dve_chain")
        pw1_p, pw1_s, pw1_g = sem("pw1_p"), sem("pw1_s"), sem("pw1_g")
        conv_a = sem("conv_a")
        mean_p, cen, cen_sq, var_p, lnz, ln_s = (sem(n) for n in ("mean_p", "cen", "cen_sq", "var_p", "lnz", "ln_s"))
        pw2_p, pw2_t, pw2_x = sem("pw2_p"), sem("pw2_t"), sem("pw2_x")
        prod_p, prod_c, rot_p, rot_r = sem("prod_p"), sem("prod_c"), sem("rot_p"), sem("rot_r")
        s_p, s_m, s_e, s_a, a_t, a_c, o_p, o_c = (sem(n) for n in (
            "s_p", "s_m", "s_e", "s_a", "a_t", "a_c", "o_p", "o_c"))
        o_sq, o_ms, o_n = sem("o_sq"), sem("o_ms"), sem("o_n")
        wo_p, wo_x = sem("wo_p"), sem("wo_x")
        fin_t, fin_c, out_w = sem("fin_t"), sem("fin_c"), sem("out_w")
        hs_pad = sem("hs_pad")
        lam_s, lam_e = sem("lam_s"), sem("lam_e")
        eps_r, root = sem("eps_r"), sem("root")
        ROOTS = {"mix0": 1, "ln": 2, "ffn0": 3, "mix1": 4, "heads": 5, "ffn1": 9, "fin": 10}

        n_sq, n_ms, n_hr, n_h = sem("n_sq"), sem("n_ms"), sem("n_hr"), sem("n_h")
        NORM = {k: i for i, k in enumerate(("mix0", "ffn0", "mix1", "ffn1", "fin"))}

        def chunk_done(eng, s, name, k):
            eng.wait_ge(s, NORM[name] * KC + k + 1)

        class Moe:
            def __init__(self, l):
                def s(k):
                    return sem(f"m{l}_{k}")
                self.route_p, self.route_c, self.route_t, self.score_r, self.pair_r, self.rank_p = (
                    s(k) for k in ("route_p", "route_c", "route_t", "score_r", "pair_r", "rank_p"))
                self.slot_r, self.over_r = s("slot_r"), s("over_r")
                self.rows_t, self.rows_c, self.scat = s("rows_t"), s("rows_c"), s("scat")
                self.h_in = [s("h_in0"), s("h_in1")]
                self.h_t, self.h_c = s("h_t"), s("h_c")
                self.gate_p, self.gate_s, self.up_p, self.act_r = (s(k) for k in ("gate_p", "gate_s", "up_p", "act_r"))
                self.act_t, self.act_c = s("act_t"), s("act_c")
                self.down_p, self.y0_c, self.y1_c = s("down_p"), s("y0_c"), s("y1_c")
                self.y_out, self.y_free = s("y_out"), s("y_free")
                self.end = s("end")
                self.o_step, self.o_in, self.o_w, self.o_out = (s(k) for k in ("o_step", "o_in", "o_w", "o_out"))
                self.y_in = [s("y_in0"), s("y_in1")][0:l and 1 or 2]
                self.w1_r = s("w1_r")
                self.mix_r, self.mix_t, self.mix_x = (s(k) for k in ("mix_r", "mix_t", "mix_x"))

        moes = [Moe(l) for l in range(DEPTH)]
        VECS = 9
        TL = [NT, SEQ // P]
        T0 = [0, CTX // P]

        def piece_src(kind, l, n):
            cols = slice(n * FE, (n + 1) * FE)
            w = {"ada": a["ada_w"][l], "pw1": a["conv_pw1_w"][0], "pw2": a["conv_pw2_w"][0],
                 "qkv": a["diff_w_qkv"][0], "wo": a["diff_w_o"][0]}[kind]
            return w[:, cols].rearrange("(j p) n -> p j n", p=P)

        def slot_tile(slot):
            return W[:, :] if slot == RING else ring[:, slot, :]

        def piece(key):
            return slot_tile(PLACE[key][0]).rearrange("p (j n) -> p j n", j=KC)

        def landed(eng, key):
            eng.wait_ge(w_in[PLACE[key][0]], 16 * (PLACE[key][1] + 1))

        DOWN_N = [2, 1]

        last_read = {}
        for n in range(ADA_PC):
            last_read[("ada", 0, n)] = (ada_p, n + 1)
            last_read[("ada", 1, n)] = (ada_p, ADA_PC + n + 1)
        last_read[("pw1", 0, 0)] = last_read[("pw1", 0, 2)] = (pw1_p, KC)
        last_read[("pw1", 0, 1)] = last_read[("pw1", 0, 3)] = (pw1_p, 2 * KC)
        last_read[("pw2", 0, 0)], last_read[("pw2", 0, 1)] = (pw2_p, KC // 2), (pw2_p, KC)
        for n in range(2):
            for q in range(3):
                last_read[("qkv", 0, 2 * q + n)] = (prod_p, 12 * n + 4 * (q + 1))
            last_read[("wo", 0, n)] = (wo_p, KC // 2 * (n + 1))
        for l in range(DEPTH):
            for b in range(2):
                last_read[("moe", l, b, 0)] = (moes[l].gate_p, E - 1 + b)
                last_read[("moe", l, b, 1)] = (moes[l].gate_p if l else moes[l].up_p, E - 1 + b)
                last_read[("moe", l, b, 2)] = (moes[l].down_p, DOWN_N[l] * (E - 1 + b))

        def expert_landed(eng, l, b, k, i):
            slot, n, _ = PLACE[("moe", l, b, k)]
            eng.wait_ge(w_in[slot], i * 16 + 16 * (n + 1))

        def halves(l):
            return TM[l] * 2 == P

        def gate_out(l, b):
            return ps[0:TM[l], b if halves(l) else 0, :]

        def up_out(l, b):
            return ps[TM[l]:P, b, :] if halves(l) else ps[:, 1, :]

        def down_out(l, h):
            return ps[h * TM[l]:(h + 1) * TM[l], 3, :] if halves(l) else ps[:, 3 + h, :]

        def y_part(l, b, h):
            return yrow[h * TM[l]:(h + 1) * TM[l], b, 0:512] if halves(l) else yrow[:, b, h * 512:(h + 1) * 512]


        def write_rows(pool, l, b, r, s):
            if halves(l):
                for h in range(2):
                    pool.dma_start(Ys[bass.ds(r, TM[l]), h * 512:(h + 1) * 512], y_part(l, b, h)).then_inc(s, 16)
            else:
                pool.dma_start(Ys[bass.ds(r, TM[l]), :], yrow[:, b, :]).then_inc(s, 16)

        WRITES = [16, 32]

        def step_done(eng, m, j, step):
            eng.wait_ge(m.o_step, j * len(STEPS) + (STEPS.index(step) + 1))

        def rotated(r):
            is_k, g = divmod(r % 8, 4)
            h = 4 * (r // 8) + g
            return K[:, h, CTX:NTOK] if is_k else Q[:, h, :]

        def gate_tile(s):
            return ring[:, s, :].rearrange("p (j n) -> p j n", j=KC)

        def down_tile(s):
            return ring[:, s, :].rearrange("p (j n) -> p j n", j=FC)

        block = ctx.enter_context(nc.Block())

        @block.sync
        def _(sp):
            def free(key):
                if PLACE[key][2] is not None:
                    sp.wait_ge(*last_read[PLACE[key][2]])

            def load(key):
                free(key)
                if PLACE[key][0] == RING and PLACE[key][1] == 0:
                    sp.wait_ge(x_t, KC)
                kind, l, m = key
                sp.dma_start(piece(key), piece_src(kind, l, m)).then_inc(w_in[PLACE[key][0]], 16)

            def expert_srcs(l, e):
                return [a["moe_w_gate"][l].rearrange("e (p j) n -> e p (j n)", j=KC)[e],
                        a["moe_w_up"][l].rearrange("e (p j) n -> e p (j n)", j=KC)[e],
                        a["moe_w_down"][l].rearrange("e (p j) n -> e p (j n)", j=FC)[e]]

            def experts(l):
                m = moes[l]
                for b in range(2):
                    for k, src in enumerate(expert_srcs(l, b)):
                        free(("moe", l, b, k))
                        slot = SETS[l][b][k]
                        sp.dma_start(ring[:, slot, :], src).then_inc(w_in[slot], 16)
                M = TM[l]
                sp.wait_ge(m.slot_r, 1)
                for b in range(2):
                    r = sp.value_load(offI[0:1, b:b + 1], min_val=0, max_val=2 * NTOK)
                    sp.wait_ge(m.scat, 32 * TL[l])
                    sp.wait_ge(hs_pad, 32)
                    sp.dma_start(hrow[0:M, b, :], Hs[bass.ds(r, M), :]).then_inc(m.h_in[b], 16)
                r = sp.value_load(offI[0:1, 2:3], min_val=0, max_val=2 * NTOK)
                sp.wait_ge(m.h_t, 2)
                sp.dma_start(hrow[0:M, 0, :], Hs[bass.ds(r, M), :]).then_inc(m.h_in[0], 16)
                with sp.Fori(0, E // 2 - 1) as i:
                    for b in range(2):
                        for k, src in enumerate(expert_srcs(l, i * 2 + (2 + b))):
                            if k == 0:
                                sp.wait_ge(m.gate_p, i * 2 + (b + 1))
                            elif k == 1:
                                sp.wait_ge(m.gate_p if halves(l) else m.up_p, i * 2 + (b + 1))
                            else:
                                r = sp.value_load(offI[0:1, bass.ds(i * 2 + (b + 3), 1)], min_val=0, max_val=2 * NTOK)
                                sp.wait_ge(m.scat, 32 * TL[l])
                                sp.wait_ge(m.h_t, i * 4 + (2 * b + 4))
                                sp.dma_start(hrow[0:M, 1 - b, :], Hs[bass.ds(r, M), :]).then_inc(m.h_in[1 - b], 16)
                                sp.wait_ge(m.down_p, i * 2 * DOWN_N[l] + DOWN_N[l] * (b + 1))
                            slot = SETS[l][b][k]
                            sp.dma_start(ring[:, slot, :], src).then_inc(w_in[slot], 16)
                sp.wait_ge(m.h_in[0], 16 * (E // 2 + 1))
                sp.wait_ge(m.over_r, 1)
                n_over = sp.value_load(novI[0:1, 0:1], min_val=0, max_val=OVER)
                with sp.If(n_over > 0):
                    with sp.Fori(0, n_over) as j:
                        e = sp.value_load(ovI[0:1, 0, bass.ds(j, 1)], min_val=0, max_val=E - 1)
                        step_done(sp, m, j, "free")
                        for k, src in enumerate(expert_srcs(l, e)):
                            sp.dma_start(ring[:, SETS[l][0][k], :], src).then_inc(m.o_w, 16)
                    sp.wait_ge(m.end, 1)
                with sp.Else():
                    sp.nop()

            sp.dma_start(Wt[:, 0:2, :], a["ctx"][0].rearrange("(t p) d -> p t d", p=P)).then_inc(x_in, 16)
            sp.dma_start(Wt[:, 2:4, :], a["x"][0].rearrange("(t p) d -> p t d", p=P)).then_inc(x_in, 16)
            sp.wait_ge(cst_in, 16)
            sp.wait_ge(vecA_in, 64)
            for key, _ in SEQ_A:
                load(key)
            experts(0)
            for n, (key, _) in enumerate(SEQ_B):
                if n == 2:
                    for s in moes[0].y_in:
                        sp.wait_ge(s, 64)
                load(key)
            experts(1)
            sp.wait_ge(fin_c, 2 * KC // 4)
            for t in range(2):
                sp.dma_start(out[0, t * P:(t + 1) * P, :], Wt[:, t, :]).then_inc(out_w, 16)
            sp.wait_ge(out_w, 32)

        @block.gpsimd
        def _(pool):
            pool.memset(UB[:, :], 0.0).then_inc(pad_z, 1)
            pool.wait_ge(ada_t, DEPTH * ADA_PC)
            pool.memset(zrow[:, :], 0.0).then_inc(pad_z, 1)
            pool.wait_ge(pad_z, 2)
            for rows in (Hs, Ys):
                pool.dma_start(rows[2 * NTOK:2 * NTOK + P, :], zrow[:, :]).then_inc(hs_pad, 16)

            def experts(l):
                m = moes[l]
                T, M = TL[l], TM[l]
                pool.wait_ge(m.slot_r, 1)
                for t in range(T):
                    pool.wait_ge(m.rows_c, 2 * (t + 1))
                    for k in range(2):
                        pool.indirect_dma_start(
                            Hs[:, :], bass.IndirectOffsetOnAxis(ap=slot[:, k * NT + t:k * NT + t + 1].bitcast(U32), axis=0),
                            Wt[:, t, :], None).then_inc(m.scat, 16)
                if l == 0:
                    pool.wait_ge(hs_pad, 32)
                for b in range(2):
                    pool.nop().then_inc(m.y_free, 1)
                def write(b, i):
                    r = pool.value_load(offI[0:1, bass.ds(i * 2 + b, 1)], min_val=0, max_val=2 * NTOK)
                    pool.wait_ge(m.y0_c, i * 2 + (b + 2))
                    if not halves(l):
                        pool.wait_ge(m.y1_c, i * 2 + (b + 2))
                    write_rows(pool, l, b, r, m.y_out)
                    pool.wait_ge(m.y_out, i * 2 * WRITES[l] + WRITES[l] * (b + 1))
                    pool.nop().then_inc(m.y_free, 1)

                with pool.Fori(0, E // 2 - 1) as i:
                    for b in range(2):
                        write(b, i)
                for b in range(2):
                    r = pool.value_load(offI[0:1, E - 2 + b:E - 1 + b], min_val=0, max_val=2 * NTOK)
                    pool.wait_ge(m.y0_c, E + b)
                    if not halves(l):
                        pool.wait_ge(m.y1_c, E + b)
                    write_rows(pool, l, b, r, m.y_out)
                    pool.wait_ge(m.y_out, WRITES[l] * (E - 1 + b))
                    pool.nop().then_inc(m.y_free, 1)
                pool.wait_ge(m.over_r, 1)
                n_over = pool.value_load(novI[0:1, 0:1], min_val=0, max_val=OVER)
                with pool.If(n_over > 0):
                    with pool.Fori(0, n_over) as j:
                        r = pool.value_load(ovI[0:1, 1, bass.ds(j, 1)], min_val=0, max_val=2 * NTOK)
                        step_done(pool, m, j, "free")
                        pool.wait_ge(m.h_in[0], 16 * (E // 2 + 1))
                        pool.wait_ge(m.scat, 32 * T)
                        pool.dma_start(hrow[0:M, 0, :], Hs[bass.ds(r, M), :]).then_inc(m.o_in, 16)
                        step_done(pool, m, j, "out")
                        r = pool.value_load(ovI[0:1, 2, bass.ds(j, 1)], min_val=0, max_val=2 * NTOK)
                        write_rows(pool, l, 0, r, m.o_out)
                        pool.wait_ge(m.o_out, j * WRITES[l] + WRITES[l])
                with pool.Else():
                    pool.nop()
                pool.wait_ge(m.end, 1)
                for t in range(T):
                    for k, dst in enumerate((Wt, Ht)):
                        pool.indirect_dma_start(
                            dst[:, t, :], None, Ys[:, :],
                            bass.IndirectOffsetOnAxis(ap=slot[:, k * NT + t:k * NT + t + 1].bitcast(U32), axis=0)
                        ).then_inc(m.y_in[t // 2], 16)

            for l in range(DEPTH):
                experts(l)

        @block.tensor
        def _(pe):
            def turn(out, in_, n=P):
                return pe.transpose(out, in_, ident[0:n, 0:n])

            def ada_rows(g):
                key = ("ada", g // ADA_PC, g % ADA_PC)
                landed(pe, key)
                if g >= 2:
                    pe.wait_ge(ada_r, g - 1)
                for r in range(KC // QUADS):
                    for q in range(QUADS):
                        k = r * QUADS + q
                        mm = pe.matmul(ps[q * QW:(q + 1) * QW, g % 2, :], sc[:, k, :], piece(key)[:, k, :],
                                       start=(r == 0), stop=(r == KC // QUADS - 1))
                mm.then_inc(ada_p, 1)

            def ada_turn(g):
                pe.wait_ge(ada_r, g + 1)
                if g >= 1:
                    pe.wait_ge(ada_c, g)
                for q in range(FC):
                    mm = pe.matmul(ps[:, 7, 2 * q:2 * q + 2], adaR[:, g % 2, q * P:(q + 1) * P], C(C_SEL, 2),
                                   start=True, stop=True)
                mm.then_inc(ada_t, 1)

            def norm(name, sq, c0, bank):
                for k in range(KC):
                    chunk_done(pe, n_sq, name, k)
                    mm = pe.matmul(ps[:, bank, c0:NTOK], mean, sq[:, k, c0:NTOK], start=(k == 0), stop=(k == KC - 1))
                mm.then_inc(n_ms, 1)

            def experts(l):
                m = moes[l]
                T, t0, M = TL[l], T0[l], TM[l]
                c0 = t0 * P
                pe.wait_ge(rw_in, 32)
                for k in range(KC):
                    chunk_done(pe, n_h, f"ffn{l}", k)
                    q, r = k % QUADS, k // QUADS
                    mm = pe.matmul(ps[q * QW:(q + 1) * QW, 3, c0:NTOK], rw[:, k, :], H[:, k, c0:NTOK],
                                   start=(r == 0), stop=(r == KC // QUADS - 1))
                mm.then_inc(m.route_p, 1)
                for t in range(T):
                    for h in range(2):
                        g = 2 * t + h
                        if g >= 4:
                            pe.wait_ge(m.rows_c, g - 3)
                        for k in range(4):
                            mm = turn(ps[:, 4 + g % 4, k * P:(k + 1) * P],
                                      H[:, 4 * h + k, (t0 + t) * P:(t0 + t + 1) * P])
                        mm.then_inc(m.rows_t, 1)
                    if t == 0:
                        pe.wait_ge(m.route_c, 1)
                        for u in range(T):
                            mm = pe.matmul(ps[:, 2, u * E:(u + 1) * E], R[:, c0 + u * P:c0 + (u + 1) * P], C(C_SELE, E),
                                           start=True, stop=True)
                        mm.then_inc(m.route_t, 1)
                pe.wait_ge(m.pair_r, 1)
                pe.matmul(ps[:, 2, 2 * T * E:3 * T * E], before, pair[:, 0, 0:T, :], start=True, stop=True)
                for q in range(2):
                    mm = pe.matmul(ps[:, 2, q * T * E:(q + 1) * T * E], ones, pair[:, q, 0:T, :], start=True, stop=True)
                mm.then_inc(m.rank_p, 1)

                def rows_turned(b, s):
                    hv = hrow[:, b, :].rearrange("p (n j) -> p j n", j=KC)
                    for k in range(KC):
                        mm = turn(ps[:, 5 + k // 4, (k % 4) * P:(k % 4 + 1) * P], hv[:, k, :])
                        if s is m.h_t and k == 3:
                            mm.then_inc(s, 1)
                    mm.then_inc(s, 1)

                def product_in(b, dst, w, s):
                    for k in range(KC):
                        mm = pe.matmul(dst, hT[:, b, k * P:k * P + M], w[:, k, :],
                                       start=(k == 0), stop=(k == KC - 1))
                    mm.then_inc(s, 1)

                def act_turned(s):
                    av = ea.rearrange("p (n j) -> p j n", j=FC)
                    for k in range(FC):
                        mm = turn(ps[:, 2, k * P:(k + 1) * P], av[:, k, :])
                    mm.then_inc(s, 1)

                def product_down(w, s):
                    hk = [(h, k) for k in range(FC) for h in range(2)] if halves(l) else [(h, k) for h in range(2) for k in range(FC)]
                    for h, k in hk:
                        mm = pe.matmul(down_out(l, h), eaT[:, k * P:k * P + M], w[:, k, h * 512:(h + 1) * 512],
                                       start=(k == 0), stop=(k == FC - 1))
                        if k == FC - 1 and (h or (s is m.down_p and DOWN_N[l] == 2)):
                            mm.then_inc(s, 1)

                tiles = [[gate_tile(SETS[l][b][0]), gate_tile(SETS[l][b][1]), down_tile(SETS[l][b][2])] for b in range(2)]

                def gate(b, i, first=False):
                    if not first:
                        pe.wait_ge(m.gate_s, i * 2 + b)
                    pe.wait_ge(m.h_c, i * 2 + (b + 1))
                    expert_landed(pe, l, b, 0, i)
                    product_in(b, gate_out(l, b), tiles[b][0], m.gate_p)

                def gate_up(b, i):
                    pe.wait_ge(m.h_c, i * 2 + (b + 1))
                    expert_landed(pe, l, b, 0, i)
                    expert_landed(pe, l, b, 1, i)
                    for k in range(KC):
                        for dst, w in ((gate_out(l, b), tiles[b][0]), (up_out(l, b), tiles[b][1])):
                            mm = pe.matmul(dst, hT[:, b, k * P:k * P + M], w[:, k, :], start=(k == 0), stop=(k == KC - 1))
                    mm.then_inc(m.gate_p, 1)

                def rows(b, i):
                    pe.wait_ge(m.h_in[b], i * 16 + 16)
                    rows_turned(b, m.h_t)

                def turned(b, i):
                    pe.wait_ge(m.act_r, i * 2 + (b + 1))
                    act_turned(m.act_t)

                def up(b, i):
                    expert_landed(pe, l, b, 1, i)
                    product_in(b, up_out(l, b), tiles[b][1], m.up_p)

                def down(b, i):
                    expert_landed(pe, l, b, 2, i)
                    pe.wait_ge(m.act_c, i * 2 + (b + 1))
                    pe.wait_ge(m.y0_c, i * 2 + (b + 1))
                    if not halves(l):
                        pe.wait_ge(m.y1_c, i * 2 + (b + 1))
                    product_down(tiles[b][2], m.down_p)

                pe.wait_ge(m.over_r, 1)
                pe.wait_ge(m.rows_c, 2 * T)
                rows(0, 0)
                last = E // 2 - 1
                if halves(l):
                    gate_up(0, 0)
                    rows(1, 0)
                    with pe.Fori(0, E // 2 - 1) as i:
                        gate_up(1, i)
                        turned(0, i)
                        rows(0, i + 1)
                        down(0, i)
                        gate_up(0, i + 1)
                        turned(1, i)
                        rows(1, i + 1)
                        down(1, i)
                    gate_up(1, last)
                    turned(0, last)
                    down(0, last)
                    turned(1, last)
                    down(1, last)
                else:
                    gate(0, 0, first=True)
                    rows(1, 0)
                    up(0, 0)
                    with pe.Fori(0, E // 2 - 1) as i:
                        gate(1, i)
                        rows(0, i + 1)
                        turned(0, i)
                        up(1, i)
                        down(0, i)
                        gate(0, i + 1)
                        rows(1, i + 1)
                        turned(1, i)
                        up(0, i + 1)
                        down(1, i)
                    gate(1, last)
                    turned(0, last)
                    up(1, last)
                    down(0, last)
                    turned(1, last)
                    down(1, last)
                pe.wait_ge(m.over_r, 1)
                n_over = pe.value_load(novI[0:1, 0:1], min_val=0, max_val=OVER)
                pe.wait_ge(m.y0_c, E + 1)
                if not halves(l):
                    pe.wait_ge(m.y1_c, E + 1)
                pe.wait_ge(m.y_free, E + 2)
                pe.nop().then_inc(m.o_step, 1)
                with pe.If(n_over > 0):
                    with pe.Fori(0, n_over) as j:
                        pe.wait_ge(m.o_in, j * 16 + 16)
                        pe.wait_ge(m.o_w, j * 48 + 48)
                        rows_turned(0, m.o_step)
                        step_done(pe, m, j, "rows")
                        product_in(0, gate_out(l, 0), tiles[0][0], m.o_step)
                        step_done(pe, m, j, "silu")
                        product_in(0, up_out(l, 0), tiles[0][1], m.o_step)
                        step_done(pe, m, j, "act")
                        act_turned(m.o_step)
                        step_done(pe, m, j, "act_rows")
                        product_down(tiles[0][2], m.o_step)
                        step_done(pe, m, j, "out")
                        pe.wait_ge(m.o_out, j * WRITES[l] + WRITES[l])
                        pe.nop().then_inc(m.o_step, 1)
                with pe.Else():
                    pe.nop()
                pe.nop().then_inc(m.end, 1)
                for g in range(KC * T // 2):
                    st, k = g // KC + t0 // 2, g % KC
                    if k == 0:
                        pe.wait_ge(m.mix_r, 2 * (g // KC) + 2)
                    if g >= 4:
                        pe.wait_ge(m.mix_x, g - 3)
                    for t in range(2):
                        mm = turn(ps[:, 4 + g % 4, t * P:(t + 1) * P], Wt[:, 2 * st - t0 + t, k * P:(k + 1) * P])
                    mm.then_inc(m.mix_t, 1)

            pe.wait_ge(cst_in, 16)
            pe.wait_ge(vecA_in, 64)
            turn(ps[:, 0, 0:P], rowsA[:, :]).then_inc(vec_t, 1)
            pe.wait_ge(x_in, 32)
            for k in range(KC):
                if k >= 4:
                    pe.wait_ge(x_c, k - 3)
                for t in range(NT):
                    mm = turn(ps[:, 4 + k % 4, t * P:(t + 1) * P], Wt[:, t, k * P:(k + 1) * P])
                mm.then_inc(x_t, 1)
            pe.wait_ge(vec_in, 16 * VECS)
            turn(ps[:, 2, 0:B_ROWS], rowsB[0:B_ROWS, :], B_ROWS)
            for k in range(KC):
                mm = turn(ps[:, 3, 32 * k:32 * k + TAPS], tap_rows[0:TAPS, k * P:(k + 1) * P], TAPS)
            mm.then_inc(vec_t, 1)
            pe.wait_ge(c_silu, 2)
            pe.wait_ge(x_c, KC)
            for g in range(4):
                ada_rows(g)
                if g:
                    ada_turn(g - 1)
            ada_turn(3)
            pe.wait_ge(vec_c, 2)
            norm("mix0", Vt, 0, 2)
            pe.wait_ge(x_c, KC)
            for j in range(KC):
                if j >= 2:
                    pe.wait_ge(pw1_g, j - 1)
                for h in (1, 0):
                    key = ("pw1", 0, 2 * h + j // 4)
                    landed(pe, key)
                    w = piece(key)
                    for k in range(KC):
                        if j == 0 and h:
                            chunk_done(pe, n_h, "mix0", k)
                        mm = pe.matmul(ps[:, 3 + 2 * (j % 2) + h, :], w[:, k, (j % 4) * P:(j % 4 + 1) * P], H[:, k, :],
                                       start=(k == 0), stop=(k == KC - 1))
                    mm.then_inc(pw1_p, 1)
                for g in FILL[j]:
                    ada_rows(g)
                    if g > 4:
                        ada_turn(g - 1)
            ada_turn(DEPTH * ADA_PC - 1)
            for k in range(KC):
                pe.wait_ge(conv_a, k + 1)
                mm = pe.matmul(ps[:, 2, :], mean, Vt[:, k, :], start=(k == 0), stop=(k == KC - 1))
            mm.then_inc(mean_p, 1)
            for k in range(KC):
                pe.wait_ge(cen_sq, k + 1)
                mm = pe.matmul(ps[:, 3, :], mean, H[:, k, :], start=(k == 0), stop=(k == KC - 1))
            mm.then_inc(var_p, 1)
            pe.wait_ge(pw1_g, KC)
            for j in range(KC):
                key = ("pw2", 0, j // 4)
                landed(pe, key)
                if j >= 4:
                    pe.wait_ge(pw2_t, j - 3)
                for k in range(KC):
                    if j == 0:
                        pe.wait_ge(ln_s, k + 1)
                    mm = pe.matmul(ps[:, 4 + j % 4, :], piece(key)[:, k, (j % 4) * P:(j % 4 + 1) * P], H[:, k, :],
                                   start=(k == 0), stop=(k == KC - 1))
                mm.then_inc(pw2_p, 1)
            norm("ffn0", Vt, 0, 2)
            experts(0)

            norm("mix1", Vt, 0, 2)
            def product(i):
                n, r = divmod(i, 12)
                q, g = divmod(r, 4)
                key = ("qkv", 0, 2 * q + n)
                landed(pe, key)
                bank = (6, 5)[i % 2] if n == 0 else 6
                if i >= 2:
                    pe.wait_ge(prod_c, i - 1 if n == 0 else i)
                for k in range(KC):
                    if i == 0:
                        chunk_done(pe, n_h, "mix1", k)
                    if q == 2:
                        mm = pe.matmul(ps[:, bank, :], H[:, k, g * P:(g + 1) * P], piece(key)[:, k, :],
                                       start=(k == 0), stop=(k == KC - 1))
                    else:
                        c0 = 0 if q else CTX
                        mm = pe.matmul(ps[:, bank, c0:NTOK], piece(key)[:, k, g * P:(g + 1) * P], H[:, k, c0:NTOK],
                                       start=(k == 0), stop=(k == KC - 1))
                mm.then_inc(prod_p, 1)

            def rotate(r):
                i = 12 * (r // 8) + r % 8
                pe.wait_ge(prod_c, i + 1)
                if r >= 1:
                    pe.wait_ge(rot_r, r)
                pe.matmul(ps[:, 7, 0:SEQ], rot, rotated(r), start=True, stop=True).then_inc(rot_p, 1)

            def scores(u):
                h, qt = divmod(u, 2)
                if u % 8 == 0:
                    pe.wait_ge(rot_r, u + 8)
                if u >= 2:
                    pe.wait_ge(s_e, 2 * (u - 1))
                for c in range(2):
                    pe.matmul(ps[:, 2 * (u % 2) + c, :], Q[c * HD:(c + 1) * HD, h, qt * P:(qt + 1) * P],
                              K[c * HD:(c + 1) * HD, h, :], start=True, stop=True).then_inc(s_p, 1)

            def weights(u):
                pe.wait_ge(s_a, u + 1)
                if u >= 1:
                    pe.wait_ge(a_c, u)
                for k in range(NT):
                    mm = turn(ps[:, 4, k * P:(k + 1) * P], pr[:, u % 2, 0, k * P:(k + 1) * P])
                mm.then_inc(a_t, 1)

            def values(h):
                pe.wait_ge(a_c, 2 * (h + 1))
                if h % 4 == 0:
                    pe.wait_ge(prod_c, 12 * (h // 4 + 1))
                if h >= 1:
                    pe.wait_ge(o_c, h)
                for k in range(NT):
                    mm = pe.matmul(ps[:, 5, 0:SEQ], Wt[:, k, h * P:(h + 1) * P], aT[h % 2][:, k, :],
                                   start=(k == 0), stop=(k == NT - 1))
                mm.then_inc(o_p, 1)

            parts = {"product": product, "rotate": rotate, "scores": scores, "weights": weights, "values": values}
            for part, n in PLAN:
                if part in parts:
                    parts[part](n)
            for g in range(HEADS // 2):
                pe.wait_ge(o_sq, g + 1)
                pe.matmul(ps[:, g, :], head_mean, V[:, g * 512:(g + 1) * 512], start=True, stop=True).then_inc(o_ms, 1)
            pe.wait_ge(o_n, HEADS // 2)
            for j in range(KC):
                key = ("wo", 0, j // 4)
                landed(pe, key)
                if j >= 4:
                    pe.wait_ge(wo_x, j - 3)
                for k in range(KC):
                    mm = pe.matmul(ps[:, 4 + j % 4, CTX:NTOK], piece(key)[:, k, (j % 4) * P:(j % 4 + 1) * P], O[:, k, :],
                                   start=(k == 0), stop=(k == KC - 1))
                mm.then_inc(wo_p, 1)
            norm("ffn1", Vt, CTX, 2)
            experts(1)
            norm("fin", Vt, CTX, 2)
            for t in range(2):
                for h in range(2):
                    for k in range(4):
                        chunk_done(pe, n_h, "fin", 4 * h + k)
                        mm = turn(ps[:, 4 + 2 * t + h, k * P:(k + 1) * P],
                                  H[:, 4 * h + k, CTX + t * P:CTX + (t + 1) * P])
                    mm.then_inc(fin_t, 1)

        @block.scalar
        def _(act):
            def rows(dst, src, n):
                act.dma_start(dst, src.rearrange("(r p) -> r p", p=P) if n > 1 else src).then_inc(
                    vecA_in if dst.tensor.name == rowsA.name else vec_in, 16)

            flat = {k: a[k] for k in ("ada_b", "norm_mix_g", "norm_ffn_g", "conv_pw1_b", "conv_dw_b", "conv_ln_g",
                                      "conv_ln_b", "conv_pw2_b", "c")}
            flat = {k: v.rearrange("l d -> (l d)") for k, v in flat.items()}
            for dst, at, n, src in ((rowsA, A_ADA, DEPTH * MODC, flat["ada_b"]), (rowsA, A_C, KC, flat["c"]),
                                    (rowsA, A_CC, KC, a["c_ctx"]), (rowsA, A_PW1, 2 * KC, flat["conv_pw1_b"]),
                                    (rowsB, B_MIX, DEPTH * KC, flat["norm_mix_g"]),
                                    (rowsB, B_FFN, DEPTH * KC, flat["norm_ffn_g"]),
                                    (rowsB, B_FIN, KC, a["final_norm_g"]), (rowsB, B_DWB, KC, flat["conv_dw_b"]),
                                    (rowsB, B_LNG, KC, flat["conv_ln_g"]), (rowsB, B_LNB, KC, flat["conv_ln_b"]),
                                    (rowsB, B_PW2, KC, flat["conv_pw2_b"])):
                rows(dst[at:at + n, :], src, n)
                if at == A_PW1 and dst is rowsA:
                    act.dma_start(cst[:, :], a["consts"]).then_inc(cst_in, 16)
            rows(rowsB[B_SUB:B_SUB + 1, :], a["diff_subln_g"], 1)
            rows(tap_rows[0:TAPS, :], a["conv_dw_w"][0], 1)
            act.wait_ge(eps_r, 1)
            act.dma_start(rw[:, :, 0:E], a["router_w"].rearrange("(j p) e -> p j e", p=P)).then_inc(rw_in, 16)
            act.dma_start(rb[:, :], a["router_b"].partition_broadcast(P)).then_inc(rw_in, 16)
            act.dma_start(lam[:, :, :].rearrange("p a b -> p (a b)"),
                          a["diff_lambda"].rearrange("l a b -> (l a b)").partition_broadcast(P)).then_inc(lam_in, 16)

            act.wait_ge(vec_c, 1)
            act.activation(sc[:, :, 0], colA[:, A_CC:A_CC + KC], ACT.Silu).then_inc(c_silu, 1)
            act.activation(sc[:, :, 1], colA[:, A_C:A_C + KC], ACT.Silu).then_inc(c_silu, 1)

            def ada_rows_copy(g):
                act.wait_ge(ada_p, g + 1)
                if g >= 2:
                    act.wait_ge(ada_t, g - 1)
                act.copy(adaR[:, g % 2, :], ps[:, g % 2, :]).then_inc(ada_r, 1)

            def ada_copy(g):
                l, n = divmod(g, ADA_PC)
                act.wait_ge(ada_t, g + 1)
                act.copy(mod[l][:, 4 * n:4 * n + 4, :].rearrange("p a b -> p (a b)"), ps[:, 7, 0:8]).then_inc(ada_c, 1)

            def squares(c0, ready):
                for k in range(KC):
                    act.wait_ge(*ready(k))
                    act.activation(Vt[:, k, c0:NTOK], X[:, k, c0:NTOK], ACT.Square).then_inc(n_sq, 1)

            def take_root(name, bank, c0):
                if name == "ln":
                    act.wait_ge(var_p, 1)
                else:
                    act.wait_ge(n_ms, NORM[name] + 1)
                act.activation(R[:, c0:NTOK], ps[:, bank, c0:NTOK], ACT.Sqrt, bias=epsc[:, 0:1]).then_inc(root, 1)

            def modulate(name, l, which, c0):
                for k in range(KC):
                    chunk_done(act, n_hr, name, k)
                    for st in range(c0 // CTX, 2):
                        v = H[:, k, st * CTX:(st + 1) * CTX]
                        i = act.activation(v, v, ACT.Identity, bias=mod[l][:, (3 * which) * KC + k, st:st + 1],
                                           scale=modA[:, which, k, st:st + 1])
                    i.then_inc(n_h, 1)

            def experts(l):
                m = moes[l]
                T, M = TL[l], TM[l]
                act.wait_ge(m.route_p, 1)
                act.copy(R[:, T0[l] * P:NTOK], ps[:, 3, T0[l] * P:NTOK]).then_inc(m.route_c, 1)
                for g in range(2 * T):
                    if g == 2:
                        act.wait_ge(m.route_t, 1)
                        act.activation(score[:, 0:T, :].rearrange("p t e -> p (t e)"), ps[:, 2, 0:T * E],
                                       ACT.Sigmoid).then_inc(m.score_r, 1)
                    act.wait_ge(m.rows_t, g + 1)
                    act.copy(Wt[:, g // 2, (g % 2) * 512:(g % 2 + 1) * 512], ps[:, 4 + g % 4, :]).then_inc(m.rows_c, 1)
                def silu(b, i):
                    act.wait_ge(m.gate_p, i * 2 + (b + 1))
                    act.activation(eg[0:M, :], gate_out(l, b), ACT.Silu).then_inc(m.gate_s, 1)

                def out_half(b, i):
                    act.wait_ge(m.down_p, i * 2 * DOWN_N[l] + (DOWN_N[l] * b + 1))
                    act.wait_ge(m.y_free, i * 2 + (b + 1))
                    act.copy(yrow[:, b, 0:512], ps[:, 3, :]).then_inc(m.y0_c, 1)

                act.nop().then_inc(m.y0_c, 1)
                silu(0, 0)
                with act.Fori(0, E // 2 - 1) as i:
                    act.wait_ge(m.act_r, i * 2 + 1)
                    silu(1, i)
                    out_half(0, i)
                    act.wait_ge(m.act_r, i * 2 + 2)
                    silu(0, i + 1)
                    out_half(1, i)
                last = E // 2 - 1
                act.wait_ge(m.act_r, E - 1)
                silu(1, last)
                out_half(0, last)
                out_half(1, last)
                act.wait_ge(m.over_r, 1)
                n_over = act.value_load(novI[0:1, 0:1], min_val=0, max_val=OVER)
                with act.If(n_over > 0):
                    with act.Fori(0, n_over) as j:
                        step_done(act, m, j, "gate")
                        act.activation(eg[0:M, :], gate_out(l, 0), ACT.Silu).then_inc(m.o_step, 1)
                with act.Else():
                    act.nop()
                for t in range(T):
                    act.wait_ge(m.y_in[t // 2], 64)
                    act.mul(Wt[:, t, :], Wt[:, t, :], wk[:, 0, t:t + 1]).then_inc(m.w1_r, 1)

            for k in range(KC):
                act.wait_ge(x_t, k + 1)
                act.copy(X[:, k, :], ps[:, 4 + k % 4, :]).then_inc(x_c, 1)
            squares(0, lambda k: (x_c, k + 1))
            for g in range(4):
                ada_rows_copy(g)
                if g:
                    ada_copy(g - 1)
            ada_copy(3)
            act.wait_ge(eps_r, 1)
            take_root("mix0", 2, 0)
            act.wait_ge(modA_r, 1)
            modulate("mix0", 0, 0, 0)
            for j in range(KC):
                act.wait_ge(pw1_p, 2 * j + 1)
                if j >= 2:
                    act.wait_ge(pw1_g, j - 1)
                act.activation(sg[:, j % 2, :], ps[:, 4 + 2 * (j % 2), :], ACT.Sigmoid,
                               bias=colA[:, A_PW1 + KC + j:A_PW1 + KC + j + 1]).then_inc(pw1_s, 1)
                for g in FILL[j]:
                    ada_rows_copy(g)
                    if g > 4:
                        ada_copy(g - 1)
            ada_copy(DEPTH * ADA_PC - 1)
            for k in range(KC):
                act.wait_ge(cen, k + 1)
                act.activation(H[:, k, :], Vt[:, k, :], ACT.Square).then_inc(cen_sq, 1)
            take_root("ln", 3, 0)
            for k in range(KC):
                act.wait_ge(lnz, k + 1)
                act.activation(H[:, k, :], Vt[:, k, :], ACT.Silu, bias=colB[:, B_LNB + k:B_LNB + k + 1],
                               scale=colB[:, B_LNG + k:B_LNG + k + 1]).then_inc(ln_s, 1)
            act.wait_ge(modA_r, 2)
            for j in range(KC):
                act.wait_ge(pw2_p, j + 1)
                if j >= 2:
                    act.wait_ge(pw2_x, j - 1)
                for st in range(2):
                    cs = slice(st * CTX, (st + 1) * CTX)
                    i = act.activation(sg[:, j % 2, cs], ps[:, 4 + j % 4, cs], ACT.Identity,
                                       bias=gb2[:, j, st:st + 1], scale=mod[0][:, 2 * KC + j, st:st + 1])
                i.then_inc(pw2_t, 1)
            squares(0, lambda k: (pw2_x, k + 1))
            take_root("ffn0", 2, 0)
            modulate("ffn0", 0, 1, 0)
            experts(0)
            squares(0, lambda k: (moes[0].mix_x, KC + k + 1))
            take_root("mix1", 2, 0)
            act.wait_ge(modB_r, 1)
            modulate("mix1", 1, 0, 0)
            act.wait_ge(lam_s, 1)
            for k in range(2):
                act.activation(lamt[:, 2 + k:3 + k], lamt[:, k:k + 1], ACT.Exp).then_inc(lam_e, 1)

            def product_copy(i):
                n, r = divmod(i, 12)
                q, g = divmod(r, 4)
                bank = (6, 5)[i % 2] if n == 0 else 6
                act.wait_ge(prod_p, i + 1)
                if q == 0:
                    c = act.copy(Q[:, 4 * n + g, :], ps[:, bank, CTX:NTOK])
                elif q == 1:
                    c = act.copy(K[:, 4 * n + g, :], ps[:, bank, :])
                else:
                    c = act.copy(Wt[:, g, n * 512:(n + 1) * 512], ps[:, bank, :])
                c.then_inc(prod_c, 1)

            def exponentials(u):
                b = u % 2
                for c in range(2):
                    act.wait_ge(s_m, 2 * u + c + 1)
                    if u >= 2:
                        act.wait_ge(a_t, u - 1)
                    act.activation(pr[:, b, c, :], ps[:, 2 * b + c, :], ACT.Exp, bias=sm[:, b, c, 0:1], scale=SCALE,
                                   accum_out=sm[:, b, c, 1:2]).then_inc(s_e, 1)

            def turned_copy(u):
                h, qt = divmod(u, 2)
                act.wait_ge(a_t, u + 1)
                if u >= 4:
                    act.wait_ge(o_p, h - 1)
                act.copy(aT[h % 2][:, :, qt * P:(qt + 1) * P],
                         ps[:, 4, :].rearrange("p (k t) -> p k t", k=NT)).then_inc(a_c, 1)

            parts = {"product": product_copy, "scores": exponentials, "weights": turned_copy}
            for part, n in PLAN:
                if part in parts:
                    parts[part](n)
            for g in range(HEADS // 2):
                act.wait_ge(o_c, 2 * (g + 1))
                act.activation(V[:, g * 512:(g + 1) * 512], OF[:, g * 512:(g + 1) * 512], ACT.Square).then_inc(o_sq, 1)
            for g in range(HEADS // 2):
                act.wait_ge(o_ms, g + 1)
                act.activation(HR[:, g * 512:(g + 1) * 512], ps[:, g, :], ACT.Sqrt, bias=epsc[:, 0:1]).then_inc(root, 1)
            squares(CTX, lambda k: (wo_x, k + 1))
            take_root("ffn1", 2, CTX)
            modulate("ffn1", 1, 1, CTX)
            experts(1)
            squares(CTX, lambda k: (moes[1].mix_x, k + 1))
            take_root("fin", 2, CTX)
            for g in range(4):
                act.wait_ge(fin_t, g + 1)
                act.copy(Wt[:, g // 2, (g % 2) * 512:(g % 2 + 1) * 512], ps[:, 4 + g, :]).then_inc(fin_c, 1)

        @block.vector
        def _(v):
            count = [0]

            def link(i):
                count[0] += 1
                i.then_inc(dve, 1)
                v.wait_ge(dve, count[0])

            def bc(ap, shape):
                return ap.to_broadcast(shape)

            def rstd(name, c0):
                v.wait_ge(root, ROOTS[name])
                link(v.reciprocal(R[:, c0:NTOK], R[:, c0:NTOK]))

            def norm(name, c0):
                rstd(name, c0)
                for k in range(KC):
                    v.tensor_tensor(H[:, k, c0:NTOK], X[:, k, c0:NTOK], R[:, c0:NTOK], ALU.mult).then_inc(n_hr, 1)

            def bias_mods(l, a0, a1):
                link(v.tensor_tensor(mod[l][:, a0:a1, :], mod[l][:, a0:a1, :],
                                     colA[:, A_ADA + l * MODC + a0:A_ADA + l * MODC + a1].unsqueeze(2).to_broadcast([P, a1 - a0, 2]), ALU.add))

            def gain(l, which):
                at = (B_FFN if which else B_MIX) + l * KC
                return v.scalar_tensor_tensor(modA[:, which, :, :], mod[l][:, (3 * which + 1) * KC:(3 * which + 2) * KC, :],
                                              1.0, colB[:, at:at + KC].unsqueeze(2).to_broadcast([P, KC, 2]), ALU.add, ALU.mult)

            def experts(l):
                m = moes[l]
                T, t0, M = TL[l], T0[l], TM[l]
                G4 = T * GROUPS

                def te(x):
                    return x[:, 0:T, :]

                def per_tok(x):
                    return x.unsqueeze(2).to_broadcast([P, T, E])

                def tok(n):
                    return t1[:, n, 0:T]

                ekey = cst[:, C_EKEY:C_EKEY + T * E].rearrange("p (t e) -> p t e", t=T)
                gkey = cst[:, C_GKEY:C_GKEY + G4].rearrange("p (t g) -> p t g", t=T)
                v.wait_ge(m.score_r, 1)
                if l == 0:
                    v.wait_ge(rw_in, 32)
                link(v.tensor_tensor(te(sel), te(score), rb[:, :].unsqueeze(1).to_broadcast([P, T, E]), ALU.add))
                s4 = te(sel).rearrange("p t (g i) -> p (t g) i", i=GS)

                def q(n):
                    return g4[:, n, 0:G4]

                v.tensor_tensor(q(0), s4[:, :, 0], s4[:, :, 1], ALU.max)
                v.tensor_tensor(q(1), s4[:, :, 0], s4[:, :, 1], ALU.min)
                v.tensor_tensor(q(2), s4[:, :, 2], s4[:, :, 3], ALU.max)
                link(v.tensor_tensor(q(3), s4[:, :, 2], s4[:, :, 3], ALU.min))
                v.tensor_tensor(q(4), q(0), q(2), ALU.max)
                v.tensor_tensor(q(5), q(0), q(2), ALU.min)
                link(v.tensor_tensor(q(6), q(1), q(3), ALU.max))
                link(v.tensor_tensor(q(5), q(5), q(6), ALU.max))
                link(v.tensor_tensor(q(7), q(4), q(5), ALU.add))

                def tg(n):
                    return q(n).rearrange("p (t g) -> p t g", t=T)

                def tok_g(n):
                    return tok(n).unsqueeze(2).to_broadcast([P, T, GROUPS])

                link(v.tensor_reduce(tok(0), tg(7), AX.X, ALU.max))
                link(v.tensor_tensor(tg(8), tg(7), tok_g(0), ALU.is_equal))
                link(v.tensor_tensor(tg(8), tg(8), gkey, ALU.mult))
                link(v.tensor_reduce(tok(1), tg(8), AX.X, ALU.max))
                link(v.tensor_tensor(tg(9), tg(8), tok_g(1), ALU.is_equal))
                m4 = te(msel).rearrange("p t (g i) -> p (t g) i", i=GS)
                in_g = q(9).unsqueeze(2).to_broadcast([P, G4, GS])
                link(v.tensor_tensor(m4, s4, in_g, ALU.mult))
                link(v.tensor_scalar(q(8), q(9), -1.0, BIG, ALU.add, ALU.mult))
                link(v.tensor_tensor(m4, m4, q(8).unsqueeze(2).to_broadcast([P, G4, GS]), ALU.add))
                for k in range(2):
                    one = oh[:, k, 0:T, :]
                    link(v.tensor_reduce(tok(2), te(msel), AX.X, ALU.max))
                    link(v.tensor_tensor(te(tA), te(msel), per_tok(tok(2)), ALU.is_equal))
                    link(v.tensor_tensor(te(tA), te(tA), ekey, ALU.mult))
                    link(v.tensor_reduce(tok(3), te(tA), AX.X, ALU.max))
                    link(v.tensor_tensor(one, te(tA), per_tok(tok(3)), ALU.is_equal))
                    link(v.tensor_tensor(te(tA) if k else te(tB), ekey, per_tok(tok(3)), ALU.is_lt))
                    if k == 0:
                        link(v.scalar_tensor_tensor(te(msel), one, -3.0 * BIG, te(msel), ALU.mult, ALU.add))
                v.tensor_tensor(pair[:, 1, 0:T, :], te(tA), te(tB), ALU.add)
                v.tensor_tensor(pair[:, 0, 0:T, :], oh[:, 0, 0:T, :], oh[:, 1, 0:T, :], ALU.add).then_inc(m.pair_r, 1)
                v.wait_ge(m.rank_p, 1)

                def sums(q):
                    return ps[:, 2, q * T * E:(q + 1) * T * E].rearrange("p (t e) -> p t e", t=T)

                off, num = ints[:, 0, 0:E], ints[:, 1, 0:E]
                v.memset(ints[:, 0, E:24], float(2 * T * P))
                link(v.tensor_reduce(off, sums(1).rearrange("p t e -> p e t"), AX.X, ALU.add))
                v.tensor_copy(tB[:, 0, :], off)
                before_t = off
                for t in range(1, T):
                    link(v.tensor_tensor(tB[:, t, :], before_t, sums(0)[:, t - 1, :], ALU.add))
                    before_t = tB[:, t, :]
                link(v.tensor_tensor(te(tB), te(tB), sums(2), ALU.add))
                mine = ov[:, :, :].rearrange("p a b -> p (a b)")[:, 0:2 * T * E].rearrange("p (k t e) -> p k t e", k=2, t=T)
                for k in range(2):
                    i = v.tensor_tensor(mine[:, k], te(tB), oh[:, k, 0:T, :], ALU.mult)
                link(i)
                for k in range(2):
                    i = v.tensor_reduce(tok(8 + k), mine[:, k], AX.X, ALU.add)
                link(i)
                v.tensor_copy(slot[:, 0:T], tok(8))
                v.tensor_copy(slot[:, NT:NT + T], tok(9))
                v.tensor_copy(offI[:, :], ints[:, 0, :]).then_inc(m.slot_r, 1)
                for k in range(2):
                    link(v.tensor_tensor(te(sel), te(score), oh[:, k, 0:T, :], ALU.mult))
                    link(v.tensor_reduce(tok(4 + k), te(sel), AX.X, ALU.add))
                link(v.tensor_tensor(tok(6), tok(4), tok(5), ALU.add))
                link(v.reciprocal(tok(7), tok(6)))
                for k in range(2):
                    link(v.tensor_tensor(wk[:, k, 0:T], tok(4 + k), tok(7), ALU.mult))
                link(v.tensor_reduce(num, sums(0).rearrange("p t e -> p e t"), AX.X, ALU.add))
                link(v.memset(cum[:, :, :], 0.0))
                link(v.tensor_scalar(tA[:, 0, :], num, float(M), None, ALU.is_gt))
                for k in range(2, T * P // M):
                    link(v.scalar_tensor_tensor(tA[:, 0, :], num, float(k * M), tA[:, 0, :], ALU.is_gt, ALU.add))
                link(v.tensor_copy(cum[:, 0, 8:8 + E], tA[:, 0, :]))
                src = 0
                for step in (1, 2, 4, 8):
                    link(v.tensor_tensor(cum[:, 1 - src, 8:8 + E], cum[:, src, 8:8 + E],
                                         cum[:, src, 8 - step:8 + E - step], ALU.add))
                    src = 1 - src
                up_to = cum[:, src, 8:8 + E]
                link(v.tensor_copy(novI[:, :], cum[:, src, 8 + E - 1:8 + E]))

                def oe(n):
                    return ov[:, n, :].rearrange("p (i e) -> p i e", e=E)

                def over_e(x):
                    return x.unsqueeze(1).to_broadcast([P, OVER, E])

                passes = cst[:, C_PASS:C_PASS + OVER * E].rearrange("p (i e) -> p i e", e=E)
                expert = cst[:, C_EXP:C_EXP + OVER * E].rearrange("p (i e) -> p i e", e=E)
                link(v.tensor_tensor(oe(0), over_e(up_to), passes, ALU.is_le))
                link(v.tensor_reduce(ovf[:, 0, 0:OVER], oe(0), AX.X, ALU.add))
                link(v.tensor_tensor(oe(1), expert, ovf[:, 0, 0:OVER].unsqueeze(2).to_broadcast([P, OVER, E]), ALU.is_equal))
                link(v.tensor_tensor(tB[:, 0, :], up_to, tA[:, 0, :], ALU.subtract))
                link(v.tensor_tensor(oe(2), passes, over_e(tB[:, 0, :]), ALU.subtract))
                link(v.tensor_scalar(oe(2), oe(2), 1.0, float(M), ALU.add, ALU.mult))
                link(v.tensor_tensor(oe(2), oe(2), over_e(off), ALU.add))
                link(v.tensor_tensor(tB[:, 1, :], off, num, ALU.add))
                link(v.tensor_scalar(tB[:, 1, :], tB[:, 1, :], -float(M), None, ALU.add))
                link(v.tensor_tensor(oe(2), oe(2), over_e(tB[:, 1, :]), ALU.min))
                link(v.tensor_tensor(oe(2), oe(2), oe(1), ALU.mult))
                link(v.tensor_reduce(ovf[:, 1, 0:OVER], oe(2), AX.X, ALU.add))
                for k in range(3):
                    link(v.tensor_copy(ovI[:, k, 0:OVER], ovf[:, min(k, 1), 0:OVER]))
                v.nop().then_inc(m.over_r, 1)

                def cols(ap, n):
                    return ap.rearrange("p (k t) -> p k t", k=n)[:, :, 0:M]

                def rows_copy(b, h):
                    return v.tensor_copy(cols(hT[:, b, h * 512:(h + 1) * 512], 4), cols(ps[:, 5 + h, :], 4))

                def rows(b, i):
                    for h in range(2):
                        v.wait_ge(m.h_t, i * 4 + (2 * b + h + 1))
                        c = rows_copy(b, h)
                    c.then_inc(m.h_c, 1)

                def turned(b, i):
                    v.wait_ge(m.act_t, i * 2 + (b + 1))
                    v.tensor_copy(cols(eaT, FC), cols(ps[:, 2, :], FC)).then_inc(m.act_c, 1)

                def gated(b, i):
                    v.wait_ge(m.gate_s, i * 2 + (b + 1))
                    if not halves(l):
                        v.wait_ge(m.up_p, i * 2 + (b + 1))
                    v.tensor_tensor(ea[0:M, :], eg[0:M, :], up_out(l, b), ALU.mult).then_inc(m.act_r, 1)

                def out_half(b, i):
                    if halves(l):
                        return
                    v.wait_ge(m.down_p, i * 4 + (2 * b + 2))
                    v.wait_ge(m.y_free, i * 2 + (b + 1))
                    v.tensor_copy(y_part(l, b, 1), down_out(l, 1)).then_inc(m.y1_c, 1)

                if not halves(l):
                    v.nop().then_inc(m.y1_c, 1)
                rows(0, 0)
                rows(1, 0)
                gated(0, 0)
                with v.Fori(0, E // 2 - 1) as i:
                    for b in range(2):
                        if halves(l):
                            turned(b, i)
                            rows(b, i + 1)
                        else:
                            rows(b, i + 1)
                            turned(b, i)
                        gated(1 - b, i + b)
                        out_half(b, i)
                last = E // 2 - 1
                turned(0, last)
                gated(1, last)
                out_half(0, last)
                turned(1, last)
                out_half(1, last)
                n_over = v.value_load(novI[0:1, 0:1], min_val=0, max_val=OVER)
                with v.If(n_over > 0):
                    with v.Fori(0, n_over) as j:
                        step_done(v, m, j, "turned")
                        rows_copy(0, 0)
                        rows_copy(0, 1).then_inc(m.o_step, 1)
                        step_done(v, m, j, "up")
                        v.tensor_tensor(ea[0:M, :], eg[0:M, :], up_out(l, 0), ALU.mult).then_inc(m.o_step, 1)
                        step_done(v, m, j, "act_turned")
                        v.tensor_copy(cols(eaT, FC), cols(ps[:, 2, :], FC)).then_inc(m.o_step, 1)
                        step_done(v, m, j, "down")
                        v.tensor_copy(y_part(l, 0, 0), down_out(l, 0))
                        v.tensor_copy(y_part(l, 0, 1), down_out(l, 1)).then_inc(m.o_step, 1)
                with v.Else():
                    v.nop()
                for t in range(T):
                    v.wait_ge(m.y_in[t // 2], 64)
                    v.wait_ge(m.w1_r, t + 1)
                    v.scalar_tensor_tensor(Wt[:, t, :], Ht[:, t, :], wk[:, 1, t:t + 1], Wt[:, t, :],
                                           ALU.mult, ALU.add).then_inc(m.mix_r, 1)
                for g in range(KC * T // 2):
                    st, k = g // KC + t0 // 2, g % KC
                    cs = slice(st * CTX, (st + 1) * CTX)
                    v.wait_ge(m.mix_t, g + 1)
                    v.scalar_tensor_tensor(X[:, k, cs], ps[:, 4 + g % 4, 0:CTX], mod[l][:, 5 * KC + k, st:st + 1],
                                           X[:, k, cs], ALU.mult, ALU.add).then_inc(m.mix_x, 1)

            v.memset(sc[:, :, :], 0.0)
            v.memset(rw[:, :, :], 0.0)
            v.memset(epsc[:, :], EPS).then_inc(eps_r, 1)
            v.wait_ge(vec_t, 1)
            v.tensor_copy(colA[:, :], ps[:, 0, 0:P]).then_inc(vec_c, 1)
            v.wait_ge(vec_t, 2)
            v.tensor_copy(colB[:, :], ps[:, 2, 0:B_ROWS])
            v.tensor_copy(cw[:, :, 0:TAPS], ps[:, 3, 0:256].rearrange("p (j t) -> p j t", j=KC)[:, :, 0:TAPS]).then_inc(vec_c, 1)
            v.wait_ge(vec_c, 2)
            v.wait_ge(ada_c, 4)
            bias_mods(0, 0, 16)
            gain(0, 0).then_inc(modA_r, 1)
            v.wait_ge(x_c, KC)
            norm("mix0", 0)
            v.wait_ge(pad_z, 1)
            for j0 in range(0, KC, 2):
                for j in (j0, j0 + 1):
                    v.wait_ge(pw1_p, 2 * j + 2)
                    v.wait_ge(pw1_s, j + 1)
                    v.scalar_tensor_tensor(U[:, j, :, PAD:PAD + SEQ],
                                           ps[:, 3 + 2 * (j % 2), :].rearrange("p (s t) -> p s t", s=2),
                                           colA[:, A_PW1 + j:A_PW1 + j + 1],
                                           sg[:, j % 2, :].rearrange("p (s t) -> p s t", s=2),
                                           ALU.add, ALU.mult).then_inc(pw1_g, 1)
                v.wait_ge(pw1_g, j0 + 2)
                j = j0
                for tap in range(TAPS):
                    for jj in (j, j + 1):
                        o = Vt[:, jj, :].rearrange("p (s t) -> p s t", s=2)
                        src = U[:, jj, :, tap:tap + SEQ]
                        w = cw[:, jj, tap:tap + 1]
                        if tap == 0:
                            i = v.tensor_scalar(o, src, w, colB[:, B_DWB + jj:B_DWB + jj + 1], ALU.mult, ALU.add)
                        else:
                            v.wait_ge(dve, count[0] - (0 if tap == TAPS - 1 and jj > j else 1))
                            i = v.scalar_tensor_tensor(o, src, w, o, ALU.mult, ALU.add)
                        if tap < TAPS - 1:
                            i.then_inc(dve, 1)
                            count[0] += 1
                        else:
                            i.then_inc(conv_a, 1)
            v.wait_ge(ada_c, 2 * ADA_PC)
            bias_mods(0, 16, MODC)
            bias_mods(1, 0, MODC)
            link(gain(0, 1))
            v.tensor_tensor(gb2[:, :, :], mod[0][:, 2 * KC:3 * KC, :],
                            colB[:, B_PW2:B_PW2 + KC].unsqueeze(2).to_broadcast([P, KC, 2]), ALU.mult).then_inc(modA_r, 1)
            v.wait_ge(mean_p, 1)
            v.wait_ge(conv_a, KC)
            for k in range(KC):
                v.tensor_tensor(Vt[:, k, :], Vt[:, k, :], ps[:, 2, :], ALU.subtract).then_inc(cen, 1)
            rstd("ln", 0)
            v.wait_ge(cen, KC)
            for k in range(KC):
                v.tensor_tensor(Vt[:, k, :], Vt[:, k, :], R[:, :], ALU.mult).then_inc(lnz, 1)
            for j in range(KC):
                v.wait_ge(pw2_t, j + 1)
                v.tensor_tensor(X[:, j, :], X[:, j, :], sg[:, j % 2, :], ALU.add).then_inc(pw2_x, 1)
            v.wait_ge(pw2_x, KC)
            norm("ffn0", 0)
            experts(0)

            chunk_done(v, n_h, "ffn0", KC - 1)
            link(gain(1, 0))
            gain(1, 1).then_inc(modB_r, 1)
            v.wait_ge(moes[0].mix_x, 2 * KC)
            norm("mix1", 0)
            v.wait_ge(lam_in, 16)
            for k in range(2):
                link(v.tensor_tensor(lam[:, 2 * k, :], lam[:, 2 * k, :], lam[:, 2 * k + 1, :], ALU.mult))
                link(v.tensor_reduce(lamt[:, k:k + 1], lam[:, 2 * k, :], AX.X, ALU.add))
            v.nop().then_inc(lam_s, 1)
            link(v.tensor_scalar(subg[:, :], colB[:, B_SUB:B_SUB + 1], 1.0 - LAM_INIT, None, ALU.mult))
            cos, sin = cst[:, C_COS:C_COS + SEQ], cst[:, C_SIN:C_SIN + SEQ]
            def rotary(r):
                t = rotated(r)
                part = R[:, (r % 2) * SEQ:(r % 2 + 1) * SEQ]
                if r >= 2:
                    v.wait_ge(rot_r, r - 1)
                v.wait_ge(rot_p, r + 1)
                v.tensor_tensor(part, ps[:, 7, 0:SEQ], sin, ALU.mult)
                link(v.tensor_tensor(t, t, cos, ALU.mult))
                v.tensor_tensor(t, t, part, ALU.add).then_inc(rot_r, 1)

            v.wait_ge(lam_e, 2)
            link(v.tensor_tensor(lamt[:, 4:5], lamt[:, 3:4], lamt[:, 2:3], ALU.subtract))
            link(v.tensor_scalar(lamt[:, 5:6], lamt[:, 4:5], -LAM_INIT, None, ALU.add))

            def maxima(u):
                b = u % 2
                for c in range(2):
                    v.wait_ge(s_p, 2 * u + c + 1)
                    if u >= 2:
                        v.wait_ge(s_e, 2 * (u - 2) + c + 1)
                    link(v.tensor_reduce(sm[:, b, c, 2:3], ps[:, 2 * b + c, :], AX.X, ALU.max))
                    v.tensor_scalar(sm[:, b, c, 0:1], sm[:, b, c, 2:3], -SCALE, None, ALU.mult).then_inc(s_m, 1)

            def combine(u):
                b = u % 2
                v.wait_ge(s_e, 2 * u + 2)
                link(v.reciprocal(sm[:, b, :, 3], sm[:, b, :, 1]))
                link(v.tensor_tensor(sm[:, b, 1, 3:4], sm[:, b, 1, 3:4], lamt[:, 5:6], ALU.mult))
                link(v.tensor_scalar(pr[:, b, 0, :], pr[:, b, 0, :], sm[:, b, 0, 3:4], None, ALU.mult))
                v.scalar_tensor_tensor(pr[:, b, 0, :], pr[:, b, 1, :], sm[:, b, 1, 3:4], pr[:, b, 0, :],
                                       ALU.mult, ALU.add).then_inc(s_a, 1)

            def out_copy(h):
                v.wait_ge(o_p, h + 1)
                v.tensor_copy(O[:, h, :], ps[:, 5, 0:SEQ]).then_inc(o_c, 1)

            parts = {"rotate": rotary, "scores": maxima, "combine": combine, "values": out_copy}
            for part, n in PLAN:
                if part in parts:
                    parts[part](n)
            for g in range(HEADS // 2):
                v.wait_ge(root, ROOTS["heads"] + g)
                r = HR[:, g * 512:(g + 1) * 512]
                link(v.reciprocal(r, r))
                o = OF[:, g * 512:(g + 1) * 512]
                if g == 0:
                    v.wait_ge(o_c, HEADS)
                v.scalar_tensor_tensor(o, o, subg[:, 0:1], r, ALU.mult, ALU.mult).then_inc(o_n, 1)
            for j in range(KC):
                v.wait_ge(wo_p, j + 1)
                v.scalar_tensor_tensor(X[:, j, CTX:NTOK], ps[:, 4 + j % 4, CTX:NTOK], mod[1][:, 2 * KC + j, 1:2],
                                       X[:, j, CTX:NTOK], ALU.mult, ALU.add).then_inc(wo_x, 1)
            v.wait_ge(wo_x, KC)
            norm("ffn1", CTX)
            experts(1)
            v.wait_ge(moes[1].mix_x, KC)
            rstd("fin", CTX)
            for k in range(KC):
                v.scalar_tensor_tensor(H[:, k, CTX:NTOK], X[:, k, CTX:NTOK], colB[:, B_FIN + k:B_FIN + k + 1],
                                       R[:, CTX:NTOK], ALU.mult, ALU.mult).then_inc(n_h, 1)


_INS = ["x", "c", "ctx", "c_ctx", "ada_w", "ada_b", "norm_mix_g", "norm_ffn_g", "final_norm_g",
        "conv_pw1_w", "conv_pw1_b", "conv_dw_w", "conv_dw_b", "conv_ln_g", "conv_ln_b", "conv_pw2_w",
        "conv_pw2_b", "diff_w_qkv", "diff_lambda", "diff_subln_g", "diff_w_o", "router_w", "router_b",
        "moe_w_gate", "moe_w_up", "moe_w_down"]


def kernel(**inputs):
    import numpy as _np
    import concourse.bacc as _bacc
    from concourse import mybir as _mybir
    from concourse.bass_utils import run_bass_kernel_spmd as _run

    nc = _bacc.Bacc("TRN2", target_bir_lowering=False, num_devices=1)
    arrays, aps = {}, {}
    given = {name: _np.ascontiguousarray(inputs[name]) for name in _INS}
    given["consts"] = constants()
    for name, arr in given.items():
        arrays[f"in_{name}"] = arr
        aps[name] = nc.dram_tensor(f"in_{name}", arr.shape, _mybir.dt.from_np(arr.dtype), kind="ExternalInput").ap()
    out = nc.dram_tensor("out_0", (1, SEQ, D), F32, kind="ExternalOutput").ap()
    build(nc, aps, out)
    r = _run(nc, [arrays], core_ids=[0])
    return r.results[0]["out_0"]
```

```python
from contextlib import ExitStack
import math

import numpy as np

import concourse.bass as bass
from concourse import mybir

F32 = mybir.dt.float32
I32 = mybir.dt.int32
U32 = mybir.dt.uint32
ALU = mybir.AluOpType
ACT = mybir.ActivationFunctionType
AX = mybir.AxisListType

P = 128
D = 1024
KC = D // P
SEQ, CTX = 256, 256
NTOK = SEQ + CTX
NT = NTOK // P
DEPTH = 2
ADA = 6
MODC = ADA * KC
TAPS = 31
PAD = TAPS // 2
UW = SEQ + 2 * PAD
HEADS = 8
HD = 64
E = 16
GROUPS = 4
GS = E // GROUPS
FE = 512
FC = FE // P
EPS = 1e-6
LAM_INIT = 0.8 - 0.6 * math.exp(-0.3 * 1)
SCALE = HD ** -0.5
GRID_W = 64
FREQS = HD // 4
THETA = 10000.0
OVER = 2 * NTOK // (P + 1)
PIECE = KC * FE
RING = 6
BIG = 1e30
QW = 32
QUADS = P // QW

C_ID, C_MEAN, C_HEAD, C_ONE, C_BEFORE, C_ROT = (P * k for k in range(6))
C_COS = 6 * P
C_SIN = C_COS + SEQ
C_EKEY = C_SIN + SEQ
C_GKEY = C_EKEY + NT * E
C_PASS = C_GKEY + NT * GROUPS
C_EXP = C_PASS + OVER * E
C_SEL = C_EXP + OVER * E
C_SELE = C_SEL + 2
C_WROW = C_SELE + E
C_WPAD = C_WROW + 4
C_END = C_WPAD + 2 * E

STEPS = ("free", "turned", "rows", "gate_up", "silu", "act", "act_turned", "act_rows", "down", "out")

A_ADA, A_C, A_CC, A_PW1 = 0, DEPTH * MODC, DEPTH * MODC + KC, DEPTH * MODC + 2 * KC
B_MIX, B_FFN, B_FIN, B_DWB, B_LNG, B_LNB, B_PW2, B_SUB = 0, 16, 32, 40, 48, 56, 64, 72
B_ROWS = 73

TM = [P, P // 2]
MH = P // 2

ADA_PC = ADA * D // FE
REST = [("ada", 0, n) for n in range(4, ADA_PC)] + [("ada", 1, n) for n in range(ADA_PC)]
SEQ_A = ([(("ada", 0, 0), 4), (("ada", 0, 1), 5), (("ada", 0, 2), 0), (("ada", 0, 3), 1),
          (("pw1", 0, 0), 2), (("pw1", 0, 2), 3)]
         + [(REST[0], 4), (REST[1], 5), (REST[2], 6), (("pw1", 0, 1), 0), (("pw1", 0, 3), 1)]
         + [(key, (4, 5, 6)[n % 3]) for n, key in enumerate(REST) if n >= 3]
         + [(("pw2", 0, 0), 2), (("pw2", 0, 1), 3)])
SEQ_B = [(("qkv", 0, n), slot) for n, slot in zip((0, 2, 4, 1, 3, 5), (0, 1, 4, 5, 2, 3))] + [(("wo", 0, 0), 0), (("wo", 0, 1), 1)]
SETS = [((0, 1, 4), (5, 2, 3)), ((4, 5, 2), (3, 0, 1))]
CONV_GROUPS = [(0,), (1, 2), (3, 4), (5, 6), (7,)]
FILL, _g = [], 4
for _n in (0, 0, 2, 2, 3, 3, 4, 6):
    FILL.append(range(_g, _g + _n))
    _g += _n
assert _g == DEPTH * ADA_PC

UNITS = 2 * HEADS
PLAN = []
for _i in range(12):
    PLAN += [("product", _i)] + ([("rotate", _i - 1)] if 1 <= _i <= 8 else [])
_next = 12
for _u in range(UNITS + 3):
    if _u < UNITS:
        PLAN.append(("scores", _u))
    if _u >= 4 and _u % 2 == 0:
        PLAN.append(("values", (_u - 3) // 2))
    if 2 <= _u < UNITS + 2:
        PLAN.append(("weights", _u - 2))
    if 1 <= _u <= UNITS:
        PLAN.append(("combine", _u - 1))
    for _ in range((2 - _u % 2) if _u < UNITS // 2 else 0):
        PLAN.append(("product", _next))
        if 13 <= _next <= 20:
            PLAN.append(("rotate", _next - 5))
        _next += 1

PLACE, _held = {}, [[] for _ in range(RING + 1)]
for _l, _seq in enumerate((SEQ_A, SEQ_B)):
    for _key, _slot in _seq:
        PLACE[_key] = (_slot, len(_held[_slot]), _held[_slot][-1] if _held[_slot] else None)
        _held[_slot].append(_key)
    for _b in range(2):
        for _k in range(3):
            _slot = SETS[_l][_b][_k]
            PLACE[("moe", _l, _b, _k)] = (_slot, len(_held[_slot]), _held[_slot][-1])
            _held[_slot] += [("moe", _l, _b, _k)] * (E // 2)


def constants():
    c = np.zeros((P, C_END), np.float32)
    i = np.arange(P)
    c[:, C_ID:C_ID + P] = np.eye(P)
    c[:, C_MEAN:C_MEAN + P] = 1.0 / D
    c[:, C_HEAD:C_HEAD + P] = 1.0 / P
    c[:, C_ONE:C_ONE + P] = 1.0
    c[:, C_BEFORE:C_BEFORE + P] = i[:, None] < i[None, :]
    half = (i // FREQS) % 2
    for m in range(P):
        if half[m]:
            c[m - FREQS, C_ROT + m] = 1.0
        else:
            c[m + FREQS, C_ROT + m] = -1.0
    axis, f = (i // (2 * FREQS)) % 2, i % FREQS
    tok = np.arange(SEQ)
    inv = (THETA ** (-np.arange(FREQS, dtype=np.float64) / FREQS)).astype(np.float32)
    pos = np.where(axis[:, None] == 0, tok[None, :] // GRID_W, tok[None, :] % GRID_W).astype(np.float32)
    ang = pos * inv[f][:, None]
    c[:, C_COS:C_COS + SEQ] = np.cos(ang)
    c[:, C_SIN:C_SIN + SEQ] = np.sin(ang)
    c[:, C_EKEY:C_EKEY + NT * E] = np.tile(E - np.arange(E), NT)
    c[:, C_GKEY:C_GKEY + NT * GROUPS] = np.tile(GROUPS - np.arange(GROUPS), NT)
    c[:, C_PASS:C_PASS + OVER * E] = np.repeat(np.arange(OVER), E)
    c[:, C_EXP:C_EXP + OVER * E] = np.tile(np.arange(E), OVER)
    for s in range(2):
        c[s::QW, C_SEL + s] = 1.0
    for e in range(E):
        c[e::QW, C_SELE + e] = 1.0
    for h in range(2):
        for e in range(E):
            c[:, C_WPAD + h * E + e] = 4 * NTOK + (2 * (e % 2) + h) * P + i
        c[:, C_WROW + 2 * h] = h * MH + i % MH
        c[:, C_WROW + 2 * h + 1] = 2 * (h * MH + i % MH) + i // MH
    return c


def build(nc, a, out):
    with ExitStack() as ctx:
        def sb(name, shape, dt=F32):
            return ctx.enter_context(nc.sbuf_tensor(name, shape, dt))

        def sem(name):
            return ctx.enter_context(nc.semaphore(name))

        ring = sb("ring", [P, RING, PIECE])
        X = sb("X", [P, KC, NTOK])
        H = sb("H", [P, KC, NTOK])
        UB = sb("UB", [P, KC * 2 * UW])
        V = sb("V", [P, KC * NTOK])
        W = sb("W", [P, NT * D])
        cst = sb("cst", [P, C_END])
        rowsA = sb("rowsA", [P, P])
        rowsB = sb("rowsB", [P, P])
        colA = sb("colA", [P, P])
        colB = sb("colB", [P, B_ROWS])
        cw = sb("cw", [P, KC, 32])
        rw = sb("rw", [P, KC, QW])
        rb = sb("rb", [P, E])
        sc = sb("sc", [P, KC, QW])
        mod = [sb(f"mod{l}", [P, MODC, 2]) for l in range(DEPTH)]
        modA = sb("modA", [P, 2, KC, 2])
        gb2 = sb("gb2", [P, KC, 2])
        R = sb("R", [P, NTOK])
        epsc = sb("epsc", [P, 1])
        sg = sb("sg", [P, 2, NTOK])
        lam = sb("lam", [P, 4, HD])
        lamt = sb("lamt", [P, 8])
        sm = sb("sm", [P, 2, 2, 4])
        subg = sb("subg", [P, 1])
        score = sb("score", [P, NT, E])
        sel = sb("sel", [P, NT, E])
        msel = sb("msel", [P, NT, E])
        tA = sb("tA", [P, NT, E])
        tB = sb("tB", [P, NT, E])
        oh = sb("oh", [P, 2, NT, E])
        pair = sb("pair", [P, 2, NT, E])
        g4 = sb("g4", [P, 10, NT * GROUPS])
        t1 = sb("t1", [P, 12, NT])
        wk = sb("wk", [P, 2, NT])
        slot = sb("slot", [P, 2 * NT], I32)
        ints = sb("ints", [P, 2, 24])
        offI = sb("offI", [P, 24], I32)
        numI = sb("numI", [P, E], I32)
        wrow = sb("wrow", [P, E, 2], I32)
        wcur = sb("wcur", [P, 2, 2], I32)
        cum = sb("cum", [P, 2, 8 + E])
        ov = sb("ov", [P, 4, OVER * E])
        ovf = sb("ovf", [P, 2, 8])
        ovI = sb("ovI", [P, 3, 8], I32)
        novI = sb("novI", [P, 1], I32)
        zrow = sb("zrow", [P, D])
        ps = ctx.enter_context(nc.psum_tensor("ps", [P, 8, 512], F32))

        tap_rows = H[:, 0:2, :].rearrange("p j t -> p (j t)")
        U = UB[:, :].rearrange("p (j s w) -> p j s w", j=KC, s=2)
        Vt = V[:, :].rearrange("p (j t) -> p j t", j=KC)
        Wt = W[:, :].rearrange("p (t d) -> p t d", t=NT)
        Ht = H[:, :, :].rearrange("p j t -> p (j t)").rearrange("p (t d) -> p t d", t=NT)
        hrow = UB[:, 0:2 * D].rearrange("p (b d) -> p b d", b=2)
        hT = UB[:, 2 * D:4 * D].rearrange("p (b d) -> p b d", b=2)
        yrow = V[:, 0:2 * D].rearrange("p (b d) -> p b d", b=2)
        eg = V[:, 2 * D:2 * D + FE]
        ea = V[:, 2 * D + FE:2 * D + 2 * FE]
        eaT = V[:, 3 * D:3 * D + FE]
        Q = UB[:, 0:HEADS * SEQ].rearrange("p (h t) -> p h t", h=HEADS)
        pr = UB[:, HEADS * SEQ:HEADS * SEQ + 4 * NTOK].rearrange("p (b c t) -> p b c t", b=2, c=2)
        K = Vt
        O = Q
        OF = UB[:, 0:HEADS * SEQ]
        aT = [x.rearrange("p (k t) -> p k t", k=NT) for x in (sg[:, :, :].rearrange("p a b -> p (a b)"), zrow[:, :])]
        adaR = zrow[:, :].rearrange("p (b n) -> p b n", b=2)
        HR = H[:, 0:4, :].rearrange("p j t -> p (j t)")

        Hs = nc.dram_tensor("token_rows", (2 * NTOK + P, D), F32, kind="Internal").ap()
        Ys = nc.dram_tensor("expert_rows", (2 * NTOK + 2 * P + 2, D), F32, kind="Internal").ap()

        def C(at, n=P):
            return cst[:, at:at + n]

        ident, mean, head_mean, ones, before, rot = (C(k) for k in (C_ID, C_MEAN, C_HEAD, C_ONE, C_BEFORE, C_ROT))

        w_in = [sem(f"w_in{s}") for s in range(RING + 1)]
        cst_in, vec_in, x_in, rw_in, lam_in = (sem(n) for n in ("cst_in", "vec_in", "x_in", "rw_in", "lam_in"))
        vecA_in = sem("vecA_in")
        vec_t, vec_c = sem("vec_t"), sem("vec_c")
        x_t, x_c = sem("x_t"), sem("x_c")
        c_silu = sem("c_silu")
        ada_p, ada_r, ada_t, ada_c = sem("ada_p"), sem("ada_r"), sem("ada_t"), sem("ada_c")
        modA_r, modB_r = sem("modA_r"), sem("modB_r")
        pad_z = sem("pad_z")
        dve = sem("dve_chain")
        pw1_p, pw1_s, pw1_g = sem("pw1_p"), sem("pw1_s"), sem("pw1_g")
        conv_a = sem("conv_a")
        mean_p, cen, cen_sq, var_p, lnz, ln_s = (sem(n) for n in ("mean_p", "cen", "cen_sq", "var_p", "lnz", "ln_s"))
        pw2_p, pw2_t, pw2_x = sem("pw2_p"), sem("pw2_t"), sem("pw2_x")
        prod_p, prod_c, rot_p, rot_r = sem("prod_p"), sem("prod_c"), sem("rot_p"), sem("rot_r")
        s_p, s_m, s_e, s_a, a_t, a_c, o_p, o_c = (sem(n) for n in (
            "s_p", "s_m", "s_e", "s_a", "a_t", "a_c", "o_p", "o_c"))
        o_sq, o_ms, o_n = sem("o_sq"), sem("o_ms"), sem("o_n")
        wo_p, wo_x = sem("wo_p"), sem("wo_x")
        fin_t, fin_c, out_w = sem("fin_t"), sem("fin_c"), sem("out_w")
        hs_pad = sem("hs_pad")
        lam_s, lam_e = sem("lam_s"), sem("lam_e")
        eps_r, n_log, n_inv = sem("eps_r"), sem("n_log"), sem("n_inv")
        FACTORS = {"mix0": 1, "ln": 2, "ffn0": 3, "mix1": 4, "heads": 5, "ffn1": 9, "fin": 10}

        n_sq, n_ms, n_hr, n_h = sem("n_sq"), sem("n_ms"), sem("n_hr"), sem("n_h")
        NORM = {k: i for i, k in enumerate(("mix0", "ffn0", "mix1", "ffn1", "fin"))}

        def chunk_done(eng, s, name, k):
            eng.wait_ge(s, NORM[name] * KC + k + 1)

        class Moe:
            def __init__(self, l):
                def s(k):
                    return sem(f"m{l}_{k}")
                self.route_p, self.route_c, self.route_t, self.score_r, self.pair_r, self.rank_p = (
                    s(k) for k in ("route_p", "route_c", "route_t", "score_r", "pair_r", "rank_p"))
                self.slot_r, self.over_r = s("slot_r"), s("over_r")
                self.rows_t, self.rows_c, self.scat = s("rows_t"), s("rows_c"), s("scat")
                self.h_in = [s("h_in0"), s("h_in1")]
                self.h_t, self.h_c = s("h_t"), s("h_c")
                self.gate_p, self.gate_s, self.act_r, self.down_p, self.y_c = (
                    [s(f"{k}{h}") for h in range(TM[l] // MH)] for k in ("gate_p", "gate_s", "act_r", "down_p", "y_c"))
                self.act_t, self.act_c = s("act_t"), s("act_c")
                self.y_out, self.y_free = [s("y_out0"), s("y_out1")], s("y_free")
                self.w_cur, self.w_now = s("w_cur"), s("w_now")
                self.end = s("end")
                self.o_step, self.o_in, self.o_w, self.o_out = (s(k) for k in ("o_step", "o_in", "o_w", "o_out"))
                self.y_in = [s("y_in0"), s("y_in1")][0:l and 1 or 2]
                self.w1_r = s("w1_r")
                self.mix_r, self.mix_t, self.mix_x = (s(k) for k in ("mix_r", "mix_t", "mix_x"))

        moes = [Moe(l) for l in range(DEPTH)]
        VECS = 9
        TL = [NT, SEQ // P]
        T0 = [0, CTX // P]

        def piece_src(kind, l, n):
            cols = slice(n * FE, (n + 1) * FE)
            w = {"ada": a["ada_w"][l], "pw1": a["conv_pw1_w"][0], "pw2": a["conv_pw2_w"][0],
                 "qkv": a["diff_w_qkv"][0], "wo": a["diff_w_o"][0]}[kind]
            return w[:, cols].rearrange("(j p) n -> p j n", p=P)

        def slot_tile(slot):
            return W[:, :] if slot == RING else ring[:, slot, :]

        def piece(key):
            return slot_tile(PLACE[key][0]).rearrange("p (j n) -> p j n", j=KC)

        def landed(eng, key):
            eng.wait_ge(w_in[PLACE[key][0]], 16 * (PLACE[key][1] + 1))

        last_read = {}
        for n in range(ADA_PC):
            last_read[("ada", 0, n)] = (ada_p, n + 1)
            last_read[("ada", 1, n)] = (ada_p, ADA_PC + n + 1)
        last_read[("pw1", 0, 0)] = last_read[("pw1", 0, 2)] = (pw1_p, KC)
        last_read[("pw1", 0, 1)] = last_read[("pw1", 0, 3)] = (pw1_p, 2 * KC)
        last_read[("pw2", 0, 0)], last_read[("pw2", 0, 1)] = (pw2_p, KC // 2), (pw2_p, KC)
        for n in range(2):
            for q in range(3):
                last_read[("qkv", 0, 2 * q + n)] = (prod_p, 12 * n + 4 * (q + 1))
            last_read[("wo", 0, n)] = (wo_p, KC // 2 * (n + 1))
        for l in range(DEPTH):
            for b in range(2):
                for k, products in enumerate((moes[l].gate_p, moes[l].gate_p, moes[l].down_p)):
                    last_read[("moe", l, b, k)] = (products, E - 1 + b)

        def expert_landed(eng, l, b, k, i):
            slot, n, _ = PLACE[("moe", l, b, k)]
            eng.wait_ge(w_in[slot], i * 16 + 16 * (n + 1))

        def gate_out(h):
            return ps[0:MH, h, :]

        def up_out(h):
            return ps[MH:P, h, :]

        def acts(x, h):
            return x[h * MH:(h + 1) * MH, :]

        def down_out(h):
            return ps[:, 3 + h, :]

        def y_part(b, h):
            return yrow[:, b, h * 512:(h + 1) * 512]

        def write_rows(pool, b, h, r, s):
            for c in range(2):
                pool.dma_start(Ys[bass.ds(r + h * MH, MH), c * 512:(c + 1) * 512],
                               y_part(b, h)[c * MH:(c + 1) * MH, :]).then_inc(s, 16)

        def with_half(eng, h, e, run, skip):
            if h == 0:
                run()
                return
            n = eng.value_load(numI[0:1, bass.ds(e, 1)], min_val=0, max_val=2 * NTOK)
            with eng.If(n > MH):
                run()
            with eng.Else():
                skip()

        def step_done(eng, m, j, step):
            eng.wait_ge(m.o_step, j * len(STEPS) + (STEPS.index(step) + 1))

        def rotated(r):
            is_k, g = divmod(r % 8, 4)
            h = 4 * (r // 8) + g
            return K[:, h, CTX:NTOK] if is_k else Q[:, h, :]

        def gate_tile(s):
            return ring[:, s, :].rearrange("p (j n) -> p j n", j=KC)

        def down_tile(s):
            return ring[:, s, :].rearrange("p (j n) -> p j n", j=FC)

        block = ctx.enter_context(nc.Block())

        @block.sync
        def _(sp):
            def free(key):
                if PLACE[key][2] is not None:
                    sems, n = last_read[PLACE[key][2]]
                    for s in sems if isinstance(sems, list) else [sems]:
                        sp.wait_ge(s, n)

            def load(key):
                free(key)
                if PLACE[key][0] == RING and PLACE[key][1] == 0:
                    sp.wait_ge(x_t, KC)
                kind, l, m = key
                sp.dma_start(piece(key), piece_src(kind, l, m)).then_inc(w_in[PLACE[key][0]], 16)

            def expert_srcs(l, e):
                return [a["moe_w_gate"][l].rearrange("e (p j) n -> e p (j n)", j=KC)[e],
                        a["moe_w_up"][l].rearrange("e (p j) n -> e p (j n)", j=KC)[e],
                        a["moe_w_down"][l].rearrange("e (p j) n -> e p (j n)", j=FC)[e]]

            def experts(l):
                m = moes[l]
                for b in range(2):
                    for k, src in enumerate(expert_srcs(l, b)):
                        free(("moe", l, b, k))
                        slot = SETS[l][b][k]
                        sp.dma_start(ring[:, slot, :], src).then_inc(w_in[slot], 16)
                M = TM[l]
                sp.wait_ge(m.slot_r, 1)
                for b in range(2):
                    r = sp.value_load(offI[0:1, b:b + 1], min_val=0, max_val=2 * NTOK)
                    sp.wait_ge(m.scat, 32 * TL[l])
                    sp.wait_ge(hs_pad, 16)
                    sp.dma_start(hrow[0:M, b, :], Hs[bass.ds(r, M), :]).then_inc(m.h_in[b], 16)
                r = sp.value_load(offI[0:1, 2:3], min_val=0, max_val=2 * NTOK)
                sp.wait_ge(m.h_t, 2)
                sp.dma_start(hrow[0:M, 0, :], Hs[bass.ds(r, M), :]).then_inc(m.h_in[0], 16)
                with sp.Fori(0, E // 2 - 1) as i:
                    for b in range(2):
                        for k, src in enumerate(expert_srcs(l, i * 2 + (2 + b))):
                            if k == 0:
                                for s in m.gate_p:
                                    sp.wait_ge(s, i * 2 + (b + 1))
                            elif k == 2:
                                r = sp.value_load(offI[0:1, bass.ds(i * 2 + (b + 3), 1)], min_val=0, max_val=2 * NTOK)
                                sp.wait_ge(m.scat, 32 * TL[l])
                                sp.wait_ge(m.h_t, i * 4 + (2 * b + 4))
                                sp.dma_start(hrow[0:M, 1 - b, :], Hs[bass.ds(r, M), :]).then_inc(m.h_in[1 - b], 16)
                                for s in m.down_p:
                                    sp.wait_ge(s, i * 2 + (b + 1))
                            slot = SETS[l][b][k]
                            sp.dma_start(ring[:, slot, :], src).then_inc(w_in[slot], 16)
                sp.wait_ge(m.h_in[0], 16 * (E // 2 + 1))
                sp.wait_ge(m.over_r, 1)
                n_over = sp.value_load(novI[0:1, 0:1], min_val=0, max_val=OVER)
                with sp.If(n_over > 0):
                    with sp.Fori(0, n_over) as j:
                        e = sp.value_load(ovI[0:1, 0, bass.ds(j, 1)], min_val=0, max_val=E - 1)
                        step_done(sp, m, j, "free")
                        for k, src in enumerate(expert_srcs(l, e)):
                            sp.dma_start(ring[:, SETS[l][0][k], :], src).then_inc(m.o_w, 16)
                    sp.wait_ge(m.end, 1)
                with sp.Else():
                    sp.nop()

            sp.dma_start(Wt[:, 0:2, :], a["ctx"][0].rearrange("(t p) d -> p t d", p=P)).then_inc(x_in, 16)
            sp.dma_start(Wt[:, 2:4, :], a["x"][0].rearrange("(t p) d -> p t d", p=P)).then_inc(x_in, 16)
            sp.wait_ge(cst_in, 16)
            sp.wait_ge(vecA_in, 64)
            for key, _ in SEQ_A:
                load(key)
            experts(0)
            for n, (key, _) in enumerate(SEQ_B):
                if n == 2:
                    for s in moes[0].y_in:
                        sp.wait_ge(s, 64)
                load(key)
            experts(1)
            sp.wait_ge(fin_c, 2 * KC // 4)
            for t in range(2):
                sp.dma_start(out[0, t * P:(t + 1) * P, :], Wt[:, t, :]).then_inc(out_w, 16)
            sp.wait_ge(out_w, 32)

        @block.gpsimd
        def _(pool):
            pool.memset(UB[:, :], 0.0).then_inc(pad_z, 1)
            pool.wait_ge(ada_t, DEPTH * ADA_PC)
            pool.memset(zrow[:, :], 0.0).then_inc(pad_z, 1)
            pool.wait_ge(pad_z, 2)
            pool.dma_start(Hs[2 * NTOK:2 * NTOK + P, :], zrow[:, :]).then_inc(hs_pad, 16)

            def experts(l):
                m = moes[l]
                T, M, NH = TL[l], TM[l], TM[l] // MH
                pool.wait_ge(m.slot_r, 1)
                for t in range(T):
                    pool.wait_ge(m.rows_c, 2 * (t + 1))
                    for k in range(2):
                        pool.indirect_dma_start(
                            Hs[:, :], bass.IndirectOffsetOnAxis(ap=slot[:, k * NT + t:k * NT + t + 1].bitcast(U32), axis=0),
                            Wt[:, t, :], None).then_inc(m.scat, 16)
                if l == 0:
                    pool.wait_ge(hs_pad, 16)
                for b in range(2):
                    pool.nop().then_inc(m.y_free, 1)
                pool.wait_ge(m.over_r, 1)
                Yhalf = Ys[:, :].rearrange("r (c n) -> (r c) n", c=2)

                def write(b, i):
                    e = i * 2 + b
                    def half(h):
                        pool.indirect_dma_start(Yhalf, bass.IndirectOffsetOnAxis(ap=wcur[:, b, h:h + 1].bitcast(U32), axis=0),
                                                y_part(b, h), None).then_inc(m.y_out[b], 16)

                    pool.tensor_copy(wcur[:, b, :], wrow[:, bass.ds(e, 1), :].rearrange("p a h -> p (a h)")).then_inc(m.w_cur, 1)
                    for s in m.y_c:
                        pool.wait_ge(s, e + 2)
                    pool.wait_ge(m.w_cur, e + 1)
                    pool.nop().then_inc(m.w_now, 1)
                    half(0)
                    if NH == 2:
                        n = pool.value_load(numI[0:1, bass.ds(e, 1)], min_val=0, max_val=2 * NTOK)
                        with pool.If(n > MH):
                            half(1)
                        with pool.Else():
                            pool.dma_start(Ys[2 * NTOK + 2 * P + b:2 * NTOK + 2 * P + b + 1, 0:QW], zrow[0:1, 0:QW]).then_inc(m.y_out[b], 16)

                def written(b, i):
                    pool.wait_ge(m.y_out[b], i * 16 * NH + 16 * NH)
                    pool.nop().then_inc(m.y_free, 1)

                write(0, 0)
                with pool.Fori(0, E // 2 - 1) as i:
                    for b in range(2):
                        write(1 - b, i + b)
                        written(b, i)
                write(1, E // 2 - 1)
                for b in range(2):
                    written(b, E // 2 - 1)
                n_over = pool.value_load(novI[0:1, 0:1], min_val=0, max_val=OVER)
                with pool.If(n_over > 0):
                    with pool.Fori(0, n_over) as j:
                        r = pool.value_load(ovI[0:1, 1, bass.ds(j, 1)], min_val=0, max_val=2 * NTOK)
                        step_done(pool, m, j, "free")
                        pool.wait_ge(m.h_in[0], 16 * (E // 2 + 1))
                        pool.wait_ge(m.scat, 32 * T)
                        pool.dma_start(hrow[0:M, 0, :], Hs[bass.ds(r, M), :]).then_inc(m.o_in, 16)
                        step_done(pool, m, j, "out")
                        r = pool.value_load(ovI[0:1, 2, bass.ds(j, 1)], min_val=0, max_val=2 * NTOK)
                        for h in range(NH):
                            write_rows(pool, 0, h, r, m.o_out)
                        pool.wait_ge(m.o_out, j * 32 * NH + 32 * NH)
                with pool.Else():
                    pool.nop()
                pool.wait_ge(m.end, 1)
                for t in range(T):
                    for k, dst in enumerate((Wt, Ht)):
                        pool.indirect_dma_start(
                            dst[:, t, :], None, Ys[0:2 * NTOK, :],
                            bass.IndirectOffsetOnAxis(ap=slot[:, k * NT + t:k * NT + t + 1].bitcast(U32), axis=0)
                        ).then_inc(m.y_in[t // 2], 16)

            for l in range(DEPTH):
                experts(l)

        @block.tensor
        def _(pe):
            def turn(out, in_, n=P):
                return pe.transpose(out, in_, ident[0:n, 0:n])

            def ada_rows(g):
                key = ("ada", g // ADA_PC, g % ADA_PC)
                landed(pe, key)
                if g >= 2:
                    pe.wait_ge(ada_r, g - 1)
                for r in range(KC // QUADS):
                    for q in range(QUADS):
                        k = r * QUADS + q
                        mm = pe.matmul(ps[q * QW:(q + 1) * QW, g % 2, :], sc[:, k, :], piece(key)[:, k, :],
                                       start=(r == 0), stop=(r == KC // QUADS - 1))
                mm.then_inc(ada_p, 1)

            def ada_turn(g):
                pe.wait_ge(ada_r, g + 1)
                if g >= 1:
                    pe.wait_ge(ada_c, g)
                for q in range(FC):
                    mm = pe.matmul(ps[:, 7, 2 * q:2 * q + 2], adaR[:, g % 2, q * P:(q + 1) * P], C(C_SEL, 2),
                                   start=True, stop=True)
                mm.then_inc(ada_t, 1)

            def norm(name, sq, c0, bank):
                for k in range(KC):
                    chunk_done(pe, n_sq, name, k)
                    mm = pe.matmul(ps[:, bank, c0:NTOK], mean, sq[:, k, c0:NTOK], start=(k == 0), stop=(k == KC - 1))
                mm.then_inc(n_ms, 1)

            def experts(l):
                m = moes[l]
                T, t0, M, NH = TL[l], T0[l], TM[l], TM[l] // MH
                c0 = t0 * P
                pe.wait_ge(rw_in, 32)
                for k in range(KC):
                    chunk_done(pe, n_h, f"ffn{l}", k)
                    q, r = k % QUADS, k // QUADS
                    mm = pe.matmul(ps[q * QW:(q + 1) * QW, 3, c0:NTOK], rw[:, k, :], H[:, k, c0:NTOK],
                                   start=(r == 0), stop=(r == KC // QUADS - 1))
                mm.then_inc(m.route_p, 1)
                for t in range(T):
                    for h in range(2):
                        g = 2 * t + h
                        if g >= 4:
                            pe.wait_ge(m.rows_c, g - 3)
                        for k in range(4):
                            mm = turn(ps[:, 4 + g % 4, k * P:(k + 1) * P],
                                      H[:, 4 * h + k, (t0 + t) * P:(t0 + t + 1) * P])
                        mm.then_inc(m.rows_t, 1)
                    if t == 0:
                        pe.wait_ge(m.route_c, 1)
                        for u in range(T):
                            mm = pe.matmul(ps[:, 2, u * E:(u + 1) * E], R[:, c0 + u * P:c0 + (u + 1) * P], C(C_SELE, E),
                                           start=True, stop=True)
                        mm.then_inc(m.route_t, 1)
                pe.wait_ge(m.pair_r, 1)
                pe.matmul(ps[:, 2, 2 * T * E:3 * T * E], before, pair[:, 0, 0:T, :], start=True, stop=True)
                for q in range(2):
                    mm = pe.matmul(ps[:, 2, q * T * E:(q + 1) * T * E], ones, pair[:, q, 0:T, :], start=True, stop=True)
                mm.then_inc(m.rank_p, 1)

                def rows_turned(b, s):
                    hv = hrow[:, b, :].rearrange("p (n j) -> p j n", j=KC)
                    for k in range(KC):
                        mm = turn(ps[:, 5 + k // 4, (k % 4) * P:(k % 4 + 1) * P], hv[:, k, :])
                        if s is m.h_t and k == 3:
                            mm.then_inc(s, 1)
                    mm.then_inc(s, 1)

                tiles = [[gate_tile(SETS[l][b][0]), gate_tile(SETS[l][b][1]), down_tile(SETS[l][b][2])] for b in range(2)]

                def product_in(b, h):
                    for k in range(KC):
                        for dst, w in ((gate_out(h), tiles[b][0]), (up_out(h), tiles[b][1])):
                            mm = pe.matmul(dst, hT[:, b, k * P + h * MH:k * P + (h + 1) * MH], w[:, k, :],
                                           start=(k == 0), stop=(k == KC - 1))
                    return mm

                def act_turned(s):
                    av = ea.rearrange("p (n j) -> p j n", j=FC)
                    for k in range(FC):
                        mm = turn(ps[:, 2, k * P:(k + 1) * P], av[:, k, :])
                    mm.then_inc(s, 1)

                def product_down(b, h):
                    for k in range(FC):
                        for c in range(2):
                            mm = pe.matmul(down_out(h)[c * MH:(c + 1) * MH, :], eaT[:, k * P + h * MH:k * P + (h + 1) * MH],
                                           tiles[b][2][:, k, c * 512:(c + 1) * 512], start=(k == 0), stop=(k == FC - 1))
                    return mm

                def rows(b, i):
                    pe.wait_ge(m.h_in[b], i * 16 + 16)
                    rows_turned(b, m.h_t)

                def gate_up(b, i, first=False):
                    e = i * 2 + b
                    pe.wait_ge(m.h_c, e + 1)
                    expert_landed(pe, l, b, 0, i)
                    expert_landed(pe, l, b, 1, i)
                    for h in range(NH):
                        def run():
                            if not first:
                                pe.wait_ge(m.act_r[h], e)
                            product_in(b, h).then_inc(m.gate_p[h], 1)

                        def skip():
                            pe.wait_ge(m.gate_p[0], e + 1)
                            pe.nop().then_inc(m.gate_p[h], 1)

                        with_half(pe, h, e, run, skip)

                def turned(b, i):
                    for s in m.act_r:
                        pe.wait_ge(s, i * 2 + (b + 1))
                    act_turned(m.act_t)

                def down(b, i):
                    e = i * 2 + b
                    expert_landed(pe, l, b, 2, i)
                    pe.wait_ge(m.act_c, e + 1)
                    for h in range(NH):
                        def run():
                            pe.wait_ge(m.y_c[h], e + 1)
                            product_down(b, h).then_inc(m.down_p[h], 1)

                        def skip():
                            pe.wait_ge(m.down_p[0], e + 1)
                            pe.nop().then_inc(m.down_p[h], 1)

                        with_half(pe, h, e, run, skip)

                pe.wait_ge(m.over_r, 1)
                pe.wait_ge(m.rows_c, 2 * T)
                rows(0, 0)
                gate_up(0, 0, first=True)
                rows(1, 0)
                with pe.Fori(0, E // 2 - 1) as i:
                    gate_up(1, i)
                    turned(0, i)
                    rows(0, i + 1)
                    down(0, i)
                    gate_up(0, i + 1)
                    turned(1, i)
                    rows(1, i + 1)
                    down(1, i)
                last = E // 2 - 1
                gate_up(1, last)
                turned(0, last)
                down(0, last)
                turned(1, last)
                down(1, last)
                pe.wait_ge(m.over_r, 1)
                n_over = pe.value_load(novI[0:1, 0:1], min_val=0, max_val=OVER)
                for s in m.y_c:
                    pe.wait_ge(s, E + 1)
                pe.wait_ge(m.y_free, E + 2)
                pe.nop().then_inc(m.o_step, 1)
                with pe.If(n_over > 0):
                    with pe.Fori(0, n_over) as j:
                        pe.wait_ge(m.o_in, j * 16 + 16)
                        pe.wait_ge(m.o_w, j * 48 + 48)
                        rows_turned(0, m.o_step)
                        step_done(pe, m, j, "rows")
                        for h in range(NH):
                            mm = product_in(0, h)
                        mm.then_inc(m.o_step, 1)
                        step_done(pe, m, j, "act")
                        act_turned(m.o_step)
                        step_done(pe, m, j, "act_rows")
                        for h in range(NH):
                            mm = product_down(0, h)
                        mm.then_inc(m.o_step, 1)
                        step_done(pe, m, j, "out")
                        pe.wait_ge(m.o_out, j * 32 * NH + 32 * NH)
                        pe.nop().then_inc(m.o_step, 1)
                with pe.Else():
                    pe.nop()
                pe.nop().then_inc(m.end, 1)
                for g in range(KC * T // 2):
                    st, k = g // KC + t0 // 2, g % KC
                    if k == 0:
                        pe.wait_ge(m.mix_r, 2 * (g // KC) + 2)
                    if g >= 4:
                        pe.wait_ge(m.mix_x, g - 3)
                    for t in range(2):
                        mm = turn(ps[:, 4 + g % 4, t * P:(t + 1) * P], Wt[:, 2 * st - t0 + t, k * P:(k + 1) * P])
                    mm.then_inc(m.mix_t, 1)

            pe.wait_ge(cst_in, 16)
            pe.wait_ge(vecA_in, 64)
            turn(ps[:, 0, 0:P], rowsA[:, :]).then_inc(vec_t, 1)
            pe.wait_ge(x_in, 32)
            for k in range(KC):
                if k >= 4:
                    pe.wait_ge(x_c, k - 3)
                for t in range(NT):
                    mm = turn(ps[:, 4 + k % 4, t * P:(t + 1) * P], Wt[:, t, k * P:(k + 1) * P])
                mm.then_inc(x_t, 1)
            pe.wait_ge(vec_in, 16 * VECS)
            turn(ps[:, 2, 0:B_ROWS], rowsB[0:B_ROWS, :], B_ROWS)
            for k in range(KC):
                mm = turn(ps[:, 3, 32 * k:32 * k + TAPS], tap_rows[0:TAPS, k * P:(k + 1) * P], TAPS)
            mm.then_inc(vec_t, 1)
            pe.wait_ge(c_silu, 2)
            pe.wait_ge(x_c, KC)
            for g in range(4):
                ada_rows(g)
                if g:
                    ada_turn(g - 1)
            ada_turn(3)
            pe.wait_ge(vec_c, 2)
            norm("mix0", Vt, 0, 2)
            pe.wait_ge(x_c, KC)
            for j in range(KC):
                if j >= 2:
                    pe.wait_ge(pw1_g, j - 1)
                for h in (1, 0):
                    key = ("pw1", 0, 2 * h + j // 4)
                    landed(pe, key)
                    w = piece(key)
                    for k in range(KC):
                        if j == 0 and h:
                            chunk_done(pe, n_h, "mix0", k)
                        mm = pe.matmul(ps[:, 3 + 2 * (j % 2) + h, :], w[:, k, (j % 4) * P:(j % 4 + 1) * P], H[:, k, :],
                                       start=(k == 0), stop=(k == KC - 1))
                    mm.then_inc(pw1_p, 1)
                for g in FILL[j]:
                    ada_rows(g)
                    if g > 4:
                        ada_turn(g - 1)
            ada_turn(DEPTH * ADA_PC - 1)
            for k in range(KC):
                pe.wait_ge(conv_a, k + 1)
                mm = pe.matmul(ps[:, 2, :], mean, Vt[:, k, :], start=(k == 0), stop=(k == KC - 1))
            mm.then_inc(mean_p, 1)
            for k in range(KC):
                pe.wait_ge(cen_sq, k + 1)
                mm = pe.matmul(ps[:, 3, :], mean, H[:, k, :], start=(k == 0), stop=(k == KC - 1))
            mm.then_inc(var_p, 1)
            pe.wait_ge(pw1_g, KC)
            for j in range(KC):
                key = ("pw2", 0, j // 4)
                landed(pe, key)
                if j >= 4:
                    pe.wait_ge(pw2_t, j - 3)
                for k in range(KC):
                    if j == 0:
                        pe.wait_ge(ln_s, k + 1)
                    mm = pe.matmul(ps[:, 4 + j % 4, :], piece(key)[:, k, (j % 4) * P:(j % 4 + 1) * P], H[:, k, :],
                                   start=(k == 0), stop=(k == KC - 1))
                mm.then_inc(pw2_p, 1)
            norm("ffn0", Vt, 0, 2)
            experts(0)

            norm("mix1", Vt, 0, 2)
            def product(i):
                n, r = divmod(i, 12)
                q, g = divmod(r, 4)
                key = ("qkv", 0, 2 * q + n)
                landed(pe, key)
                bank = (6, 5)[i % 2] if n == 0 else 6
                if i >= 2:
                    pe.wait_ge(prod_c, i - 1 if n == 0 else i)
                for k in range(KC):
                    if i == 0:
                        chunk_done(pe, n_h, "mix1", k)
                    if q == 2:
                        mm = pe.matmul(ps[:, bank, :], H[:, k, g * P:(g + 1) * P], piece(key)[:, k, :],
                                       start=(k == 0), stop=(k == KC - 1))
                    else:
                        c0 = 0 if q else CTX
                        mm = pe.matmul(ps[:, bank, c0:NTOK], piece(key)[:, k, g * P:(g + 1) * P], H[:, k, c0:NTOK],
                                       start=(k == 0), stop=(k == KC - 1))
                mm.then_inc(prod_p, 1)

            def rotate(r):
                i = 12 * (r // 8) + r % 8
                pe.wait_ge(prod_c, i + 1)
                if r >= 1:
                    pe.wait_ge(rot_r, r)
                pe.matmul(ps[:, 7, 0:SEQ], rot, rotated(r), start=True, stop=True).then_inc(rot_p, 1)

            def scores(u):
                h, qt = divmod(u, 2)
                if u % 8 == 0:
                    pe.wait_ge(rot_r, u + 8)
                if u >= 2:
                    pe.wait_ge(s_e, 2 * (u - 1))
                for c in range(2):
                    pe.matmul(ps[:, 2 * (u % 2) + c, :], Q[c * HD:(c + 1) * HD, h, qt * P:(qt + 1) * P],
                              K[c * HD:(c + 1) * HD, h, :], start=True, stop=True).then_inc(s_p, 1)

            def weights(u):
                pe.wait_ge(s_a, u + 1)
                if u >= 1:
                    pe.wait_ge(a_c, u)
                for k in range(NT):
                    mm = turn(ps[:, 4, k * P:(k + 1) * P], pr[:, u % 2, 0, k * P:(k + 1) * P])
                mm.then_inc(a_t, 1)

            def values(h):
                pe.wait_ge(a_c, 2 * (h + 1))
                if h % 4 == 0:
                    pe.wait_ge(prod_c, 12 * (h // 4 + 1))
                if h >= 1:
                    pe.wait_ge(o_c, h)
                for k in range(NT):
                    mm = pe.matmul(ps[:, 5, 0:SEQ], Wt[:, k, h * P:(h + 1) * P], aT[h % 2][:, k, :],
                                   start=(k == 0), stop=(k == NT - 1))
                mm.then_inc(o_p, 1)

            parts = {"product": product, "rotate": rotate, "scores": scores, "weights": weights, "values": values}
            for part, n in PLAN:
                if part in parts:
                    parts[part](n)
            for g in range(HEADS // 2):
                pe.wait_ge(o_sq, g + 1)
                pe.matmul(ps[:, g, :], head_mean, V[:, g * 512:(g + 1) * 512], start=True, stop=True).then_inc(o_ms, 1)
            for j in range(KC):
                key = ("wo", 0, j // 4)
                landed(pe, key)
                if j >= 4:
                    pe.wait_ge(wo_x, j - 3)
                for k in range(KC):
                    if j == 0 and k % 2 == 0:
                        pe.wait_ge(o_n, k // 2 + 1)
                    mm = pe.matmul(ps[:, 4 + j % 4, CTX:NTOK], piece(key)[:, k, (j % 4) * P:(j % 4 + 1) * P], O[:, k, :],
                                   start=(k == 0), stop=(k == KC - 1))
                mm.then_inc(wo_p, 1)
            norm("ffn1", Vt, CTX, 2)
            experts(1)
            norm("fin", Vt, CTX, 2)
            for t in range(2):
                for h in range(2):
                    for k in range(4):
                        chunk_done(pe, n_h, "fin", 4 * h + k)
                        mm = turn(ps[:, 4 + 2 * t + h, k * P:(k + 1) * P],
                                  H[:, 4 * h + k, CTX + t * P:CTX + (t + 1) * P])
                    mm.then_inc(fin_t, 1)

        @block.scalar
        def _(act):
            def rows(dst, src, n):
                act.dma_start(dst, src.rearrange("(r p) -> r p", p=P) if n > 1 else src).then_inc(
                    vecA_in if dst.tensor.name == rowsA.name else vec_in, 16)

            flat = {k: a[k] for k in ("ada_b", "norm_mix_g", "norm_ffn_g", "conv_pw1_b", "conv_dw_b", "conv_ln_g",
                                      "conv_ln_b", "conv_pw2_b", "c")}
            flat = {k: v.rearrange("l d -> (l d)") for k, v in flat.items()}
            for dst, at, n, src in ((rowsA, A_ADA, DEPTH * MODC, flat["ada_b"]), (rowsA, A_C, KC, flat["c"]),
                                    (rowsA, A_CC, KC, a["c_ctx"]), (rowsA, A_PW1, 2 * KC, flat["conv_pw1_b"]),
                                    (rowsB, B_MIX, DEPTH * KC, flat["norm_mix_g"]),
                                    (rowsB, B_FFN, DEPTH * KC, flat["norm_ffn_g"]),
                                    (rowsB, B_FIN, KC, a["final_norm_g"]), (rowsB, B_DWB, KC, flat["conv_dw_b"]),
                                    (rowsB, B_LNG, KC, flat["conv_ln_g"]), (rowsB, B_LNB, KC, flat["conv_ln_b"]),
                                    (rowsB, B_PW2, KC, flat["conv_pw2_b"])):
                rows(dst[at:at + n, :], src, n)
                if at == A_PW1 and dst is rowsA:
                    act.dma_start(cst[:, :], a["consts"]).then_inc(cst_in, 16)
            rows(rowsB[B_SUB:B_SUB + 1, :], a["diff_subln_g"], 1)
            rows(tap_rows[0:TAPS, :], a["conv_dw_w"][0], 1)
            act.wait_ge(eps_r, 1)
            act.dma_start(rw[:, :, 0:E], a["router_w"].rearrange("(j p) e -> p j e", p=P)).then_inc(rw_in, 16)
            act.dma_start(rb[:, :], a["router_b"].partition_broadcast(P)).then_inc(rw_in, 16)
            act.dma_start(lam[:, :, :].rearrange("p a b -> p (a b)"),
                          a["diff_lambda"].rearrange("l a b -> (l a b)").partition_broadcast(P)).then_inc(lam_in, 16)

            act.wait_ge(vec_c, 1)
            act.activation(sc[:, :, 0], colA[:, A_CC:A_CC + KC], ACT.Silu).then_inc(c_silu, 1)
            act.activation(sc[:, :, 1], colA[:, A_C:A_C + KC], ACT.Silu).then_inc(c_silu, 1)

            def ada_rows_copy(g):
                act.wait_ge(ada_p, g + 1)
                if g >= 2:
                    act.wait_ge(ada_t, g - 1)
                act.copy(adaR[:, g % 2, :], ps[:, g % 2, :]).then_inc(ada_r, 1)

            def ada_copy(g):
                l, n = divmod(g, ADA_PC)
                act.wait_ge(ada_t, g + 1)
                act.copy(mod[l][:, 4 * n:4 * n + 4, :].rearrange("p a b -> p (a b)"), ps[:, 7, 0:8]).then_inc(ada_c, 1)

            def squares(c0, ready):
                for k in range(KC):
                    act.wait_ge(*ready(k))
                    act.activation(Vt[:, k, c0:NTOK], X[:, k, c0:NTOK], ACT.Square).then_inc(n_sq, 1)

            def take_factor(name, bank, c0):
                if name == "ln":
                    act.wait_ge(var_p, 1)
                else:
                    act.wait_ge(n_ms, NORM[name] + 1)
                act.activation(R[:, c0:NTOK], ps[:, bank, c0:NTOK], ACT.Ln, bias=epsc[:, 0:1]).then_inc(n_log, 1)
                act.wait_ge(n_log, FACTORS[name])
                act.activation(R[:, c0:NTOK], R[:, c0:NTOK], ACT.Exp, scale=-0.5).then_inc(n_inv, 1)

            def modulate(name, l, which, c0):
                for k in range(KC):
                    chunk_done(act, n_hr, name, k)
                    for st in range(c0 // CTX, 2):
                        v = H[:, k, st * CTX:(st + 1) * CTX]
                        i = act.activation(v, v, ACT.Identity, bias=mod[l][:, (3 * which) * KC + k, st:st + 1],
                                           scale=modA[:, which, k, st:st + 1])
                    i.then_inc(n_h, 1)

            def experts(l):
                m = moes[l]
                T, NH = TL[l], TM[l] // MH
                act.wait_ge(m.route_p, 1)
                act.copy(R[:, T0[l] * P:NTOK], ps[:, 3, T0[l] * P:NTOK]).then_inc(m.route_c, 1)
                for g in range(2 * T):
                    if g == 2:
                        act.wait_ge(m.route_t, 1)
                        act.activation(score[:, 0:T, :].rearrange("p t e -> p (t e)"), ps[:, 2, 0:T * E],
                                       ACT.Sigmoid).then_inc(m.score_r, 1)
                    act.wait_ge(m.rows_t, g + 1)
                    act.copy(Wt[:, g // 2, (g % 2) * 512:(g % 2 + 1) * 512], ps[:, 4 + g % 4, :]).then_inc(m.rows_c, 1)
                def silu(e, first=False):
                    for h in range(NH):
                        def run():
                            act.wait_ge(m.gate_p[h], e + 1)
                            if not first:
                                act.wait_ge(m.act_r[h], e)
                            act.activation(acts(eg, h), gate_out(h), ACT.Silu).then_inc(m.gate_s[h], 1)

                        def skip():
                            act.wait_ge(m.gate_s[0], e + 1)
                            act.nop().then_inc(m.gate_s[h], 1)

                        with_half(act, h, e, run, skip)

                def output(b, i):
                    act.wait_ge(m.down_p[0], i * 2 + (b + 1))
                    act.wait_ge(m.y_free, i * 2 + (b + 1))
                    act.copy(y_part(b, 0), down_out(0)).then_inc(m.y_c[0], 1)

                act.nop().then_inc(m.y_c[0], 1)
                silu(0, first=True)
                with act.Fori(0, E // 2 - 1) as i:
                    silu(i * 2 + 1)
                    output(0, i)
                    silu(i * 2 + 2)
                    output(1, i)
                last = E // 2 - 1
                silu(E - 1)
                output(0, last)
                output(1, last)
                act.wait_ge(m.over_r, 1)
                n_over = act.value_load(novI[0:1, 0:1], min_val=0, max_val=OVER)
                with act.If(n_over > 0):
                    with act.Fori(0, n_over) as j:
                        step_done(act, m, j, "gate_up")
                        for h in range(NH):
                            i = act.activation(acts(eg, h), gate_out(h), ACT.Silu)
                        i.then_inc(m.o_step, 1)
                with act.Else():
                    act.nop()
                for t in range(T):
                    act.wait_ge(m.y_in[t // 2], 64)
                    act.mul(Wt[:, t, :], Wt[:, t, :], wk[:, 0, t:t + 1]).then_inc(m.w1_r, 1)

            for k in range(KC):
                act.wait_ge(x_t, k + 1)
                act.copy(X[:, k, :], ps[:, 4 + k % 4, :]).then_inc(x_c, 1)
            squares(0, lambda k: (x_c, k + 1))
            for g in range(4):
                ada_rows_copy(g)
                if g:
                    ada_copy(g - 1)
            ada_copy(3)
            act.wait_ge(eps_r, 1)
            take_factor("mix0", 2, 0)
            act.wait_ge(modA_r, 1)
            modulate("mix0", 0, 0, 0)
            for j in range(KC):
                act.wait_ge(pw1_p, 2 * j + 1)
                if j >= 2:
                    act.wait_ge(pw1_g, j - 1)
                act.activation(sg[:, j % 2, :], ps[:, 4 + 2 * (j % 2), :], ACT.Sigmoid,
                               bias=colA[:, A_PW1 + KC + j:A_PW1 + KC + j + 1]).then_inc(pw1_s, 1)
                for g in FILL[j]:
                    ada_rows_copy(g)
                    if g > 4:
                        ada_copy(g - 1)
            ada_copy(DEPTH * ADA_PC - 1)
            for k in range(KC):
                act.wait_ge(cen, k + 1)
                act.activation(H[:, k, :], Vt[:, k, :], ACT.Square).then_inc(cen_sq, 1)
            take_factor("ln", 3, 0)
            for k in range(KC):
                act.wait_ge(lnz, k + 1)
                act.activation(H[:, k, :], Vt[:, k, :], ACT.Silu, bias=colB[:, B_LNB + k:B_LNB + k + 1],
                               scale=colB[:, B_LNG + k:B_LNG + k + 1]).then_inc(ln_s, 1)
            act.wait_ge(modA_r, 2)
            for j in range(KC):
                act.wait_ge(pw2_p, j + 1)
                if j >= 2:
                    act.wait_ge(pw2_x, j - 1)
                for st in range(2):
                    cs = slice(st * CTX, (st + 1) * CTX)
                    i = act.activation(sg[:, j % 2, cs], ps[:, 4 + j % 4, cs], ACT.Identity,
                                       bias=gb2[:, j, st:st + 1], scale=mod[0][:, 2 * KC + j, st:st + 1])
                i.then_inc(pw2_t, 1)
            squares(0, lambda k: (pw2_x, k + 1))
            take_factor("ffn0", 2, 0)
            modulate("ffn0", 0, 1, 0)
            experts(0)
            squares(0, lambda k: (moes[0].mix_x, KC + k + 1))
            take_factor("mix1", 2, 0)
            act.wait_ge(modB_r, 1)
            modulate("mix1", 1, 0, 0)
            act.wait_ge(lam_s, 1)
            for k in range(2):
                act.activation(lamt[:, 2 + k:3 + k], lamt[:, k:k + 1], ACT.Exp).then_inc(lam_e, 1)

            def product_copy(i):
                n, r = divmod(i, 12)
                q, g = divmod(r, 4)
                bank = (6, 5)[i % 2] if n == 0 else 6
                act.wait_ge(prod_p, i + 1)
                if q == 0:
                    c = act.copy(Q[:, 4 * n + g, :], ps[:, bank, CTX:NTOK])
                elif q == 1:
                    c = act.copy(K[:, 4 * n + g, :], ps[:, bank, :])
                else:
                    c = act.copy(Wt[:, g, n * 512:(n + 1) * 512], ps[:, bank, :])
                c.then_inc(prod_c, 1)

            def exponentials(u):
                b = u % 2
                for c in range(2):
                    act.wait_ge(s_m, 2 * u + c + 1)
                    if u >= 2:
                        act.wait_ge(a_t, u - 1)
                    act.activation(pr[:, b, c, :], ps[:, 2 * b + c, :], ACT.Exp, bias=sm[:, b, c, 0:1], scale=SCALE,
                                   accum_out=sm[:, b, c, 1:2]).then_inc(s_e, 1)

            def turned_copy(u):
                h, qt = divmod(u, 2)
                act.wait_ge(a_t, u + 1)
                if u >= 4:
                    act.wait_ge(o_p, h - 1)
                act.copy(aT[h % 2][:, :, qt * P:(qt + 1) * P],
                         ps[:, 4, :].rearrange("p (k t) -> p k t", k=NT)).then_inc(a_c, 1)

            parts = {"product": product_copy, "scores": exponentials, "weights": turned_copy}
            for part, n in PLAN:
                if part in parts:
                    parts[part](n)
            for g in range(HEADS // 2):
                act.wait_ge(o_c, 2 * (g + 1))
                act.activation(V[:, g * 512:(g + 1) * 512], OF[:, g * 512:(g + 1) * 512], ACT.Square).then_inc(o_sq, 1)
            for g in range(HEADS // 2):
                act.wait_ge(o_ms, g + 1)
                act.activation(HR[:, g * 512:(g + 1) * 512], ps[:, g, :], ACT.Ln, bias=epsc[:, 0:1]).then_inc(n_log, 1)
            for g in range(HEADS // 2):
                act.wait_ge(n_log, FACTORS["heads"] + g)
                r = HR[:, g * 512:(g + 1) * 512]
                act.activation(r, r, ACT.Exp, scale=-0.5).then_inc(n_inv, 1)
            squares(CTX, lambda k: (wo_x, k + 1))
            take_factor("ffn1", 2, CTX)
            modulate("ffn1", 1, 1, CTX)
            experts(1)
            squares(CTX, lambda k: (moes[1].mix_x, k + 1))
            take_factor("fin", 2, CTX)
            for g in range(4):
                act.wait_ge(fin_t, g + 1)
                act.copy(Wt[:, g // 2, (g % 2) * 512:(g % 2 + 1) * 512], ps[:, 4 + g, :]).then_inc(fin_c, 1)

        @block.vector
        def _(v):
            count = [0]

            def link(i):
                count[0] += 1
                i.then_inc(dve, 1)
                v.wait_ge(dve, count[0])

            def bc(ap, shape):
                return ap.to_broadcast(shape)

            def norm(name, c0):
                v.wait_ge(n_inv, FACTORS[name])
                for k in range(KC):
                    v.tensor_tensor(H[:, k, c0:NTOK], X[:, k, c0:NTOK], R[:, c0:NTOK], ALU.mult).then_inc(n_hr, 1)

            def bias_mods(l, a0, a1):
                link(v.tensor_tensor(mod[l][:, a0:a1, :], mod[l][:, a0:a1, :],
                                     colA[:, A_ADA + l * MODC + a0:A_ADA + l * MODC + a1].unsqueeze(2).to_broadcast([P, a1 - a0, 2]), ALU.add))

            def gain(l, which):
                at = (B_FFN if which else B_MIX) + l * KC
                return v.scalar_tensor_tensor(modA[:, which, :, :], mod[l][:, (3 * which + 1) * KC:(3 * which + 2) * KC, :],
                                              1.0, colB[:, at:at + KC].unsqueeze(2).to_broadcast([P, KC, 2]), ALU.add, ALU.mult)

            def experts(l):
                m = moes[l]
                T, t0, M, NH = TL[l], T0[l], TM[l], TM[l] // MH
                G4 = T * GROUPS

                def te(x):
                    return x[:, 0:T, :]

                def per_tok(x):
                    return x.unsqueeze(2).to_broadcast([P, T, E])

                def tok(n):
                    return t1[:, n, 0:T]

                ekey = cst[:, C_EKEY:C_EKEY + T * E].rearrange("p (t e) -> p t e", t=T)
                gkey = cst[:, C_GKEY:C_GKEY + G4].rearrange("p (t g) -> p t g", t=T)
                v.wait_ge(m.score_r, 1)
                if l == 0:
                    v.wait_ge(rw_in, 32)
                link(v.tensor_tensor(te(sel), te(score), rb[:, :].unsqueeze(1).to_broadcast([P, T, E]), ALU.add))
                s4 = te(sel).rearrange("p t (g i) -> p (t g) i", i=GS)

                def q(n):
                    return g4[:, n, 0:G4]

                v.tensor_tensor(q(0), s4[:, :, 0], s4[:, :, 1], ALU.max)
                v.tensor_tensor(q(1), s4[:, :, 0], s4[:, :, 1], ALU.min)
                v.tensor_tensor(q(2), s4[:, :, 2], s4[:, :, 3], ALU.max)
                link(v.tensor_tensor(q(3), s4[:, :, 2], s4[:, :, 3], ALU.min))
                v.tensor_tensor(q(4), q(0), q(2), ALU.max)
                v.tensor_tensor(q(5), q(0), q(2), ALU.min)
                link(v.tensor_tensor(q(6), q(1), q(3), ALU.max))
                link(v.tensor_tensor(q(5), q(5), q(6), ALU.max))
                link(v.tensor_tensor(q(7), q(4), q(5), ALU.add))

                def tg(n):
                    return q(n).rearrange("p (t g) -> p t g", t=T)

                def tok_g(n):
                    return tok(n).unsqueeze(2).to_broadcast([P, T, GROUPS])

                link(v.tensor_reduce(tok(0), tg(7), AX.X, ALU.max))
                link(v.tensor_tensor(tg(8), tg(7), tok_g(0), ALU.is_equal))
                link(v.tensor_tensor(tg(8), tg(8), gkey, ALU.mult))
                link(v.tensor_reduce(tok(1), tg(8), AX.X, ALU.max))
                link(v.tensor_tensor(tg(9), tg(8), tok_g(1), ALU.is_equal))
                m4 = te(msel).rearrange("p t (g i) -> p (t g) i", i=GS)
                in_g = q(9).unsqueeze(2).to_broadcast([P, G4, GS])
                link(v.tensor_tensor(m4, s4, in_g, ALU.mult))
                link(v.tensor_scalar(q(8), q(9), -1.0, BIG, ALU.add, ALU.mult))
                link(v.tensor_tensor(m4, m4, q(8).unsqueeze(2).to_broadcast([P, G4, GS]), ALU.add))
                for k in range(2):
                    one = oh[:, k, 0:T, :]
                    link(v.tensor_reduce(tok(2), te(msel), AX.X, ALU.max))
                    link(v.tensor_tensor(te(tA), te(msel), per_tok(tok(2)), ALU.is_equal))
                    link(v.tensor_tensor(te(tA), te(tA), ekey, ALU.mult))
                    link(v.tensor_reduce(tok(3), te(tA), AX.X, ALU.max))
                    link(v.tensor_tensor(one, te(tA), per_tok(tok(3)), ALU.is_equal))
                    link(v.tensor_tensor(te(tA) if k else te(tB), ekey, per_tok(tok(3)), ALU.is_lt))
                    if k == 0:
                        link(v.scalar_tensor_tensor(te(msel), one, -3.0 * BIG, te(msel), ALU.mult, ALU.add))
                v.tensor_tensor(pair[:, 1, 0:T, :], te(tA), te(tB), ALU.add)
                v.tensor_tensor(pair[:, 0, 0:T, :], oh[:, 0, 0:T, :], oh[:, 1, 0:T, :], ALU.add).then_inc(m.pair_r, 1)
                v.wait_ge(m.rank_p, 1)

                def sums(q):
                    return ps[:, 2, q * T * E:(q + 1) * T * E].rearrange("p (t e) -> p t e", t=T)

                off, num = ints[:, 0, 0:E], ints[:, 1, 0:E]
                v.memset(ints[:, 0, E:24], float(2 * T * P))
                link(v.tensor_reduce(num, sums(0).rearrange("p t e -> p e t"), AX.X, ALU.add))
                v.tensor_copy(numI[:, :], num)
                link(v.tensor_reduce(off, sums(1).rearrange("p t e -> p e t"), AX.X, ALU.add))
                v.tensor_copy(tB[:, 0, :], off)
                before_t = off
                for t in range(1, T):
                    link(v.tensor_tensor(tB[:, t, :], before_t, sums(0)[:, t - 1, :], ALU.add))
                    before_t = tB[:, t, :]
                link(v.tensor_tensor(te(tB), te(tB), sums(2), ALU.add))
                mine = ov[:, :, :].rearrange("p a b -> p (a b)")[:, 0:2 * T * E].rearrange("p (k t e) -> p k t e", k=2, t=T)
                for k in range(2):
                    i = v.tensor_tensor(mine[:, k], te(tB), oh[:, k, 0:T, :], ALU.mult)
                link(i)
                for k in range(2):
                    i = v.tensor_reduce(tok(8 + k), mine[:, k], AX.X, ALU.add)
                link(i)
                v.tensor_copy(slot[:, 0:T], tok(8))
                v.tensor_copy(slot[:, NT:NT + T], tok(9))
                v.tensor_copy(offI[:, :], ints[:, 0, :]).then_inc(m.slot_r, 1)
                for k in range(2):
                    link(v.tensor_tensor(te(sel), te(score), oh[:, k, 0:T, :], ALU.mult))
                    link(v.tensor_reduce(tok(4 + k), te(sel), AX.X, ALU.add))
                link(v.tensor_tensor(tok(6), tok(4), tok(5), ALU.add))
                link(v.reciprocal(tok(7), tok(6)))
                for k in range(2):
                    link(v.tensor_tensor(wk[:, k, 0:T], tok(4 + k), tok(7), ALU.mult))
                place = ov[:, :, :].rearrange("p a b -> p (a b)")
                mine, at = place[:, 0:2 * E], place[:, 2 * E:4 * E]
                for h in range(NH):
                    v.tensor_scalar(mine[:, h * E:(h + 1) * E], num, C(C_WROW + 2 * h, 1), None, ALU.is_gt)
                    i = v.tensor_scalar(at[:, h * E:(h + 1) * E], off, 2.0, C(C_WROW + 2 * h + 1, 1), ALU.mult, ALU.add)
                link(i)
                link(v.tensor_tensor(at[:, 0:NH * E], at[:, 0:NH * E], C(C_WPAD, NH * E), ALU.subtract))
                link(v.tensor_tensor(at[:, 0:NH * E], at[:, 0:NH * E], mine[:, 0:NH * E], ALU.mult))
                link(v.tensor_tensor(at[:, 0:NH * E], at[:, 0:NH * E], C(C_WPAD, NH * E), ALU.add))
                for h in range(NH):
                    i = v.tensor_copy(wrow[:, :, h], at[:, h * E:(h + 1) * E])
                link(i)
                link(v.memset(cum[:, :, :], 0.0))
                link(v.tensor_scalar(tA[:, 0, :], num, float(M), None, ALU.is_gt))
                for k in range(2, T * P // M):
                    link(v.scalar_tensor_tensor(tA[:, 0, :], num, float(k * M), tA[:, 0, :], ALU.is_gt, ALU.add))
                link(v.tensor_copy(cum[:, 0, 8:8 + E], tA[:, 0, :]))
                src = 0
                for step in (1, 2, 4, 8):
                    link(v.tensor_tensor(cum[:, 1 - src, 8:8 + E], cum[:, src, 8:8 + E],
                                         cum[:, src, 8 - step:8 + E - step], ALU.add))
                    src = 1 - src
                up_to = cum[:, src, 8:8 + E]
                link(v.tensor_copy(novI[:, :], cum[:, src, 8 + E - 1:8 + E]))

                def oe(n):
                    return ov[:, n, :].rearrange("p (i e) -> p i e", e=E)

                def over_e(x):
                    return x.unsqueeze(1).to_broadcast([P, OVER, E])

                passes = cst[:, C_PASS:C_PASS + OVER * E].rearrange("p (i e) -> p i e", e=E)
                expert = cst[:, C_EXP:C_EXP + OVER * E].rearrange("p (i e) -> p i e", e=E)
                link(v.tensor_tensor(oe(0), over_e(up_to), passes, ALU.is_le))
                link(v.tensor_reduce(ovf[:, 0, 0:OVER], oe(0), AX.X, ALU.add))
                link(v.tensor_tensor(oe(1), expert, ovf[:, 0, 0:OVER].unsqueeze(2).to_broadcast([P, OVER, E]), ALU.is_equal))
                link(v.tensor_tensor(tB[:, 0, :], up_to, tA[:, 0, :], ALU.subtract))
                link(v.tensor_tensor(oe(2), passes, over_e(tB[:, 0, :]), ALU.subtract))
                link(v.tensor_scalar(oe(2), oe(2), 1.0, float(M), ALU.add, ALU.mult))
                link(v.tensor_tensor(oe(2), oe(2), over_e(off), ALU.add))
                link(v.tensor_tensor(tB[:, 1, :], off, num, ALU.add))
                link(v.tensor_scalar(tB[:, 1, :], tB[:, 1, :], -float(M), None, ALU.add))
                link(v.tensor_tensor(oe(2), oe(2), over_e(tB[:, 1, :]), ALU.min))
                link(v.tensor_tensor(oe(2), oe(2), oe(1), ALU.mult))
                link(v.tensor_reduce(ovf[:, 1, 0:OVER], oe(2), AX.X, ALU.add))
                for k in range(3):
                    link(v.tensor_copy(ovI[:, k, 0:OVER], ovf[:, min(k, 1), 0:OVER]))
                v.nop().then_inc(m.over_r, 1)

                def cols(ap, n):
                    return ap.rearrange("p (k t) -> p k t", k=n)[:, :, 0:M]

                def rows_copy(b, h):
                    return v.tensor_copy(cols(hT[:, b, h * 512:(h + 1) * 512], 4), cols(ps[:, 5 + h, :], 4))

                def rows(b, i):
                    for h in range(2):
                        v.wait_ge(m.h_t, i * 4 + (2 * b + h + 1))
                        c = rows_copy(b, h)
                    c.then_inc(m.h_c, 1)

                def turned(b, i):
                    v.wait_ge(m.act_t, i * 2 + (b + 1))
                    v.tensor_copy(cols(eaT, FC), cols(ps[:, 2, :], FC)).then_inc(m.act_c, 1)

                def gated(b, i):
                    e = i * 2 + b
                    for h in range(NH):
                        def run():
                            v.wait_ge(m.gate_s[h], e + 1)
                            v.tensor_tensor(acts(ea, h), acts(eg, h), up_out(h), ALU.mult).then_inc(m.act_r[h], 1)

                        def skip():
                            v.wait_ge(m.act_r[0], e + 1)
                            v.nop().then_inc(m.act_r[h], 1)

                        with_half(v, h, e, run, skip)

                def output(b, i):
                    e = i * 2 + b
                    for h in range(1, NH):
                        def run():
                            v.wait_ge(m.down_p[h], e + 1)
                            v.wait_ge(m.y_free, e + 1)
                            v.tensor_copy(y_part(b, h), down_out(h)).then_inc(m.y_c[h], 1)

                        def skip():
                            v.wait_ge(m.y_c[h], e + 1)
                            v.nop().then_inc(m.y_c[h], 1)

                        with_half(v, h, e, run, skip)

                for h in range(1, NH):
                    v.nop().then_inc(m.y_c[h], 1)
                rows(0, 0)
                rows(1, 0)
                gated(0, 0)
                with v.Fori(0, E // 2 - 1) as i:
                    for b in range(2):
                        turned(b, i)
                        gated(1 - b, i + b)
                        rows(b, i + 1)
                        output(b, i)
                last = E // 2 - 1
                turned(0, last)
                gated(1, last)
                output(0, last)
                turned(1, last)
                output(1, last)
                n_over = v.value_load(novI[0:1, 0:1], min_val=0, max_val=OVER)
                with v.If(n_over > 0):
                    with v.Fori(0, n_over) as j:
                        step_done(v, m, j, "turned")
                        rows_copy(0, 0)
                        rows_copy(0, 1).then_inc(m.o_step, 1)
                        step_done(v, m, j, "silu")
                        for h in range(NH):
                            i = v.tensor_tensor(acts(ea, h), acts(eg, h), up_out(h), ALU.mult)
                        i.then_inc(m.o_step, 1)
                        step_done(v, m, j, "act_turned")
                        v.tensor_copy(cols(eaT, FC), cols(ps[:, 2, :], FC)).then_inc(m.o_step, 1)
                        step_done(v, m, j, "down")
                        for h in range(NH):
                            i = v.tensor_copy(y_part(0, h), down_out(h))
                        i.then_inc(m.o_step, 1)
                with v.Else():
                    v.nop()
                for t in range(T):
                    v.wait_ge(m.y_in[t // 2], 64)
                    v.wait_ge(m.w1_r, t + 1)
                    v.scalar_tensor_tensor(Wt[:, t, :], Ht[:, t, :], wk[:, 1, t:t + 1], Wt[:, t, :],
                                           ALU.mult, ALU.add).then_inc(m.mix_r, 1)
                for g in range(KC * T // 2):
                    st, k = g // KC + t0 // 2, g % KC
                    cs = slice(st * CTX, (st + 1) * CTX)
                    v.wait_ge(m.mix_t, g + 1)
                    v.scalar_tensor_tensor(X[:, k, cs], ps[:, 4 + g % 4, 0:CTX], mod[l][:, 5 * KC + k, st:st + 1],
                                           X[:, k, cs], ALU.mult, ALU.add).then_inc(m.mix_x, 1)

            v.memset(sc[:, :, :], 0.0)
            v.memset(rw[:, :, :], 0.0)
            v.memset(epsc[:, :], EPS).then_inc(eps_r, 1)
            v.wait_ge(vec_t, 1)
            v.tensor_copy(colA[:, :], ps[:, 0, 0:P]).then_inc(vec_c, 1)
            v.wait_ge(vec_t, 2)
            v.tensor_copy(colB[:, :], ps[:, 2, 0:B_ROWS])
            v.tensor_copy(cw[:, :, 0:TAPS], ps[:, 3, 0:256].rearrange("p (j t) -> p j t", j=KC)[:, :, 0:TAPS]).then_inc(vec_c, 1)
            v.wait_ge(vec_c, 2)
            v.wait_ge(ada_c, 4)
            bias_mods(0, 0, 16)
            gain(0, 0).then_inc(modA_r, 1)
            v.wait_ge(x_c, KC)
            norm("mix0", 0)
            v.wait_ge(pad_z, 1)
            for group in CONV_GROUPS:
                for j in group:
                    v.wait_ge(pw1_p, 2 * j + 2)
                    v.wait_ge(pw1_s, j + 1)
                    v.scalar_tensor_tensor(U[:, j, :, PAD:PAD + SEQ],
                                           ps[:, 3 + 2 * (j % 2), :].rearrange("p (s t) -> p s t", s=2),
                                           colA[:, A_PW1 + j:A_PW1 + j + 1],
                                           sg[:, j % 2, :].rearrange("p (s t) -> p s t", s=2),
                                           ALU.add, ALU.mult).then_inc(pw1_g, 1)
                v.wait_ge(pw1_g, group[-1] + 1)
                for tap in range(TAPS):
                    for j in group:
                        o = Vt[:, j, :].rearrange("p (s t) -> p s t", s=2)
                        src = U[:, j, :, tap:tap + SEQ]
                        w = cw[:, j, tap:tap + 1]
                        if tap == 0:
                            i = v.tensor_scalar(o, src, w, colB[:, B_DWB + j:B_DWB + j + 1], ALU.mult, ALU.add)
                        else:
                            since = 0 if tap == TAPS - 1 and j > group[0] else len(group) - 1
                            v.wait_ge(dve, count[0] - since)
                            i = v.scalar_tensor_tensor(o, src, w, o, ALU.mult, ALU.add)
                        if tap < TAPS - 1:
                            i.then_inc(dve, 1)
                            count[0] += 1
                        else:
                            i.then_inc(conv_a, 1)
            v.wait_ge(ada_c, 2 * ADA_PC)
            bias_mods(0, 16, MODC)
            bias_mods(1, 0, MODC)
            link(gain(0, 1))
            v.tensor_tensor(gb2[:, :, :], mod[0][:, 2 * KC:3 * KC, :],
                            colB[:, B_PW2:B_PW2 + KC].unsqueeze(2).to_broadcast([P, KC, 2]), ALU.mult).then_inc(modA_r, 1)
            v.wait_ge(mean_p, 1)
            v.wait_ge(conv_a, KC)
            for k in range(KC):
                v.tensor_tensor(Vt[:, k, :], Vt[:, k, :], ps[:, 2, :], ALU.subtract).then_inc(cen, 1)
            v.wait_ge(n_inv, FACTORS["ln"])
            v.wait_ge(cen, KC)
            for k in range(KC):
                v.tensor_tensor(Vt[:, k, :], Vt[:, k, :], R[:, :], ALU.mult).then_inc(lnz, 1)
            for j in range(KC):
                v.wait_ge(pw2_t, j + 1)
                v.tensor_tensor(X[:, j, :], X[:, j, :], sg[:, j % 2, :], ALU.add).then_inc(pw2_x, 1)
            v.wait_ge(pw2_x, KC)
            norm("ffn0", 0)
            experts(0)

            chunk_done(v, n_h, "ffn0", KC - 1)
            link(gain(1, 0))
            gain(1, 1).then_inc(modB_r, 1)
            v.wait_ge(moes[0].mix_x, 2 * KC)
            norm("mix1", 0)
            v.wait_ge(lam_in, 16)
            for k in range(2):
                link(v.tensor_tensor(lam[:, 2 * k, :], lam[:, 2 * k, :], lam[:, 2 * k + 1, :], ALU.mult))
                link(v.tensor_reduce(lamt[:, k:k + 1], lam[:, 2 * k, :], AX.X, ALU.add))
            v.nop().then_inc(lam_s, 1)
            link(v.tensor_scalar(subg[:, :], colB[:, B_SUB:B_SUB + 1], 1.0 - LAM_INIT, None, ALU.mult))
            cos, sin = cst[:, C_COS:C_COS + SEQ], cst[:, C_SIN:C_SIN + SEQ]
            def rotary(r):
                t = rotated(r)
                part = R[:, (r % 2) * SEQ:(r % 2 + 1) * SEQ]
                if r >= 2:
                    v.wait_ge(rot_r, r - 1)
                v.wait_ge(rot_p, r + 1)
                v.tensor_tensor(part, ps[:, 7, 0:SEQ], sin, ALU.mult)
                link(v.tensor_tensor(t, t, cos, ALU.mult))
                v.tensor_tensor(t, t, part, ALU.add).then_inc(rot_r, 1)

            v.wait_ge(lam_e, 2)
            link(v.tensor_tensor(lamt[:, 4:5], lamt[:, 3:4], lamt[:, 2:3], ALU.subtract))
            link(v.tensor_scalar(lamt[:, 5:6], lamt[:, 4:5], -LAM_INIT, None, ALU.add))

            def maxima(u):
                b = u % 2
                for c in range(2):
                    v.wait_ge(s_p, 2 * u + c + 1)
                    if u >= 2:
                        v.wait_ge(s_e, 2 * (u - 2) + c + 1)
                    link(v.tensor_reduce(sm[:, b, c, 2:3], ps[:, 2 * b + c, :], AX.X, ALU.max))
                    v.tensor_scalar(sm[:, b, c, 0:1], sm[:, b, c, 2:3], -SCALE, None, ALU.mult).then_inc(s_m, 1)

            def combine(u):
                b = u % 2
                v.wait_ge(s_e, 2 * u + 2)
                link(v.reciprocal(sm[:, b, :, 3], sm[:, b, :, 1]))
                link(v.tensor_tensor(sm[:, b, 1, 3:4], sm[:, b, 1, 3:4], lamt[:, 5:6], ALU.mult))
                link(v.tensor_scalar(pr[:, b, 0, :], pr[:, b, 0, :], sm[:, b, 0, 3:4], None, ALU.mult))
                v.scalar_tensor_tensor(pr[:, b, 0, :], pr[:, b, 1, :], sm[:, b, 1, 3:4], pr[:, b, 0, :],
                                       ALU.mult, ALU.add).then_inc(s_a, 1)

            def out_copy(h):
                v.wait_ge(o_p, h + 1)
                v.tensor_copy(O[:, h, :], ps[:, 5, 0:SEQ]).then_inc(o_c, 1)

            parts = {"rotate": rotary, "scores": maxima, "combine": combine, "values": out_copy}
            for part, n in PLAN:
                if part in parts:
                    parts[part](n)
            for g in range(HEADS // 2):
                v.wait_ge(n_inv, FACTORS["heads"] + g)
                r = HR[:, g * 512:(g + 1) * 512]
                o = OF[:, g * 512:(g + 1) * 512]
                if g == 0:
                    v.wait_ge(o_c, HEADS)
                v.scalar_tensor_tensor(o, o, subg[:, 0:1], r, ALU.mult, ALU.mult).then_inc(o_n, 1)
            for j in range(KC):
                v.wait_ge(wo_p, j + 1)
                v.scalar_tensor_tensor(X[:, j, CTX:NTOK], ps[:, 4 + j % 4, CTX:NTOK], mod[1][:, 2 * KC + j, 1:2],
                                       X[:, j, CTX:NTOK], ALU.mult, ALU.add).then_inc(wo_x, 1)
            v.wait_ge(wo_x, KC)
            norm("ffn1", CTX)
            experts(1)
            v.wait_ge(moes[1].mix_x, KC)
            v.wait_ge(n_inv, FACTORS["fin"])
            for k in range(KC):
                v.scalar_tensor_tensor(H[:, k, CTX:NTOK], X[:, k, CTX:NTOK], colB[:, B_FIN + k:B_FIN + k + 1],
                                       R[:, CTX:NTOK], ALU.mult, ALU.mult).then_inc(n_h, 1)


_INS = ["x", "c", "ctx", "c_ctx", "ada_w", "ada_b", "norm_mix_g", "norm_ffn_g", "final_norm_g",
        "conv_pw1_w", "conv_pw1_b", "conv_dw_w", "conv_dw_b", "conv_ln_g", "conv_ln_b", "conv_pw2_w",
        "conv_pw2_b", "diff_w_qkv", "diff_lambda", "diff_subln_g", "diff_w_o", "router_w", "router_b",
        "moe_w_gate", "moe_w_up", "moe_w_down"]


def kernel(**inputs):
    import numpy as _np
    import concourse.bacc as _bacc
    from concourse import mybir as _mybir
    from concourse.bass_utils import run_bass_kernel_spmd as _run

    nc = _bacc.Bacc("TRN2", target_bir_lowering=False, num_devices=1)
    arrays, aps = {}, {}
    given = {name: _np.ascontiguousarray(inputs[name]) for name in _INS}
    given["consts"] = constants()
    for name, arr in given.items():
        arrays[f"in_{name}"] = arr
        aps[name] = nc.dram_tensor(f"in_{name}", arr.shape, _mybir.dt.from_np(arr.dtype), kind="ExternalInput").ap()
    out = nc.dram_tensor("out_0", (1, SEQ, D), F32, kind="ExternalOutput").ap()
    build(nc, aps, out)
    r = _run(nc, [arrays], core_ids=[0])
    return r.results[0]["out_0"]
```
